# Optimizing a Trainium2 kernel written in Bass

```python
import math
import jax, jax.numpy as jnp
from jax import lax
import numpy as np

D_MODEL = 2048
BATCH = 1
SEQ = 512
DEPTH = 1

CHUNK = 64
Q_BLOCK = 128
HEAD_DIM = 128
N_HEADS_DIFF = D_MODEL // 256
DIFF_QK_DIM = HEAD_DIM // 2
N_HEADS_FOX = D_MODEL // 256
WIDTH_DIFF = N_HEADS_DIFF * HEAD_DIM
WIDTH_FOX = N_HEADS_FOX * HEAD_DIM
D_IN_PROJ = 3 * WIDTH_DIFF + 3 * WIDTH_FOX + N_HEADS_FOX
D_FF = 4 * D_MODEL
EPS = 1e-6

OFF_QA = WIDTH_DIFF
OFF_KA = 2 * WIDTH_DIFF
OFF_VA = 3 * WIDTH_DIFF
OFF_QB = 3 * WIDTH_DIFF + WIDTH_FOX
OFF_KB = 3 * WIDTH_DIFF + 2 * WIDTH_FOX
OFF_VB = 3 * WIDTH_DIFF + 3 * WIDTH_FOX

kernel_name = "hybrid_diff_fox_gated_block"

def rms_norm(x, g):
    xf = x.astype(jnp.float32)
    r = lax.rsqrt(jnp.mean(xf * xf, axis=-1, keepdims=True) + EPS)
    return (xf * r).astype(x.dtype) * g

def alibi_slopes(n_heads):
    return 2.0 ** (-8.0 * jnp.arange(1, n_heads + 1, dtype=jnp.float32) / n_heads)

def diff_attention(q1, q2, k1, k2, v, lam, slopes):
    S = q1.shape[2]
    scale = DIFF_QK_DIM ** -0.5
    outs = []
    for start in range(0, S, Q_BLOCK):
        end = start + Q_BLOCK
        t = jnp.arange(start, end)[:, None]
        s = jnp.arange(end)[None, :]
        allowed = (s // CHUNK) <= (t // CHUNK)
        bias = -slopes[:, None, None] * jnp.abs(t - s).astype(jnp.float32)
        bias = jnp.where(allowed[None], bias, -jnp.inf)

        def probs(q, k):
            logits = jnp.einsum('bhqd,bhkd->bhqk', q[:, :, start:end], k[:, :, :end]).astype(jnp.float32)
            return jax.nn.softmax(logits * scale + bias[None], axis=-1)

        p = probs(q1, k1) - lam * probs(q2, k2)
        outs.append(jnp.einsum('bhqk,bhkd->bhqd', p.astype(v.dtype), v[:, :, :end]))
    return jnp.concatenate(outs, axis=2)

def forgetting_attention(q, k, v, log_f_cum):
    S = q.shape[2]
    scale = HEAD_DIM ** -0.5
    outs = []
    for start in range(0, S, Q_BLOCK):
        end = start + Q_BLOCK
        t = jnp.arange(start, end)[:, None]
        s = jnp.arange(end)[None, :]
        allowed = s <= t
        decay = log_f_cum[:, :, start:end, None] - log_f_cum[:, :, None, :end]
        logits = jnp.einsum('bhqd,bhkd->bhqk', q[:, :, start:end], k[:, :, :end]).astype(jnp.float32)
        logits = jnp.where(allowed[None, None], logits * scale + decay, -jnp.inf)
        p = jax.nn.softmax(logits, axis=-1)
        outs.append(jnp.einsum('bhqk,bhkd->bhqd', p.astype(v.dtype), v[:, :, :end]))
    return jnp.concatenate(outs, axis=2)

def setup_inputs(seed: int = 0) -> dict:
    key = jax.random.key(seed)
    ks = jax.random.split(key, 24)
    f32 = jnp.float32

    def dense(k, fan_in, fan_out):
        return jax.random.normal(k, (DEPTH, fan_in, fan_out), f32) * fan_in ** -0.5

    def gain(k, n):
        return 1.0 + 0.05 * jax.random.normal(k, (DEPTH, n), f32)

    def small(k, n, scale=0.01):
        return scale * jax.random.normal(k, (DEPTH, n), f32)

    return {
        "x": jax.random.normal(ks[0], (BATCH, SEQ, D_MODEL), f32),
        "norm_mix": gain(ks[1], D_MODEL),
        "w_in": dense(ks[2], D_MODEL, D_IN_PROJ),
        "b_forget": 2.0 + 0.5 * jax.random.normal(ks[3], (DEPTH, N_HEADS_FOX), f32),
        "qnorm_diff": gain(ks[4], DIFF_QK_DIM),
        "knorm_diff": gain(ks[5], DIFF_QK_DIM),
        "lambda_q1": small(ks[6], DIFF_QK_DIM, 0.1),
        "lambda_k1": small(ks[7], DIFF_QK_DIM, 0.1),
        "lambda_q2": small(ks[8], DIFF_QK_DIM, 0.1),
        "lambda_k2": small(ks[9], DIFF_QK_DIM, 0.1),
        "subln_diff": gain(ks[10], HEAD_DIM),
        "qnorm_fox": gain(ks[11], HEAD_DIM),
        "knorm_fox": gain(ks[12], HEAD_DIM),
        "w_branch_diff": dense(ks[13], WIDTH_DIFF, D_MODEL),
        "w_branch_fox": dense(ks[14], WIDTH_FOX, D_MODEL),
        "w_gate": dense(ks[15], D_MODEL, 2 * D_MODEL),
        "b_gate": small(ks[16], 2 * D_MODEL),
        "w_out": dense(ks[17], D_MODEL, D_MODEL),
        "norm_mlp": gain(ks[18], D_MODEL),
        "w_mlp_up": dense(ks[19], D_MODEL, D_FF),
        "w_mlp_down": dense(ks[20], D_FF, D_MODEL),
    }

def reference(x, norm_mix, w_in, b_forget, qnorm_diff, knorm_diff, lambda_q1, lambda_k1,
              lambda_q2, lambda_k2, subln_diff, qnorm_fox, knorm_fox, w_branch_diff, w_branch_fox,
              w_gate, b_gate, w_out, norm_mlp, w_mlp_up, w_mlp_down):
    B, S, D = x.shape
    slopes = alibi_slopes(N_HEADS_DIFF)
    for layer in range(DEPTH):
        lambda_init = 0.8 - 0.6 * math.exp(-0.3 * layer)

        h = rms_norm(x, norm_mix[layer])
        proj = h @ w_in[layer]
        qa = proj[..., :OFF_QA]
        ka = proj[..., OFF_QA:OFF_KA]
        va = proj[..., OFF_KA:OFF_VA]
        qb = proj[..., OFF_VA:OFF_QB]
        kb = proj[..., OFF_QB:OFF_KB]
        vb = proj[..., OFF_KB:OFF_VB]
        f_logit = proj[..., OFF_VB:]

        qa = rms_norm(qa.reshape(B, S, N_HEADS_DIFF, 2, DIFF_QK_DIM), qnorm_diff[layer])
        ka = rms_norm(ka.reshape(B, S, N_HEADS_DIFF, 2, DIFF_QK_DIM), knorm_diff[layer])
        qa = jnp.transpose(qa, (0, 2, 3, 1, 4))
        ka = jnp.transpose(ka, (0, 2, 3, 1, 4))
        va = jnp.transpose(va.reshape(B, S, N_HEADS_DIFF, HEAD_DIM), (0, 2, 1, 3))
        lam = (jnp.exp(jnp.sum(lambda_q1[layer] * lambda_k1[layer]).astype(jnp.float32))
               - jnp.exp(jnp.sum(lambda_q2[layer] * lambda_k2[layer]).astype(jnp.float32))
               + lambda_init)
        oa = diff_attention(qa[:, :, 0], qa[:, :, 1], ka[:, :, 0], ka[:, :, 1], va, lam, slopes)
        oa = rms_norm(oa, subln_diff[layer]) * (1.0 - lambda_init)
        oa = jnp.transpose(oa, (0, 2, 1, 3)).reshape(B, S, WIDTH_DIFF)

        qb = rms_norm(qb.reshape(B, S, N_HEADS_FOX, HEAD_DIM), qnorm_fox[layer])
        kb = rms_norm(kb.reshape(B, S, N_HEADS_FOX, HEAD_DIM), knorm_fox[layer])
        qb = jnp.transpose(qb, (0, 2, 1, 3))
        kb = jnp.transpose(kb, (0, 2, 1, 3))
        vb = jnp.transpose(vb.reshape(B, S, N_HEADS_FOX, HEAD_DIM), (0, 2, 1, 3))
        log_f = jax.nn.log_sigmoid(f_logit.astype(jnp.float32) + b_forget[layer].astype(jnp.float32))
        log_f_cum = jnp.transpose(jnp.cumsum(log_f, axis=1), (0, 2, 1))
        ob = forgetting_attention(qb, kb, vb, log_f_cum)
        ob = jnp.transpose(ob, (0, 2, 1, 3)).reshape(B, S, WIDTH_FOX)

        gates = jax.nn.sigmoid((h @ w_gate[layer] + b_gate[layer]).astype(jnp.float32)).astype(h.dtype)
        g_diff = gates[..., :D_MODEL]
        g_fox = gates[..., D_MODEL:]
        merged = g_diff * (oa @ w_branch_diff[layer]) + g_fox * (ob @ w_branch_fox[layer])
        x = x + merged @ w_out[layer]

        h2 = rms_norm(x, norm_mlp[layer])
        u = jax.nn.relu(h2 @ w_mlp_up[layer])
        x = x + (u * u) @ w_mlp_down[layer]
    return x


_drawn_inputs = setup_inputs


def setup_inputs(seed=0):
    import zlib

    import numpy as np

    out = dict(_drawn_inputs(seed))
    spreads = {}
    factors = {'qnorm_diff': 3.07,
     'lambda_q1': 132.872,
     'lambda_k2': 166.166,
     'qnorm_fox': 6.37,
     'knorm_fox': 7.322,
     'b_gate': 24.169,
     'lambda_k1': 4.879}
    for name, (base, spread) in spreads.items():
        noise = np.random.default_rng([zlib.crc32(name.encode()), seed]).standard_normal(out[name].shape)
        drawn = base * np.exp(spread * noise) if base else spread * noise
        out[name] = __import__('jax').numpy.asarray(drawn.astype(out[name].dtype))
    for name, factor in factors.items():
        out[name] = (out[name] * factor).astype(out[name].dtype)
    return out
```

```python
import math
from contextlib import ExitStack

import concourse.bass as bass
from concourse import mybir

F32 = mybir.dt.float32
F32R = mybir.dt.float32r
ACT = mybir.ActivationFunctionType
ALU = mybir.AluOpType

P = 128
KU = 4
SPLITS = 4
RAWS = 4
LEAD = 3
EPS = 1e-6
SOFTMAX_STEPS = (13, 14, 16, 18)
MASKED = 1e30
LAMBDA_INIT = 0.8 - 0.6 * math.exp(-0.3 * 0)


def at_least(eng, sem, value):
    if not (isinstance(value, int) and value <= 0):
        eng.wait_ge(sem, value)


class Work:

    def __init__(self, unit, job, loop=0, units_per_turn=0, jobs_per_turn=0):
        assert units_per_turn % (2 * RAWS) == 0 and jobs_per_turn % 2 == 0
        self.unit, self.job = unit, job
        self.loop, self.upt, self.jpt = loop, units_per_turn, jobs_per_turn

    def then(self, units, jobs=1):
        return Work(self.unit + units, self.job + jobs, self.loop, self.upt, self.jpt)

    def units_done(self, n):
        return self.unit + n + self.loop * self.upt if self.upt else self.unit + n

    def loads(self, n):
        half = (self.unit + n) // 2
        v = 16 * (half // RAWS + 1)
        return v + self.loop * (16 * self.upt // 2 // RAWS) if self.upt else v

    def bank(self):
        return self.job % 2


def tile(tensor, m):
    return tensor[:, m] if isinstance(m, int) else tensor[:, bass.ds(m, 1)].rearrange("p a s -> p (a s)")


def build(nc, x, norm_mix, w_in, b_forget, qnorm_diff, knorm_diff, lambda_q1, lambda_k1, lambda_q2,
          lambda_k2, subln_diff, qnorm_fox, knorm_fox, w_branch_diff, w_branch_fox, w_gate, b_gate,
          w_out, norm_mlp, w_mlp_up, w_mlp_down, out):
    _, S, D = x.shape
    assert x.shape[0] == 1 and w_in.shape[0] == 1 and S == 512
    DT = D // P
    TB = S // P
    HD = qnorm_fox.shape[1]
    WD, WF = w_branch_diff.shape[1], w_branch_fox.shape[1]
    H = WD // P
    NF = b_forget.shape[1]
    FF = w_mlp_up.shape[2]
    CH = FF // D
    JU = DT // KU
    BU = H // KU
    assert HD == P and WF == WD and NF == H == 8 and DT == 16 and CH * D == FF

    FORGET = Work(0, 0)
    HEADS = FORGET.then(JU)
    HU, HJ = 6 * JU, 6
    MERGE = HEADS.then(H * HU, H * HJ)
    MU, MJ = 2 * JU + 2 * BU, 4
    PROJ = MERGE.then(DT * MU, DT * MJ)
    MLP = PROJ.then(DT * JU, DT)
    CU, CJ = 2 * DT * JU, 2 * DT
    ALL_UNITS = MLP.unit + CH * CU

    xt = x[0].rearrange("(b p) d -> p b d", p=P)
    outt = out[0].rearrange("(b p) d -> p b d", p=P)

    with ExitStack() as ctx:
        def sb(name, shape, dt=F32):
            return ctx.enter_context(nc.sbuf_tensor(name, shape, dt))

        def sem(name):
            return ctx.enter_context(nc.semaphore(name))

        a_hi, a_lo = sb("a_hi", [P, DT, S], F32R), sb("a_lo", [P, DT, S], F32R)
        b_hi, b_lo = sb("b_hi", [P, DT, S], F32R), sb("b_lo", [P, DT, S], F32R)
        main = sb("main", [P, DT, S])
        side = sb("side", [P, 4, S])
        raw = sb("raw", [P, RAWS, 2 * KU, P])
        w_hi, w_lo = sb("w_hi", [P, SPLITS, KU, P], F32R), sb("w_lo", [P, SPLITS, KU, P], F32R)
        spare = sb("spare", [P, S])
        f_row = sb("f_row", [H, S])
        ident = sb("ident", [P, P])
        ones = sb("ones", [P, P])
        causal = sb("causal", [P, P])
        cols = sb("cols", [P, P])
        neg_bgate = sb("neg_bgate", [P, 2 * DT])
        gains = sb("gains", [P, 8])
        mean2 = sb("mean2", [P, 4])
        stat = sb("stat", [P, 5, 8])
        bforget = sb("bforget", [P, NF])
        lf = sb("lf", [P, TB, NF])
        lf_t = sb("lf_t", [P, 3, TB, NF])
        neg_f = sb("neg_f", [P, TB, H])
        lam = sb("lam", [P, 6])
        pause = sb("pause", [P, 1])
        one_half = sb("one_half", [P, 1])
        row_min, row_sum, row_inv = sb("row_min", [P, 2]), sb("row_sum", [P, 2]), sb("row_inv", [P, 2])

        x_tok = main[:, :, :].rearrange("p (b f) s -> p b (f s)", b=TB)
        qn, kn = [main[:, 0], main[:, 2]], [main[:, 1], main[:, 3]]
        v_tok = [main[:, 4], main[:, 5]]
        v_feat, squares, scaled = main[:, 6], main[:, 7], main[:, 8]
        r_wide = squares
        p_keys = main[:, 9:13]
        bias_fox = main[:, 13:16].rearrange("p a s -> p (a s)")
        f_pick = bias_fox[0:H, 0:S]
        bias_at = [P * b * (b + 1) // 2 for b in range(TB + 1)]
        logits = [side[:, 0], side[:, 1]]
        probs = [side[:, 2], side[:, 3]]
        x_slot, x_feat, x_sq = [side[:, 0], side[:, 1]], side[:, 2], side[:, 3]
        fin, stage = [side[:, 0], side[:, 1]], [side[:, 2], side[:, 3]]
        gate_d, gate_f, part_d, part_f = (side[:, j] for j in (1, 2, 3, 0))
        relu_in, relu_sq = side[:, 0], side[:, 1]
        param_rows, f_feat, tri = side[:, 0, 0:P], side[:, 1], side[:, 2]
        q_gain = [gains[:, 0:1], gains[:, 1:2]]
        k_gain = [cols[:, 68:69], cols[:, 66:67]]
        o_gain = gains[:, 2:3]
        lam_col = lam[:, 4:5]

        jobs = [ctx.enter_context(nc.psum_tensor(f"job{i}", [P, S], F32)) for i in range(2)]
        scores = [ctx.enter_context(nc.psum_tensor(f"scores{i}", [P, S], F32)) for i in range(2)]
        turned = ctx.enter_context(nc.psum_tensor("turned", [P, S], F32))
        wide = ctx.enter_context(nc.psum_tensor("wide", [P, S], F32))
        stats = ctx.enter_context(nc.psum_tensor("stats", [P, S], F32))
        heads_out = ctx.enter_context(nc.psum_tensor("heads_out", [P, S], F32))
        turn4 = [scores[0], scores[1], turned, wide]

        raw_loaded = [sem(f"raw_loaded{i}") for i in range(RAWS)]
        x_loaded = [sem(f"x_loaded{i}") for i in range(TB)]
        (rows_cleared, params_loaded, bforget_loaded, ident_ready, consts_ready, tri_ready,
         cols_turned, cols_ready, gains_ready, lam_product, lam_sums, lam_exps, lam_step,
         x_summed, x_eps, x_guess, x_newton, x_scaled, x_turned, h_hi, h_ready,
         hi_ready, split_ready, unit_used) = (sem(n) for n in (
             "rows_cleared", "params_loaded", "bforget_loaded", "ident_ready", "consts_ready",
             "tri_ready", "cols_turned", "cols_ready", "gains_ready", "lam_product", "lam_sums",
             "lam_exps", "lam_step", "x_summed", "x_eps", "x_guess", "x_newton", "x_scaled",
             "x_turned", "h_hi", "h_ready", "hi_ready", "split_ready", "unit_used"))
        (f_copied, f_turned, f_logit, f_neg, f_exp, f_one, f_ln, f_ready, f_summed, f_row_ready,
         f_back, neg_f_ready) = (sem(n) for n in (
             "f_copied", "f_turned", "f_logit", "f_neg", "f_exp", "f_one", "f_ln", "f_ready", "f_summed",
             "f_row_ready", "f_back", "neg_f_ready"))
        (sq_ready, stat_ready, eps_ready, ln_ready, guess_ready, newton1, newton2, newton3,
         r_ready, wide_ready, norm_ready) = (sem(n) for n in (
             "sq_ready", "stat_ready", "eps_ready", "ln_ready", "guess_ready", "newton1",
             "newton2", "newton3", "r_ready", "wide_ready", "norm_ready"))
        (scores_ready, logits_ready, exp_ready, inv_ready, second_scaled, probs_ready,
         probs_turned, p_keys_ready) = (sem(n) for n in (
             "scores_ready", "logits_ready", "exp_ready", "inv_ready", "second_scaled",
             "probs_ready", "probs_turned", "p_keys_ready"))
        (v_copied, v_turned, v_ready, pv_ready, o_copied, o_hi, o_ready, f_picked, f_wide,
         bias_open, bias_ready, dist_ready) = (sem(n) for n in (
             "v_copied", "v_turned", "v_ready", "pv_ready", "o_copied", "o_hi", "o_ready",
             "f_picked", "f_wide", "bias_open", "bias_ready", "dist_ready"))
        (gate_exp, gate_one, gate_ready, parts_ready, merged_ready, m_hi, m_ready) = (
            sem(n) for n in ("gate_exp", "gate_one", "gate_ready", "parts_ready", "merged_ready",
                             "m_hi", "m_ready"))
        xr_loaded = [sem(f"xr_loaded{i}") for i in range(2)]
        (xr_turned, xr_ready, x2_ready, x2_sq, x2_hi, x2_lo, sum_ready,
         rms_ready) = (sem(n) for n in (
             "xr_turned", "xr_ready", "x2_ready", "x2_sq", "x2_hi", "x2_lo",
             "sum_ready", "rms_ready"))
        (up_scaled, up_squared, up_hi, up_ready, down_added, fin_ready, fin_turned,
         stage_ready) = (sem(n) for n in (
             "up_scaled", "up_squared", "up_hi", "up_ready", "down_added", "fin_ready",
             "fin_turned", "stage_ready"))
        out_stored = [sem(f"out_stored{i}") for i in range(2)]


        def head_hooks(step, u, i, work):
            half = HU // 2
            if not (isinstance(i, int) and i == 0):
                before = work.then(-HU, -HJ)
                step(0, i - 1, u + HU, before)
                step(1, i - 1, u + half, before.then(half, HJ // 2))
            if not (isinstance(i, int) and i == H):
                step(0, i, u, work)
                step(1, i, u - half, work.then(half, HJ // 2))

        block = ctx.enter_context(nc.Block())

        @block.sync
        def _(sp):
            def load_half(work, half, source):
                slot = (work.unit // 2 + half) % RAWS
                at_least(sp, split_ready, work.units_done(2 * half) - 2 * RAWS + 2)
                sp.dma_start(raw[:, slot], source).then_inc(raw_loaded[slot], 16)

            def load_job(work, weights, col, halves=2):
                w = weights[0].rearrange("(k p) c -> p k c", p=P)
                for half in range(halves):
                    k = 2 * KU * half
                    load_half(work, half, w[:, k:k + 2 * KU, bass.ds(col, P)])

            for b in range(TB):
                sp.dma_start(x_tok[:, b], xt[:, b]).then_inc(x_loaded[b], 16)
            load_job(FORGET, w_in, w_in.shape[2] - P)

            def head_loads(work, i):
                for j in range(HJ):
                    load_job(work.then(j * JU, j), w_in, i * P + j * WD)

            head_loads(HEADS, 0)
            with sp.Fori(1, H) as i:
                head_loads(Work(HEADS.unit, HEADS.job, i, HU, HJ), i)

            def merge_loads(work, m):
                load_job(work, w_gate, m * P)
                load_job(work.then(JU), w_gate, m * P + D)
                load_job(work.then(2 * JU, 2), w_branch_diff, m * P, halves=1)
                load_job(work.then(2 * JU + BU, 3), w_branch_fox, m * P, halves=1)

            with sp.Fori(0, DT // 2) as i:
                work = Work(MERGE.unit, MERGE.job, i, 2 * MU, 2 * MJ)
                for j in range(2):
                    merge_loads(work.then(j * MU, j * MJ), i * 2 + j)

            def load_residual(j, m):
                at_least(sp, xr_turned, m - 1)
                sp.dma_start(x_slot[j].rearrange("p (b f) -> p b f", b=TB),
                             xt[:, :, bass.ds(m * P, P)]).then_inc(xr_loaded[j], 16)

            load_job(PROJ, w_out, 0)
            load_job(PROJ.then(JU), w_out, P)
            sp.wait_ge(merged_ready, DT)
            load_residual(0, 0)
            load_residual(1, 1)
            with sp.Fori(1, DT // 2) as i:
                work = Work(PROJ.unit, PROJ.job, i, 2 * JU, 2)
                for j in range(2):
                    load_job(work.then(j * JU), w_out, i * (2 * P) + j * P)
                    load_residual(j, i * 2 + j)

            with sp.Fori(0, CH) as c:
                with sp.Fori(0, DT // 2) as i:
                    work = Work(MLP.unit, MLP.job, c * DT + i, 2 * JU, 2)
                    for j in range(2):
                        load_job(work.then(j * JU), w_mlp_up, c * D + i * (2 * P) + j * P)
                with sp.Fori(0, DT // 2) as i:
                    work = Work(MLP.unit + DT * JU, MLP.job + DT, c * DT + i, 2 * JU, 2)
                    for j in range(2):
                        for half in range(2):
                            src = w_mlp_down[0, bass.ds(c * D + half * 2 * KU * P, 2 * KU * P),
                                             bass.ds(i * (2 * P) + j * P, P)]
                            load_half(work.then(j * JU), half, src.rearrange("(k p) c -> p k c", p=P))

        @block.gpsimd
        def _(pool):
            pool.memset(param_rows, 0.0).then_inc(rows_cleared, 1)
            pool.memset(ident[:, :], 0.0).then_inc(consts_ready, 1)
            pool.memset(ones[:, :], 1.0).then_inc(consts_ready, 1)
            pool.memset(causal[:, :], 0.0).then_inc(consts_ready, 1)
            pool.memset(mean2[:, 0:2], 1.0 / 64).then_inc(consts_ready, 1)
            pool.memset(mean2[:, 2:4], 1.0 / 128).then_inc(consts_ready, 1)
            pool.memset(tri, 1.0).then_inc(consts_ready, 1)
            pool.memset(one_half[:, :], 0.5).then_inc(consts_ready, 1)
            pool.wait_ge(consts_ready, 7)
            pool.affine_select(out=ident[:, :], in_=ident[:, :], compare_op=ALU.not_equal, fill=1.0,
                               base=0, pattern=[[-1, P]], channel_multiplier=1).then_inc(ident_ready, 1)
            pool.affine_select(out=mean2[:, 0:1], in_=mean2[:, 0:1], compare_op=ALU.is_ge, fill=0.0,
                               base=63, pattern=[[0, 1]], channel_multiplier=-1).then_inc(consts_ready, 1)
            pool.affine_select(out=mean2[:, 1:2], in_=mean2[:, 1:2], compare_op=ALU.is_ge, fill=0.0,
                               base=-64, pattern=[[0, 1]], channel_multiplier=1).then_inc(consts_ready, 1)
            pool.affine_select(out=causal[:, :], in_=causal[:, :], compare_op=ALU.is_ge, fill=MASKED,
                               base=0, pattern=[[-1, P]], channel_multiplier=1).then_inc(consts_ready, 1)
            pool.affine_select(out=tri, in_=tri, compare_op=ALU.is_ge, fill=0.0,
                               base=0, pattern=[[1, S]], channel_multiplier=-1).then_inc(tri_ready, 1)
            pool.iota(spare[:, :], [[-1, S]], base=S - P, channel_multiplier=1,
                      allow_small_or_imprecise_dtypes=True).then_inc(dist_ready, 1)
            pool.wait_ge(dist_ready, 1)
            pool.tensor_scalar(side[:, 3], spare[:, :], 0.0, 1.0, ALU.max, ALU.mult).then_inc(dist_ready, 1)
            pool.tensor_scalar(spare[:, :], spare[:, :], -0.5, 0.0, ALU.mult, ALU.add).then_inc(dist_ready, 1)
            pool.wait_ge(dist_ready, 3)
            pool.tensor_tensor(spare[:, :], spare[:, :], side[:, 3], ALU.add).then_inc(dist_ready, 1)
            pool.wait_ge(dist_ready, 4)
            pool.memset(spare[0:64, S - 64:S], MASKED * 2 ** H).then_inc(dist_ready, 1)
            with pool.Fori(0, H) as i:
                pool.wait_ge(logits_ready, i * (2 * TB) + TB)
                pool.wait_ge(dist_ready, i + 5)
                pool.wait_ge(consts_ready, 10)
                pool.tensor_tensor(spare[:, :], spare[:, :], one_half[:, :].broadcast_to([P, S]),
                                   ALU.mult).then_inc(dist_ready, 1)
                pool.wait_ge(bias_open, i * TB + TB)
                for b in range(TB):
                    diagonal = bias_fox[:, bias_at[b + 1] - P:bias_at[b + 1]]
                    pool.tensor_tensor(diagonal, diagonal, causal[:, :], ALU.add).then_inc(bias_ready, 1)

        @block.scalar
        def _(act):
            def round_unit(work, n):
                u = work.unit + n
                if not work.upt and u >= ALL_UNITS:
                    return
                slot, part = u // 2 % RAWS, KU * (u % 2)
                act.wait_ge(raw_loaded[slot], work.loads(n))
                at_least(act, unit_used, work.units_done(n + 1) - SPLITS)
                nc.scalar.activation(w_hi[:, u % SPLITS], raw[:, slot, part:part + KU],
                                     ACT.Copy).then_inc(hi_ready, 1)

            def guess(n):
                act.wait_ge(eps_ready, n + 1)
                nc.scalar.activation(stat[:, 1], stat[:, 0], ACT.Ln).then_inc(ln_ready, 1)
                act.wait_ge(ln_ready, n + 1)
                nc.scalar.activation(stat[:, 2], stat[:, 1], ACT.Exp, scale=-0.5).then_inc(guess_ready, 1)

            def take_for_norm(work, n, gain):
                act.wait_ge(unit_used, work.units_done(JU))
                at_least(act, norm_ready, n)
                nc.scalar.activation(scaled, jobs[work.bank()][:, :], ACT.Copy, scale=gain)
                nc.scalar.activation(squares, jobs[work.bank()][:, :], ACT.Square).then_inc(sq_ready, 1)

            def head_step(kind, i, t, work):
                n = i * 5 + 2 * kind
                if t == JU:
                    if kind == 0:
                        at_least(act, o_ready, i * 2 - 1)
                    take_for_norm(work, n, q_gain[kind])
                if t == JU + 1:
                    guess(n)
                if t == 2 * JU:
                    take_for_norm(work.then(JU), n + 1, k_gain[kind])
                if t == 2 * JU + 1:
                    guess(n + 1)
                if t == 3 * JU:
                    values = work.then(2 * JU, 2)
                    act.wait_ge(unit_used, values.units_done(JU))
                    at_least(act, v_turned, i * 2 + kind)
                    nc.scalar.activation(v_feat, jobs[values.bank()][:, :], ACT.Copy).then_inc(v_copied, 1)
                if t == 3 * JU and kind == 1:
                    act.wait_ge(f_wide, i + 1)
                    for b in range(TB):
                        nc.scalar.activation(bias_fox[:, bias_at[b]:bias_at[b + 1]], scores[1][:, 0:P * (b + 1)],
                                             ACT.Identity, bias=neg_f[:, b, bass.ds(i, 1)]).then_inc(bias_open, 1)
                for b, when in enumerate(SOFTMAX_STEPS):
                    if t == when:
                        block_no = i * (2 * TB) + TB * kind + b
                        act.wait_ge(logits_ready, block_no + 1)
                        for m in range(2 - kind):
                            e = nc.scalar.activation(logits[m][:, 0:P * (b + 1)], logits[m][:, 0:P * (b + 1)],
                                                     ACT.Exp, scale=-1.0, bias=row_min[:, m:m + 1],
                                                     accum_out=row_sum[:, m:m + 1])
                        e.then_inc(exp_ready, 1)
                if kind == 1 and t == 22:
                    act.wait_ge(pv_ready, i * 2 + 2)
                    nc.scalar.activation(logits[0], heads_out[:, :], ACT.Copy).then_inc(o_copied, 1)
                    act.wait_ge(o_copied, i * 2 + 2)
                    nc.scalar.activation(tile(b_hi, i + H), logits[0], ACT.Copy).then_inc(o_hi, 1)
                if kind == 0 and t == 24:
                    act.wait_ge(pv_ready, i * 2 + 1)
                    act.wait_ge(norm_ready, n + 4)
                    nc.scalar.activation(scaled, heads_out[:, :], ACT.Copy, scale=o_gain).then_inc(o_copied, 1)
                    nc.scalar.activation(squares, heads_out[:, :], ACT.Square).then_inc(sq_ready, 1)
                if kind == 0 and t == 25:
                    guess(n + 4)
                if kind == 0 and t == 27:
                    act.wait_ge(norm_ready, n + 5)
                    nc.scalar.activation(tile(b_hi, i), squares, ACT.Copy).then_inc(o_hi, 1)

            act.wait_ge(rows_cleared, 1)
            for r, (vector, n) in enumerate(((norm_mix, DT), (norm_mlp, DT), (b_gate, 2 * DT))):
                r = (0, DT, 2 * DT)[r]
                act.dma_start(side[r:r + n, 0, 0:P], vector.rearrange("a (r p) -> (a r) p", p=P)
                              ).then_inc(params_loaded, 16)
            for r, c, vector in ((64, 0, subln_diff), (65, 0, qnorm_fox), (66, 0, knorm_fox),
                                 (67, 0, qnorm_diff), (67, 64, qnorm_diff), (68, 0, knorm_diff),
                                 (68, 64, knorm_diff), (69, 0, lambda_q1), (69, 64, lambda_q2),
                                 (70, 0, lambda_k1), (70, 64, lambda_k2)):
                act.dma_start(side[r:r + 1, 0, c:c + vector.shape[1]], vector).then_inc(params_loaded, 16)
            act.dma_start(bforget[:, :], b_forget[0:1, :].broadcast_to([P, NF])).then_inc(bforget_loaded, 16)

            for b in range(TB):
                act.wait_ge(x_loaded[b], 16)
                nc.scalar.activation(b_hi[:, 4 * b:4 * b + 4].rearrange("p a s -> p (a s)"), x_tok[:, b], ACT.Square,
                                     accum_out=stat[:, 0, b:b + 1]).then_inc(x_summed, 1)
            act.wait_ge(x_eps, 1)
            nc.scalar.activation(stat[:, 2, 0:TB], stat[:, 1, 0:TB], ACT.Ln).then_inc(x_guess, 1)
            act.wait_ge(x_guess, 1)
            nc.scalar.activation(stat[:, 3, 0:TB], stat[:, 2, 0:TB], ACT.Exp, scale=-0.5).then_inc(x_guess, 1)
            act.wait_ge(lam_sums, 1)
            nc.scalar.activation(lam[:, 2:4], stats[:, 0:2], ACT.Exp, scale=64.0).then_inc(lam_exps, 1)
            for n in range(LEAD):
                round_unit(FORGET, n)
            act.wait_ge(cols_ready, 1)
            for k in range(DT):
                act.wait_ge(x_turned, k + 1)
                nc.scalar.activation(a_hi[:, k], turn4[k % 4][:, :], ACT.Copy,
                                     scale=cols[:, k:k + 1]).then_inc(h_hi, 1)
            for n in range(JU):
                round_unit(FORGET, n + LEAD)
            act.wait_ge(unit_used, FORGET.units_done(JU))
            nc.scalar.activation(f_feat, jobs[FORGET.bank()][:, :], ACT.Copy).then_inc(f_copied, 1)

            def heads_turn(i, work):
                for u in range(HU):
                    round_unit(work, u + LEAD)
                    if isinstance(i, int) and i == 0 and u == 0:
                        act.wait_ge(f_neg, 1)
                        nc.scalar.activation(lf_t[:, 2], lf_t[:, 1], ACT.Exp).then_inc(f_exp, 1)
                        act.wait_ge(f_one, 1)
                        nc.scalar.activation(lf_t[:, 1], lf_t[:, 2], ACT.Ln).then_inc(f_ln, 1)
                    head_hooks(head_step, u, i, work)

            heads_turn(0, HEADS)
            with act.Fori(1, H) as i:
                heads_turn(i, Work(HEADS.unit, HEADS.job, i, HU, HJ))

            def merge(m, work, last=False):
                for u in range(MU):
                    round_unit(work, u + LEAD)
                    if isinstance(m, int) and m == 0:
                        head_hooks(head_step, u, H, work)
                    for g, gate in enumerate((gate_d, gate_f)):
                        if u == (g + 1) * JU - 1:
                            act.wait_ge(unit_used, work.units_done((g + 1) * JU))
                            at_least(act, merged_ready, m)
                            if isinstance(m, int) and m == 0:
                                act.wait_ge(probs_turned, 2 * TB * H if g else 2 * TB * H - TB)
                                at_least(act, o_ready, 2 * H - 1)
                            nc.scalar.activation(gate, jobs[work.then(0, g).bank()][:, :], ACT.Exp, scale=-1.0,
                                                 bias=neg_bgate[:, bass.ds(m + g * DT, 1)]).then_inc(gate_exp, 1)
                    if last and u >= 2 * JU:
                        for k in range((u - 2 * JU) * 3, (u - 2 * JU) * 3 + 3):
                            round_merged(k)

            def round_merged(k):
                act.wait_ge(unit_used, MERGE.unit + (DT - 1) * MU + 2 * JU)
                act.wait_ge(merged_ready, k + 1)
                nc.scalar.activation(a_hi[:, k], main[:, k], ACT.Copy).then_inc(m_hi, 1)

            merge(0, MERGE)
            with act.Fori(0, DT // 2 - 1) as i:
                work = Work(MERGE.unit + MU, MERGE.job + MJ, i, 2 * MU, 2 * MJ)
                merge(i * 2 + 1, work)
                merge(i * 2 + 2, work.then(MU, MJ))
            merge(DT - 1, MERGE.then((DT - 1) * MU, (DT - 1) * MJ), last=True)
            for k in range(2 * BU * 3, DT):
                round_merged(k)

            def projected(m, work):
                for u in range(JU):
                    round_unit(work, u + LEAD)
                    if u == 2:
                        act.wait_ge(xr_turned, m + 1)
                        act.wait_ge(sum_ready, m + 1)
                        nc.scalar.activation(x_feat, turned[:, :], ACT.Copy).then_inc(xr_ready, 1)
                act.wait_ge(x2_ready, m + 1)
                act.wait_ge(sum_ready, m + 1)
                nc.scalar.activation(x_sq, tile(main, m), ACT.Square).then_inc(x2_sq, 1)
                nc.scalar.activation(tile(b_hi, m), tile(main, m), ACT.Copy,
                                     scale=cols[:, bass.ds(m + DT, 1)]).then_inc(x2_hi, 1)

            with act.Fori(0, DT // 2) as i:
                work = Work(PROJ.unit, PROJ.job, i, 2 * JU, 2)
                for j in range(2):
                    projected(i * 2 + j, work.then(j * JU, j))

            def up(m, c, work, first=False):
                for u in range(JU):
                    round_unit(work, u + LEAD)
                    if first and u == 1:
                        guess(5 * H)
                    if first and u == 3:
                        act.wait_ge(wide_ready, 5 * H + 1)
                        nc.scalar.activation(spare[:, :], wide[:, :], ACT.Copy).then_inc(rms_ready, 1)
                act.wait_ge(up_squared, c * DT + m + 1)
                nc.scalar.activation(tile(a_hi, m), relu_sq, ACT.Copy).then_inc(up_hi, 1)

            def ups(c, first_turn):
                with act.Fori(first_turn, DT // 2) as i:
                    work = Work(MLP.unit, MLP.job, c * DT + i, 2 * JU, 2)
                    for j in range(2):
                        up(i * 2 + j, c, work.then(j * JU, j))

            def down_rounds(c):
                with act.Fori(0, DT // 2) as i:
                    work = Work(MLP.unit + DT * JU, MLP.job + DT, c * DT + i, 2 * JU, 2)
                    for u in range(2 * JU):
                        round_unit(work, u + LEAD)

            for j in range(2):
                up(j, 0, MLP.then(j * JU, j), first=j == 0)
            ups(0, 1)
            down_rounds(0)
            with act.Fori(1, CH - 1) as c:
                ups(c, 0)
                down_rounds(c)
            ups(CH - 1, 0)

            def store(j, m):
                act.wait_ge(fin_turned, m + 1)
                if j == 0:
                    at_least(act, out_stored[0], m * 8)
                else:
                    at_least(act, out_stored[1], m * 8 - 8)
                nc.scalar.activation(stage[j], (turned, wide)[j][:, :], ACT.Copy).then_inc(stage_ready, 1)
                act.wait_ge(stage_ready, m + 1)
                act.dma_start(outt[:, :, bass.ds(m * P, P)], stage[j].rearrange("p (b f) -> p b f", b=TB)
                              ).then_inc(out_stored[j], 16)

            LAST = MLP.then((CH - 1) * CU + DT * JU, (CH - 1) * CJ + DT)

            def last_down(m, work, j):
                for u in range(JU):
                    round_unit(work, u + LEAD)
                    if u == 2 and not (isinstance(m, int) and m == 0):
                        store(1 - j, m - 1)

            last_down(0, LAST, 0)
            for m in (1, 2):
                last_down(m, LAST.then(m * JU, m), m % 2)
            with act.Fori(1, DT // 2 - 1) as i:
                work = Work(LAST.unit + JU, LAST.job + 1, i, 2 * JU, 2)
                last_down(i * 2 + 1, work, 1)
                last_down(i * 2 + 2, work.then(JU), 0)
            last_down(DT - 1, LAST.then((DT - 1) * JU, DT - 1), 1)
            store(1, DT - 1)
            for j in range(2):
                act.wait_ge(out_stored[j], 16 * (DT // 2))

        @block.vector
        def _(dve):
            def split_unit(work, n):
                u = work.unit + n
                if not work.upt and u >= ALL_UNITS:
                    return
                slot, part = u // 2 % RAWS, KU * (u % 2)
                dve.wait_ge(hi_ready, work.units_done(n + 1))
                nc.vector.tensor_tensor(w_lo[:, u % SPLITS], raw[:, slot, part:part + KU],
                                        w_hi[:, u % SPLITS].bitcast(F32), ALU.subtract).then_inc(split_ready, 1)

            def mean_square(n, share=1.0):
                dve.wait_ge(stat_ready, n + 1)
                nc.vector.tensor_scalar(stat[:, 0], stats[:, 0:8], share, EPS, ALU.mult, ALU.add).then_inc(eps_ready, 1)

            def refine(n, into):
                dve.wait_ge(guess_ready, n + 1)
                nc.vector.tensor_tensor(stat[:, 3], stat[:, 2], stat[:, 2], ALU.mult).then_inc(newton1, 1)
                dve.wait_ge(newton1, n + 1)
                nc.vector.tensor_tensor(stat[:, 4], stat[:, 3], stat[:, 0], ALU.mult).then_inc(newton2, 1)
                dve.wait_ge(newton2, n + 1)
                nc.vector.tensor_scalar(stat[:, 3], stat[:, 4], -0.5, 1.5, ALU.mult, ALU.add).then_inc(newton3, 1)
                dve.wait_ge(newton3, n + 1)
                nc.vector.tensor_tensor(into.rearrange("p (a c) -> p a c", c=64),
                                        stat[:, 2].unsqueeze(2).broadcast_to([P, 8, 64]),
                                        stat[:, 3].unsqueeze(2).broadcast_to([P, 8, 64]),
                                        ALU.mult).then_inc(r_ready, 1)

            def scale_by_rms(n, result):
                dve.wait_ge(wide_ready, n + 1)
                nc.vector.tensor_tensor(result, scaled, wide[:, :], ALU.mult).then_inc(norm_ready, 1)

            def take_logits(kind, i, b):
                block_no = i * (2 * TB) + TB * kind + b
                n = P * (b + 1)
                if kind == 0:
                    dve.wait_ge(dist_ready, i + 5)
                else:
                    dve.wait_ge(bias_ready, i * TB + b + 1)
                at_least(dve, probs_ready, block_no)
                dve.wait_ge(scores_ready, block_no + 1)
                nc.vector.memset(pause[:, :], 0.0)
                for m in range(2 - kind):
                    bias = spare[:, S - n:S] if kind == 0 else bias_fox[:, bias_at[b]:bias_at[b + 1]]
                    r = nc.vector.tensor_tensor_reduce(out=logits[m][:, 0:n], in0=scores[m][:, 0:n], in1=bias,
                                                       scale=1.0, scalar=3e38, op0=ALU.add, op1=ALU.min,
                                                       accum_out=row_min[:, m:m + 1])
                r.then_inc(logits_ready, 1)

            def take_probs(kind, i, b):
                block_no = i * (2 * TB) + TB * kind + b
                n = P * (b + 1)
                dve.wait_ge(exp_ready, block_no + 1)
                at_least(dve, probs_turned, block_no - 1)
                maps = 2 - kind
                nc.vector.reciprocal(row_inv[:, 0:maps], row_sum[:, 0:maps]).then_inc(inv_ready, 1)
                dve.wait_ge(inv_ready, block_no + 1)
                if kind == 0:
                    nc.vector.tensor_scalar(logits[1][:, 0:n], logits[1][:, 0:n], row_inv[:, 1:2], lam_col,
                                            ALU.mult, ALU.mult).then_inc(second_scaled, 1)
                    dve.wait_ge(second_scaled, i * TB + b + 1)
                    nc.vector.scalar_tensor_tensor(probs[b % 2][:, 0:n], logits[0][:, 0:n], row_inv[:, 0:1],
                                                   logits[1][:, 0:n], ALU.mult, ALU.subtract).then_inc(probs_ready, 1)
                else:
                    nc.vector.tensor_scalar(probs[b % 2][:, 0:n], logits[0][:, 0:n], row_inv[:, 0:1], None,
                                            ALU.mult).then_inc(probs_ready, 1)

            def keep_turned(kind, i, b):
                block_no = i * (2 * TB) + TB * kind + b
                dve.wait_ge(probs_turned, block_no + 1)
                at_least(dve, pv_ready, i * 2 + kind)
                nc.vector.tensor_copy(p_keys[:, 0:b + 1, P * b:P * (b + 1)],
                                      turned[:, 0:P * (b + 1)].rearrange("p (j q) -> p j q", q=P)
                                      ).then_inc(p_keys_ready, 1)

            def head_step(kind, i, t, work):
                n = i * 5 + 2 * kind
                for first, which, result in ((JU + 1, 0, qn[kind]), (2 * JU + 1, 1, kn[kind])):
                    if t == first:
                        mean_square(n + which)
                    if t == first + 1:
                        refine(n + which, r_wide)
                    if t == first + 2:
                        scale_by_rms(n + which, result)
                if kind == 1 and t == 10:
                    at_least(dve, f_row_ready, 1)
                    nc.vector.tensor_scalar(f_pick, f_row[:, :], ident[0:H, bass.ds(i, 1)], None,
                                            ALU.mult).then_inc(f_picked, 1)
                if t == 13:
                    dve.wait_ge(v_turned, i * 2 + kind + 1)
                    nc.vector.tensor_copy(v_tok[kind], turned[:, :]).then_inc(v_ready, 1)
                for b, when in enumerate(SOFTMAX_STEPS):
                    if t == when + 1:
                        take_probs(kind, i, b)
                for b, when in enumerate(SOFTMAX_STEPS):
                    if t == when:
                        take_logits(kind, i, b)
                    if t == when + 2:
                        keep_turned(kind, i, b)
                if kind == 1 and t == 23:
                    dve.wait_ge(o_hi, i * 2 + 2)
                    nc.vector.tensor_tensor(tile(b_lo, i + H), logits[0], tile(b_hi, i + H).bitcast(F32),
                                            ALU.subtract).then_inc(o_ready, 1)
                if kind == 0 and t == 25:
                    mean_square(n + 4)
                if kind == 0 and t == 26:
                    refine(n + 4, r_wide)
                if kind == 0 and t == 27:
                    scale_by_rms(n + 4, squares)
                    dve.wait_ge(o_hi, i * 2 + 1)
                    nc.vector.tensor_tensor(tile(b_lo, i), squares, tile(b_hi, i).bitcast(F32),
                                            ALU.subtract).then_inc(o_ready, 1)

            dve.wait_ge(cols_turned, 1)
            nc.vector.tensor_copy(cols[:, :], stats[:, 0:P]).then_inc(cols_ready, 1)
            dve.wait_ge(cols_ready, 1)
            nc.vector.tensor_scalar(neg_bgate[:, :], cols[:, 32:64], -1.0, None, ALU.mult)
            nc.vector.tensor_scalar(gains[:, 0:1], cols[:, 67:68], -(HD // 2) ** -0.5, None, ALU.mult)
            nc.vector.tensor_scalar(gains[:, 1:2], cols[:, 65:66], -HD ** -0.5, None, ALU.mult)
            nc.vector.tensor_scalar(gains[:, 2:3], cols[:, 64:65], 1.0 - LAMBDA_INIT, None,
                                    ALU.mult).then_inc(gains_ready, 1)
            nc.vector.tensor_tensor(lam[:, 5:6], cols[:, 69:70], cols[:, 70:71], ALU.mult).then_inc(lam_step, 1)
            dve.wait_ge(lam_step, 1)
            dve.wait_ge(consts_ready, 9)
            nc.vector.tensor_scalar(lam[:, 0:2], mean2[:, 0:2], lam[:, 5:6], None, ALU.mult).then_inc(lam_product, 1)

            dve.wait_ge(x_summed, TB)
            nc.vector.tensor_scalar(stat[:, 1, 0:TB], stat[:, 0, 0:TB], 1.0 / D, EPS, ALU.mult,
                                    ALU.add).then_inc(x_eps, 1)
            dve.wait_ge(x_guess, 2)
            nc.vector.tensor_tensor(stat[:, 4, 0:TB], stat[:, 3, 0:TB], stat[:, 3, 0:TB], ALU.mult).then_inc(x_newton, 1)
            dve.wait_ge(x_newton, 1)
            nc.vector.tensor_tensor(stat[:, 2, 0:TB], stat[:, 4, 0:TB], stat[:, 1, 0:TB], ALU.mult).then_inc(x_newton, 1)
            dve.wait_ge(x_newton, 2)
            nc.vector.tensor_scalar(stat[:, 4, 0:TB], stat[:, 2, 0:TB], -0.5, 1.5, ALU.mult, ALU.add).then_inc(x_newton, 1)
            dve.wait_ge(x_newton, 3)
            nc.vector.tensor_tensor(stat[:, 0, 0:TB], stat[:, 3, 0:TB], stat[:, 4, 0:TB], ALU.mult).then_inc(x_newton, 1)
            dve.wait_ge(x_newton, 4)
            for b in range(TB):
                nc.vector.tensor_scalar(x_tok[:, b], x_tok[:, b], stat[:, 0, b:b + 1], None,
                                        ALU.mult).then_inc(x_scaled, 1)
            dve.wait_ge(lam_exps, 1)
            nc.vector.scalar_tensor_tensor(lam_col, lam[:, 2:3], LAMBDA_INIT, lam[:, 3:4], ALU.add,
                                           ALU.subtract).then_inc(lam_step, 1)
            for n in range(LEAD):
                split_unit(FORGET, n)
            for k in range(DT):
                dve.wait_ge(h_hi, k + 1)
                nc.vector.scalar_tensor_tensor(a_lo[:, k], turn4[k % 4][:, :], cols[:, k:k + 1],
                                               a_hi[:, k].bitcast(F32), ALU.mult, ALU.subtract).then_inc(h_ready, 1)
            for n in range(JU):
                split_unit(FORGET, n + LEAD)

            def forget_logits():
                dve.wait_ge(f_turned, 1)
                dve.wait_ge(bforget_loaded, 16)
                z = heads_out[:, :].rearrange("p (b c) -> p b c", b=TB)[:, :, P - NF:P]
                nc.vector.tensor_tensor(lf_t[:, 0], z, bforget[:, :].unsqueeze(1).broadcast_to([P, TB, NF]),
                                        ALU.add).then_inc(f_logit, 1)
                dve.wait_ge(f_logit, 1)
                nc.vector.scalar_tensor_tensor(lf_t[:, 1], lf_t[:, 0], -1.0, lf_t[:, 0], ALU.mult,
                                               ALU.min).then_inc(f_neg, 1)
                dve.wait_ge(f_exp, 1)
                nc.vector.tensor_scalar(lf_t[:, 2], lf_t[:, 2], 1.0, None, ALU.add).then_inc(f_one, 1)
                dve.wait_ge(f_ln, 1)
                nc.vector.scalar_tensor_tensor(lf[:, :, :], lf_t[:, 0], 0.0, lf_t[:, 1], ALU.min,
                                               ALU.subtract).then_inc(f_ready, 1)

            def heads_turn(i, work):
                first = isinstance(i, int) and i == 0
                for u in range(HU):
                    split_unit(work, u + LEAD)
                    if first and u == 0:
                        forget_logits()
                    if first and u == 2:
                        dve.wait_ge(f_summed, 1)
                        nc.vector.tensor_copy(f_row[:, :], heads_out[0:H, :]).then_inc(f_row_ready, 1)
                    if first and u == 3:
                        dve.wait_ge(f_back, 1)
                        nc.vector.tensor_scalar(neg_f[:, :, :], heads_out[:, 0:TB * H].rearrange("p (b h) -> p b h", b=TB),
                                                -1.0, None, ALU.mult).then_inc(neg_f_ready, 1)
                    head_hooks(head_step, u, i, work)

            heads_turn(0, HEADS)
            with dve.Fori(1, H) as i:
                heads_turn(i, Work(HEADS.unit, HEADS.job, i, HU, HJ))

            def merge(m, work, last=False):
                for u in range(MU):
                    split_unit(work, u + LEAD)
                    if isinstance(m, int) and m == 0:
                        head_hooks(head_step, u, H, work)
                    for g, gate in enumerate((gate_d, gate_f)):
                        if u == (g + 1) * JU:
                            dve.wait_ge(gate_exp, m * 2 + g + 1)
                            nc.vector.tensor_scalar(gate, gate, 1.0, None, ALU.add).then_inc(gate_one, 1)
                            dve.wait_ge(gate_one, m * 2 + g + 1)
                            nc.vector.reciprocal(gate, gate).then_inc(gate_ready, 1)
                    if last and u >= 2 * JU:
                        for k in range((u - 2 * JU) * 3, (u - 2 * JU) * 3 + 3):
                            split_merged(k)
                    for g, gate, part in ((0, gate_d, part_d), (1, gate_f, part_f)):
                        if u == 2 * JU + (g + 1) * BU - 1:
                            dve.wait_ge(gate_ready, m * 2 + g + 1)
                            dve.wait_ge(unit_used, work.units_done(2 * JU + (g + 1) * BU))
                            nc.vector.tensor_tensor(part, jobs[work.then(0, g).bank()][:, :], gate,
                                                    ALU.mult).then_inc(parts_ready, 1)
                dve.wait_ge(parts_ready, m * 2 + 2)
                nc.vector.tensor_tensor(tile(main, m), part_d, part_f, ALU.add).then_inc(merged_ready, 1)

            def split_merged(k):
                dve.wait_ge(m_hi, k + 1)
                nc.vector.tensor_tensor(a_lo[:, k], main[:, k], a_hi[:, k].bitcast(F32),
                                        ALU.subtract).then_inc(m_ready, 1)

            merge(0, MERGE)
            with dve.Fori(0, DT // 2 - 1) as i:
                work = Work(MERGE.unit + MU, MERGE.job + MJ, i, 2 * MU, 2 * MJ)
                merge(i * 2 + 1, work)
                merge(i * 2 + 2, work.then(MU, MJ))
            merge(DT - 1, MERGE.then((DT - 1) * MU, (DT - 1) * MJ), last=True)
            for k in range(2 * BU * 3, DT):
                split_merged(k)

            dve.wait_ge(dist_ready, 5 + H)
            nc.vector.memset(spare[:, :], 0.0).then_inc(sum_ready, 1)

            def projected(m, work):
                for u in range(JU):
                    split_unit(work, u + LEAD)
                dve.wait_ge(unit_used, work.units_done(JU))
                dve.wait_ge(xr_ready, m + 1)
                nc.vector.tensor_tensor(tile(main, m), jobs[work.bank()][:, :], x_feat, ALU.add).then_inc(x2_ready, 1)
                dve.wait_ge(x2_sq, m + 1)
                dve.wait_ge(sum_ready, m + 1)
                nc.vector.tensor_tensor(spare[:, :], spare[:, :], x_sq, ALU.add).then_inc(sum_ready, 1)
                dve.wait_ge(x2_hi, m + 1)
                nc.vector.scalar_tensor_tensor(tile(b_lo, m), tile(main, m), cols[:, bass.ds(m + DT, 1)],
                                               tile(b_hi, m).bitcast(F32), ALU.mult, ALU.subtract).then_inc(x2_lo, 1)

            with dve.Fori(0, DT // 2) as i:
                work = Work(PROJ.unit, PROJ.job, i, 2 * JU, 2)
                for j in range(2):
                    projected(i * 2 + j, work.then(j * JU, j))

            def up(m, c, work, first=False):
                for u in range(JU):
                    split_unit(work, u + LEAD)
                    if first and u == 1:
                        mean_square(5 * H, share=P / D)
                        refine(5 * H, x_sq)
                n = c * DT + m + 1
                dve.wait_ge(unit_used, work.units_done(JU))
                dve.wait_ge(rms_ready, 1)
                nc.vector.tensor_tensor(relu_in, jobs[work.bank()][:, :], spare[:, :], ALU.mult).then_inc(up_scaled, 1)
                dve.wait_ge(up_scaled, n)
                nc.vector.scalar_tensor_tensor(relu_sq, relu_in, 0.0, relu_in, ALU.max, ALU.mult).then_inc(up_squared, 1)
                dve.wait_ge(up_hi, n)
                nc.vector.tensor_tensor(tile(a_lo, m), relu_sq, tile(a_hi, m).bitcast(F32),
                                        ALU.subtract).then_inc(up_ready, 1)

            def ups(c, first_turn):
                with dve.Fori(first_turn, DT // 2) as i:
                    work = Work(MLP.unit, MLP.job, c * DT + i, 2 * JU, 2)
                    for j in range(2):
                        up(i * 2 + j, c, work.then(j * JU, j))

            def downs(c):
                with dve.Fori(0, DT // 2) as i:
                    work = Work(MLP.unit + DT * JU, MLP.job + DT, c * DT + i, 2 * JU, 2)
                    for j in range(2):
                        for u in range(JU):
                            split_unit(work.then(j * JU), u + LEAD)
                        dve.wait_ge(unit_used, work.then(j * JU).units_done(JU))
                        at_least(dve, down_added, c * DT)
                        m = i * 2 + j
                        nc.vector.tensor_tensor(tile(main, m), jobs[work.then(0, j).bank()][:, :], tile(main, m),
                                                ALU.add).then_inc(down_added, 1)

            dve.wait_ge(x2_ready, DT)
            for j in range(2):
                up(j, 0, MLP.then(j * JU, j), first=j == 0)
            ups(0, 1)
            downs(0)
            with dve.Fori(1, CH - 1) as c:
                ups(c, 0)
                downs(c)
            ups(CH - 1, 0)
            dve.wait_ge(down_added, (CH - 1) * DT)

            LAST = MLP.then((CH - 1) * CU + DT * JU, (CH - 1) * CJ + DT)

            def last_down(m, work, j):
                for u in range(JU):
                    split_unit(work, u + LEAD)
                dve.wait_ge(unit_used, work.units_done(JU))
                at_least(dve, fin_turned, m - 1)
                nc.vector.tensor_tensor(fin[j], jobs[work.bank()][:, :], tile(main, m), ALU.add).then_inc(down_added, 1)

            last_down(0, LAST, 0)
            for m in (1, 2):
                last_down(m, LAST.then(m * JU, m), m % 2)
            with dve.Fori(1, DT // 2 - 1) as i:
                work = Work(LAST.unit + JU, LAST.job + 1, i, 2 * JU, 2)
                last_down(i * 2 + 1, work, 1)
                last_down(i * 2 + 2, work.then(JU), 0)
            last_down(DT - 1, LAST.then((DT - 1) * JU, DT - 1), 1)

        @block.tensor
        def _(pe):
            def job(work, act_hi, act_lo, first_tile=0, units=JU, before_unit=None):
                result = jobs[work.bank()]
                for n in range(units):
                    if before_unit is not None:
                        before_unit(n)
                    pe.wait_ge(split_ready, work.units_done(n + 1))
                    slot = (work.unit + n) % SPLITS
                    for k in range(KU):
                        f = first_tile + n * KU + k
                        nc.tensor.matmul(result[:, :], w_hi[:, slot, k], act_hi[:, f], start=(n == 0 and k == 0),
                                         stop=False)
                        nc.tensor.matmul(result[:, :], w_hi[:, slot, k], act_lo[:, f], start=False, stop=False)
                        done = nc.tensor.matmul(result[:, :], w_lo[:, slot, k], act_hi[:, f], start=False,
                                                stop=(n == units - 1 and k == KU - 1))
                    done.then_inc(unit_used, 1)

            def mean_squares(n, squared, averages):
                at_least(pe, eps_ready, n)
                for b in range(TB):
                    last = nc.tensor.matmul(stats[:, 2 * b:2 * b + 2], squared[:, P * b:P * (b + 1)], averages,
                                            start=True, stop=True)
                last.then_inc(stat_ready, 1)

            def widen(n, repeated):
                pe.wait_ge(r_ready, n + 1)
                at_least(pe, norm_ready, n)
                for b in range(TB):
                    last = nc.tensor.matmul(wide[:, P * b:P * (b + 1)], repeated[:, P * b:P * (b + 1)], ident[:, :],
                                            start=True, stop=True)
                last.then_inc(wide_ready, 1)

            def norm_steps(n, kind, t, first):
                if t == first:
                    pe.wait_ge(sq_ready, n + 1)
                    mean_squares(n, squares, mean2[:, 2 * kind:2 * kind + 2])
                if t == first + 2:
                    widen(n, r_wide)

            def take_scores(kind, i, b):
                block_no = i * (2 * TB) + TB * kind + b
                at_least(pe, logits_ready, block_no)
                n = P * (b + 1)
                for m in range(2 - kind):
                    part = slice(64 * m, 64 * m + 64) if kind == 0 else slice(0, P)
                    last = nc.tensor.matmul(scores[m][:, 0:n], qn[kind][part, P * b:P * (b + 1)],
                                            kn[kind][part, 0:n], start=True, stop=True)
                last.then_inc(scores_ready, 1)

            def turn_probs(kind, i, b):
                block_no = i * (2 * TB) + TB * kind + b
                pe.wait_ge(probs_ready, block_no + 1)
                at_least(pe, p_keys_ready, block_no)
                pe.wait_ge(v_ready, i * 2 + kind + 1)
                for j in range(b + 1):
                    last = nc.tensor.transpose(turned[:, P * j:P * (j + 1)], probs[b % 2][:, P * j:P * (j + 1)],
                                               ident[:, :])
                last.then_inc(probs_turned, 1)

            def head_step(kind, i, t, work):
                n = i * 5 + 2 * kind
                norm_steps(n, kind, t, JU + 1)
                norm_steps(n + 1, kind, t, 2 * JU + 1)
                if kind == 1 and t == 11:
                    pe.wait_ge(f_picked, i + 1)
                    pe.wait_ge(logits_ready, i * (2 * TB) + TB)
                    nc.tensor.matmul(scores[1][:, :], ones[0:H, :], f_pick, start=True, stop=True
                                     ).then_inc(f_wide, 1)
                if t == 13:
                    pe.wait_ge(v_copied, i * 2 + kind + 1)
                    at_least(pe, p_keys_ready, i * (2 * TB) + TB * kind)
                    for b in range(TB):
                        last = nc.tensor.transpose(turned[:, P * b:P * (b + 1)], v_feat[:, P * b:P * (b + 1)],
                                                   ident[:, :])
                    last.then_inc(v_turned, 1)
                    pe.wait_ge(norm_ready, n + 2)
                for b, when in enumerate(SOFTMAX_STEPS):
                    if t == when:
                        take_scores(kind, i, b)
                for b, when in enumerate(SOFTMAX_STEPS):
                    if t == when + 2:
                        turn_probs(kind, i, b)
                if t == 22:
                    pe.wait_ge(p_keys_ready, i * (2 * TB) + TB * kind + TB)
                    if kind == 0:
                        at_least(pe, o_copied, i * 2)
                    else:
                        pe.wait_ge(sq_ready, i * 5 + 5)
                    for j in range(TB):
                        last = nc.tensor.matmul(heads_out[:, P * j:S], v_tok[kind][:, P * j:P * (j + 1)],
                                                p_keys[:, j, P * j:S], start=(j == 0), stop=(j == TB - 1))
                    last.then_inc(pv_ready, 1)
                if kind == 0:
                    norm_steps(n + 4, 1, t, HU + 1)

            pe.wait_ge(params_loaded, 16 * 14)
            pe.wait_ge(ident_ready, 1)
            nc.tensor.transpose(stats[:, 0:P], param_rows, ident[:, :]).then_inc(cols_turned, 1)
            pe.wait_ge(lam_product, 1)
            nc.tensor.matmul(stats[:, 0:2], ones[:, :], lam[:, 0:2], start=True, stop=True).then_inc(lam_sums, 1)
            pe.wait_ge(x_scaled, TB)
            for k in range(DT):
                at_least(pe, h_ready, k - 3)
                for b in range(TB):
                    last = nc.tensor.transpose(turn4[k % 4][:, P * b:P * (b + 1)], x_tok[:, b, P * k:P * (k + 1)],
                                               ident[:, :])
                last.then_inc(x_turned, 1)

            job(FORGET, a_hi, a_lo, before_unit=lambda n: pe.wait_ge(h_ready, KU * (n + 1)))

            def forget_step(u):
                if u == 0:
                    pe.wait_ge(f_copied, 1)
                    for b in range(TB):
                        last = nc.tensor.transpose(heads_out[:, P * b:P * (b + 1)], f_feat[:, P * b:P * (b + 1)],
                                                   ident[:, :])
                    last.then_inc(f_turned, 1)
                if u == 2:
                    pe.wait_ge(f_ready, 1)
                    pe.wait_ge(tri_ready, 1)
                    for b in range(TB):
                        last = nc.tensor.matmul(heads_out[0:H, P * b:S], lf[:, b], tri[:, 0:S - P * b],
                                                start=(b == 0), stop=(b == TB - 1))
                    last.then_inc(f_summed, 1)
                if u == 3:
                    pe.wait_ge(f_row_ready, 1)
                    for b in range(TB):
                        last = nc.tensor.transpose(heads_out[:, H * b:H * (b + 1)], f_row[:, P * b:P * (b + 1)],
                                                   ident[0:H, 0:H])
                    last.then_inc(f_back, 1)
                if u == 5:
                    pe.wait_ge(neg_f_ready, 1)
                    pe.wait_ge(gains_ready, 1)
                    pe.wait_ge(lam_step, 2)

            def heads_turn(i, work):
                first = isinstance(i, int) and i == 0
                for j in range(HJ):
                    if j == 0:
                        at_least(pe, sq_ready, i * 5 - 1)
                    elif j == 1:
                        pe.wait_ge(f_copied, 1) if first else pe.wait_ge(v_copied, i * 2)
                    elif j == 4:
                        pe.wait_ge(v_copied, i * 2 + 1)
                    else:
                        pe.wait_ge(sq_ready, i * 5 + {2: 1, 3: 2, 5: 3}[j])

                    def before_unit(n):
                        if first:
                            forget_step(j * JU + n)
                        head_hooks(head_step, j * JU + n, i, work)

                    job(work.then(j * JU, j), a_hi, a_lo, before_unit=before_unit)

            heads_turn(0, HEADS)
            with pe.Fori(1, H) as i:
                heads_turn(i, Work(HEADS.unit, HEADS.job, i, HU, HJ))

            def merge(m, work):
                first = isinstance(m, int) and m == 0

                def hooks(at):
                    return (lambda n: head_hooks(head_step, at + n, H, work)) if first else None

                if first:
                    pe.wait_ge(sq_ready, 5 * H - 1)
                else:
                    pe.wait_ge(parts_ready, m * 2 - 1)
                job(work, a_hi, a_lo, before_unit=hooks(0))
                if first:
                    pe.wait_ge(v_copied, 2 * H)
                else:
                    pe.wait_ge(parts_ready, m * 2)
                job(work.then(JU), a_hi, a_lo, before_unit=hooks(JU))
                pe.wait_ge(gate_exp, m * 2 + 1)
                if first:
                    pe.wait_ge(o_ready, 2 * H - 1)
                job(work.then(2 * JU, 2), b_hi, b_lo, 0, BU, before_unit=hooks(2 * JU))

                def last_hooks(n):
                    head_hooks(head_step, 2 * JU + BU + n, H, work)
                    if n == BU - 1:
                        pe.wait_ge(o_ready, 2 * H)

                pe.wait_ge(gate_exp, m * 2 + 2)
                job(work.then(2 * JU + BU, 3), b_hi, b_lo, H, BU, before_unit=last_hooks if first else None)

            merge(0, MERGE)
            with pe.Fori(0, DT // 2 - 1) as i:
                work = Work(MERGE.unit + MU, MERGE.job + MJ, i, 2 * MU, 2 * MJ)
                merge(i * 2 + 1, work)
                merge(i * 2 + 2, work.then(MU, MJ))
            merge(DT - 1, MERGE.then((DT - 1) * MU, (DT - 1) * MJ))

            def projected(m, j, work):
                first = isinstance(m, int) and m == 0

                def before_unit(n):
                    if first:
                        pe.wait_ge(m_ready, KU * (n + 1))
                    if n == 2:
                        if isinstance(m, int):
                            pe.wait_ge(xr_loaded[j], 16)
                        else:
                            pe.wait_ge(xr_loaded[j], m * 8 + (16 - 8 * j))
                        at_least(pe, xr_ready, m)
                        for b in range(TB):
                            last = nc.tensor.transpose(turned[:, P * b:P * (b + 1)],
                                                       x_slot[j][:, P * b:P * (b + 1)], ident[:, :])
                        last.then_inc(xr_turned, 1)

                if isinstance(m, int):
                    pe.wait_ge(parts_ready, 2 * DT - 1 + m)
                else:
                    pe.wait_ge(x2_ready, m - 1)
                job(work, a_hi, a_lo, before_unit=before_unit)

            for j in range(2):
                projected(j, j, PROJ.then(j * JU, j))
            with pe.Fori(1, DT // 2) as i:
                work = Work(PROJ.unit, PROJ.job, i, 2 * JU, 2)
                for j in range(2):
                    projected(i * 2 + j, j, work.then(j * JU, j))

            def ups(c, bank_taken):
                def turn(i, work):
                    for j in range(2):
                        m = i * 2 + j
                        first = isinstance(c, int) and isinstance(i, int) and c == 0 and j == 0
                        if isinstance(i, int):
                            pe.wait_ge(bank_taken, c * DT + (j - 1) if bank_taken is down_added else DT - 1 + j)
                        else:
                            pe.wait_ge(up_scaled, c * DT + m - 1)

                        def before_unit(n):
                            if isinstance(c, int) and c == 0 and isinstance(i, int):
                                pe.wait_ge(x2_lo, min(DT, KU * (n + 1)))
                            if first and n == 1:
                                pe.wait_ge(sum_ready, DT + 1)
                                mean_squares(5 * H, spare, mean2[:, 2:4])
                            if first and n == 3:
                                widen(5 * H, x_sq)

                        job(work.then(j * JU, j), b_hi, b_lo, before_unit=before_unit)

                turn(0, Work(MLP.unit, MLP.job, c * DT, 2 * JU, 2))
                with pe.Fori(1, DT // 2) as i:
                    turn(i, Work(MLP.unit, MLP.job, c * DT + i, 2 * JU, 2))

            def downs(c):
                def turn(i, work):
                    for j in range(2):
                        m = i * 2 + j
                        if isinstance(i, int):
                            pe.wait_ge(up_scaled, c * DT + DT - 1 + j)
                        else:
                            pe.wait_ge(down_added, c * DT + m - 1)

                        def before_unit(n):
                            if isinstance(i, int) and j == 0:
                                pe.wait_ge(up_ready, c * DT + KU * (n + 1))

                        job(work.then(j * JU, j), a_hi, a_lo, before_unit=before_unit)

                turn(0, Work(MLP.unit + DT * JU, MLP.job + DT, c * DT, 2 * JU, 2))
                with pe.Fori(1, DT // 2) as i:
                    turn(i, Work(MLP.unit + DT * JU, MLP.job + DT, c * DT + i, 2 * JU, 2))

            ups(0, x2_ready)
            downs(0)
            with pe.Fori(1, CH - 1) as c:
                ups(c, down_added)
                downs(c)
            ups(CH - 1, down_added)

            LAST = MLP.then((CH - 1) * CU + DT * JU, (CH - 1) * CJ + DT)
            done_before = (CH - 1) * DT

            def turn_output(m, j):
                pe.wait_ge(down_added, m + (done_before + 1))
                at_least(pe, stage_ready, m - 1)
                for b in range(TB):
                    last = nc.tensor.transpose((turned, wide)[j][:, P * b:P * (b + 1)], fin[j][:, P * b:P * (b + 1)],
                                               ident[:, :])
                last.then_inc(fin_turned, 1)

            def last_down(m, work, j):
                static = isinstance(m, int)
                if static and m <= 1:
                    pe.wait_ge(up_scaled, CH * DT - 1 + m)
                else:
                    pe.wait_ge(down_added, m + (done_before - 1))

                def before_unit(n):
                    if static and m == 0:
                        pe.wait_ge(up_ready, done_before + KU * (n + 1))
                    if n == 1 and not (static and m == 0):
                        turn_output(m - 1, 1 - j)

                job(work, a_hi, a_lo, before_unit=before_unit)

            last_down(0, LAST, 0)
            for m in (1, 2):
                last_down(m, LAST.then(m * JU, m), m % 2)
            with pe.Fori(1, DT // 2 - 1) as i:
                work = Work(LAST.unit + JU, LAST.job + 1, i, 2 * JU, 2)
                last_down(i * 2 + 1, work, 1)
                last_down(i * 2 + 2, work.then(JU), 0)
            last_down(DT - 1, LAST.then((DT - 1) * JU, DT - 1), 1)
            turn_output(DT - 1, 1)


INPUTS = ["x", "norm_mix", "w_in", "b_forget", "qnorm_diff", "knorm_diff", "lambda_q1", "lambda_k1", "lambda_q2",
          "lambda_k2", "subln_diff", "qnorm_fox", "knorm_fox", "w_branch_diff", "w_branch_fox", "w_gate", "b_gate",
          "w_out", "norm_mlp", "w_mlp_up", "w_mlp_down"]


def kernel(**inputs):
    import numpy as np
    import concourse.bacc as bacc
    from concourse.bass_utils import run_bass_kernel_spmd

    nc = bacc.Bacc("TRN2", target_bir_lowering=False, num_devices=1)
    arrays, args = {}, []
    for name in INPUTS:
        a = np.ascontiguousarray(inputs[name])
        arrays[f"in_{name}"] = a
        args.append(nc.dram_tensor(f"in_{name}", a.shape, mybir.dt.from_np(a.dtype), kind="ExternalInput").ap())
    shape = arrays["in_x"].shape
    args.append(nc.dram_tensor("out", shape, F32, kind="ExternalOutput").ap())
    build(nc, *args)
    result = run_bass_kernel_spmd(nc, [arrays], core_ids=[0])
    return result.results[0]["out"]
```

```python
import math
from contextlib import ExitStack

import concourse.bass as bass
from concourse import mybir

F32 = mybir.dt.float32
F32R = mybir.dt.float32r
I32 = mybir.dt.int32
ACT = mybir.ActivationFunctionType
ALU = mybir.AluOpType

P = 128
KU = 4
SPLITS = 4
RAWS = 4
LEAD = 3
EPS = 1e-6
RSQRT_MAGIC = 0x5F3759DF
RSQRT_STEPS = 12
SOFTMAX_STEPS = (14, 15, 17, 19)
TURN_STEPS = ((16, 17, 19, 22), (16, 17, 19, 21))
PV_STEPS = (23, 22)
NORM_STEPS = (4, 8, 24)
NORM_LENGTH = 4
MASKED = 1e30
LAMBDA_INIT = 0.8 - 0.6 * math.exp(-0.3 * 0)


def at_least(eng, sem, value):
    if not (isinstance(value, int) and value <= 0):
        eng.wait_ge(sem, value)


class Work:

    def __init__(self, unit, job, loop=0, units_per_turn=0, jobs_per_turn=0):
        assert units_per_turn % (2 * RAWS) == 0 and jobs_per_turn % 2 == 0
        self.unit, self.job = unit, job
        self.loop, self.upt, self.jpt = loop, units_per_turn, jobs_per_turn

    def then(self, units, jobs=1):
        return Work(self.unit + units, self.job + jobs, self.loop, self.upt, self.jpt)

    def units_done(self, n):
        return self.unit + n + self.loop * self.upt if self.upt else self.unit + n

    def loads(self, n):
        half = (self.unit + n) // 2
        v = 16 * (half // RAWS + 1)
        return v + self.loop * (16 * self.upt // 2 // RAWS) if self.upt else v

    def bank(self):
        return self.job % 2


def tile(tensor, m):
    return tensor[:, m] if isinstance(m, int) else tensor[:, bass.ds(m, 1)].rearrange("p a s -> p (a s)")


def build(nc, x, norm_mix, w_in, b_forget, qnorm_diff, knorm_diff, lambda_q1, lambda_k1, lambda_q2,
          lambda_k2, subln_diff, qnorm_fox, knorm_fox, w_branch_diff, w_branch_fox, w_gate, b_gate,
          w_out, norm_mlp, w_mlp_up, w_mlp_down, out):
    _, S, D = x.shape
    assert x.shape[0] == 1 and w_in.shape[0] == 1 and S == 512
    DT = D // P
    TB = S // P
    HD = qnorm_fox.shape[1]
    WD, WF = w_branch_diff.shape[1], w_branch_fox.shape[1]
    H = WD // P
    NF = b_forget.shape[1]
    FF = w_mlp_up.shape[2]
    CH = FF // D
    JU = DT // KU
    BU = H // KU
    assert HD == P and WF == WD and NF == H == 8 and DT == 16 and CH * D == FF

    FORGET = Work(0, 0)
    HEADS = FORGET.then(JU)
    HU, HJ = 6 * JU, 6
    MERGE = HEADS.then(H * HU, H * HJ)
    MU, MJ = 2 * JU + 2 * BU, 4
    PROJ = MERGE.then(DT * MU, DT * MJ)
    MLP = PROJ.then(DT * JU, DT)
    CU, CJ = 2 * DT * JU, 2 * DT
    ALL_UNITS = MLP.unit + CH * CU

    xt = x[0].rearrange("(b p) d -> p b d", p=P)
    outt = out[0].rearrange("(b p) d -> p b d", p=P)

    with ExitStack() as ctx:
        def sb(name, shape, dt=F32):
            return ctx.enter_context(nc.sbuf_tensor(name, shape, dt))

        def sem(name):
            return ctx.enter_context(nc.semaphore(name))

        a_hi, a_lo = sb("a_hi", [P, DT, S], F32R), sb("a_lo", [P, DT, S], F32R)
        b_hi, b_lo = sb("b_hi", [P, DT, S], F32R), sb("b_lo", [P, DT, S], F32R)
        main = sb("main", [P, DT, S])
        side = sb("side", [P, 4, S])
        raw = sb("raw", [P, RAWS, 2 * KU, P])
        w_hi, w_lo = sb("w_hi", [P, SPLITS, KU, P], F32R), sb("w_lo", [P, SPLITS, KU, P], F32R)
        spare = sb("spare", [P, S])
        f_row = sb("f_row", [H, S])
        ident = sb("ident", [P, P])
        ones = sb("ones", [P, P])
        causal = sb("causal", [P, P])
        cols = sb("cols", [P, P])
        neg_bgate = sb("neg_bgate", [P, 2 * DT])
        gains = sb("gains", [P, 8])
        mean2 = sb("mean2", [P, 4])
        stat, x_stat = sb("stat", [P, 6, 8]), sb("x_stat", [P, 6, TB])
        x_sums, x_r, x_r2 = sb("x_sums", [P, 2 * TB]), sb("x_r", [P, 2 * TB]), sb("x_r2", [P, 2 * TB])
        x_r1 = x_r[:, :].rearrange("p (b e) -> p b e", e=2)[:, :, 0:1]
        bforget = sb("bforget", [P, NF])
        lf = sb("lf", [P, TB, NF])
        lf_t = sb("lf_t", [P, 3, TB, NF])
        neg_f = sb("neg_f", [P, TB, H])
        lam = sb("lam", [P, 6])
        pause = sb("pause", [P, 1])
        one_half = sb("one_half", [P, 1])
        row_min, row_sum, row_inv = sb("row_min", [P, 2]), sb("row_sum", [P, 2]), sb("row_inv", [P, 2])

        x_tok = main[:, :, :].rearrange("p (b f) s -> p b (f s)", b=TB)
        qn, kn = [main[:, 0], main[:, 2]], [main[:, 1], main[:, 3]]
        v_tok = [main[:, 4], main[:, 5]]
        v_feat, squares, scaled = main[:, 6], main[:, 7], main[:, 8]
        r_wide = squares
        p_keys = main[:, 9:13]
        bias_fox = main[:, 13:16].rearrange("p a s -> p (a s)")
        f_pick = bias_fox[0:H, 0:S]
        bias_at = [P * b * (b + 1) // 2 for b in range(TB + 1)]
        logits = [side[:, 0], side[:, 1]]
        probs = [side[:, 2], side[:, 3]]
        x_slot, x_feat, x_sq = [side[:, 1], side[:, 0]], side[:, 2], side[:, 3]
        fin, stage = [side[:, 0], side[:, 1]], [side[:, 2], side[:, 3]]
        gate_d, gate_f, part_d, part_f = (side[:, j] for j in (1, 2, 3, 0))
        relu_in, relu_sq = side[:, 0], side[:, 1]
        param_rows, f_feat, tri = side[:, 0, 0:P], side[:, 1], side[:, 2]
        q_gain = [gains[:, 0:1], gains[:, 1:2]]
        k_gain = [cols[:, 68:69], cols[:, 66:67]]
        o_gain = gains[:, 2:3]
        lam_col = lam[:, 4:5]

        jobs = [ctx.enter_context(nc.psum_tensor(f"job{i}", [P, S], F32)) for i in range(2)]
        scores = [ctx.enter_context(nc.psum_tensor(f"scores{i}", [P, S], F32)) for i in range(2)]
        turned = ctx.enter_context(nc.psum_tensor("turned", [P, S], F32))
        wide = ctx.enter_context(nc.psum_tensor("wide", [P, S], F32))
        stats = ctx.enter_context(nc.psum_tensor("stats", [P, S], F32))
        heads_out = ctx.enter_context(nc.psum_tensor("heads_out", [P, S], F32))
        turn_banks = [scores[0], scores[1], turned, wide, heads_out, jobs[1]]
        TURNS = len(turn_banks)

        raw_loaded = [sem(f"raw_loaded{i}") for i in range(RAWS)]
        x_loaded = [sem(f"x_loaded{i}") for i in range(JU)]
        (rows_cleared, params_loaded, small_loaded, small_turned, small_ready, bforget_loaded, ident_ready, consts_ready, tri_ready,
         table_loaded, cols_turned, cols_ready, gains_ready, lam_product, lam_sums, lam_exps, lam_step,
         x_summed, x_eps, x_newton, x_r_ready, x_turned, h_hi, h_ready,
         hi_ready, split_ready, unit_used) = (sem(n) for n in (
             "rows_cleared", "params_loaded", "small_loaded", "small_turned", "small_ready", "bforget_loaded", "ident_ready", "consts_ready",
             "tri_ready", "table_loaded", "cols_turned", "cols_ready", "gains_ready", "lam_product", "lam_sums",
             "lam_exps", "lam_step", "x_summed", "x_eps", "x_newton", "x_r_ready",
             "x_turned", "h_hi", "h_ready", "hi_ready", "split_ready", "unit_used"))
        (f_copied, f_turned, f_logit, f_neg, f_exp, f_one, f_ln, f_ready, f_summed, f_row_ready,
         f_back, neg_f_ready) = (sem(n) for n in (
             "f_copied", "f_turned", "f_logit", "f_neg", "f_exp", "f_one", "f_ln", "f_ready", "f_summed",
             "f_row_ready", "f_back", "neg_f_ready"))
        (sq_ready, taken, stat_ready, with_r, eps_ready, newton, r_ready, wide_ready, norm_ready) = (sem(n) for n in (
             "sq_ready", "taken", "stat_ready", "with_r", "eps_ready", "newton", "r_ready", "wide_ready", "norm_ready"))
        (scores_ready, logits_ready, exp_ready, inv_ready, second_scaled, probs_ready,
         probs_turned, p_keys_ready) = (sem(n) for n in (
             "scores_ready", "logits_ready", "exp_ready", "inv_ready", "second_scaled",
             "probs_ready", "probs_turned", "p_keys_ready"))
        (v_copied, v_turned, v_ready, pv_ready, o_copied, o_hi, o_ready, f_picked, f_wide,
         bias_open, bias_ready, dist_ready) = (sem(n) for n in (
             "v_copied", "v_turned", "v_ready", "pv_ready", "o_copied", "o_hi", "o_ready",
             "f_picked", "f_wide", "bias_open", "bias_ready", "dist_ready"))
        (r_repeated, r_row_wide, r_row_ready, gate_scaled, gate_exp, gate_one, gate_ready, parts_ready, merged_ready, m_hi, m_ready, m_ready_too, sum_cleared) = (
            sem(n) for n in ("r_repeated", "r_row_wide", "r_row_ready", "gate_scaled", "gate_exp", "gate_one", "gate_ready", "parts_ready", "merged_ready",
                             "m_hi", "m_ready", "m_ready_too", "sum_cleared"))
        xr_loaded = [sem(f"xr_loaded{i}") for i in range(2)]
        (xr_turned, xr_ready, x2_ready, x2_sq, x2_hi, x2_lo, sum_ready,
         rms_ready) = (sem(n) for n in (
             "xr_turned", "xr_ready", "x2_ready", "x2_sq", "x2_hi", "x2_lo",
             "sum_ready", "rms_ready"))
        (up_scaled, up_squared, up_hi, up_ready, down_added, fin_ready, fin_turned,
         stage_ready) = (sem(n) for n in (
             "up_scaled", "up_squared", "up_hi", "up_ready", "down_added", "fin_ready",
             "fin_turned", "stage_ready"))
        out_stored = [sem(f"out_stored{i}") for i in range(2)]


        def head_hooks(step, u, i, work):
            half = HU // 2
            if not (isinstance(i, int) and i == 0):
                before = work.then(-HU, -HJ)
                step(0, i - 1, u + HU, before)
                step(1, i - 1, u + half, before.then(half, HJ // 2))
            if not (isinstance(i, int) and i == H):
                step(0, i, u, work)
                step(1, i, u - half, work.then(half, HJ // 2))

        block = ctx.enter_context(nc.Block())

        @block.sync
        def _(sp):
            def load_half(work, half, source):
                slot = (work.unit // 2 + half) % RAWS
                at_least(sp, split_ready, work.units_done(2 * half) - 2 * RAWS + 2)
                sp.dma_start(raw[:, slot], source).then_inc(raw_loaded[slot], 16)

            def load_job(work, weights, col, halves=2):
                w = weights[0].rearrange("(k p) c -> p k c", p=P)
                for half in range(halves):
                    k = 2 * KU * half
                    load_half(work, half, w[:, k:k + 2 * KU, bass.ds(col, P)])

            sp.wait_ge(rows_cleared, 1)
            w = w_in[0].rearrange("(k p) c -> p k c", p=P)
            for quarter in range(JU):
                features = slice(KU * P * quarter, KU * P * (quarter + 1))
                for b in range(TB):
                    sp.dma_start(x_tok[:, b, features], xt[:, b, features]).then_inc(x_loaded[quarter], 16)
                if quarter % 2 == 0:
                    k = KU * quarter
                    load_half(FORGET, quarter // 2, w[:, k:k + 2 * KU, w_in.shape[2] - P:])

            def head_loads(work, i, first_job=0):
                for j in range(first_job, HJ):
                    load_job(work.then(j * JU, j), w_in, i * P + j * WD)

            load_job(HEADS, w_in, 0)
            for r, c, vector in ((64, 0, subln_diff), (65, 0, qnorm_fox), (66, 0, knorm_fox),
                                 (67, 0, qnorm_diff), (67, 64, qnorm_diff), (68, 0, knorm_diff),
                                 (68, 64, knorm_diff), (69, 0, lambda_q1), (69, 64, lambda_q2),
                                 (70, 0, lambda_k1), (70, 64, lambda_k2)):
                sp.dma_start(side[r:r + 1, 0, c:c + vector.shape[1]], vector).then_inc(small_loaded, 16)
            sp.dma_start(bforget[:, :], b_forget[0:1, :].broadcast_to([P, NF])).then_inc(bforget_loaded, 16)
            head_loads(HEADS, 0, first_job=1)
            with sp.Fori(1, H) as i:
                head_loads(Work(HEADS.unit, HEADS.job, i, HU, HJ), i)

            def merge_loads(work, m):
                load_job(work, w_gate, m * P)
                load_job(work.then(JU), w_gate, m * P + D)
                load_job(work.then(2 * JU, 2), w_branch_diff, m * P, halves=1)
                load_job(work.then(2 * JU + BU, 3), w_branch_fox, m * P, halves=1)

            with sp.Fori(0, DT // 2) as i:
                work = Work(MERGE.unit, MERGE.job, i, 2 * MU, 2 * MJ)
                for j in range(2):
                    merge_loads(work.then(j * MU, j * MJ), i * 2 + j)

            def load_residual(j, m):
                at_least(sp, xr_turned, m - 1)
                sp.dma_start(x_slot[j].rearrange("p (b f) -> p b f", b=TB),
                             xt[:, :, bass.ds(m * P, P)]).then_inc(xr_loaded[j], 16)

            load_job(PROJ, w_out, 0)
            load_job(PROJ.then(JU), w_out, P)
            sp.wait_ge(parts_ready, 2 * DT - 1)
            load_residual(0, 0)
            sp.wait_ge(merged_ready, DT)
            load_residual(1, 1)
            with sp.Fori(1, DT // 2) as i:
                work = Work(PROJ.unit, PROJ.job, i, 2 * JU, 2)
                for j in range(2):
                    load_job(work.then(j * JU), w_out, i * (2 * P) + j * P)
                    load_residual(j, i * 2 + j)

            with sp.Fori(0, CH) as c:
                with sp.Fori(0, DT // 2) as i:
                    work = Work(MLP.unit, MLP.job, c * DT + i, 2 * JU, 2)
                    for j in range(2):
                        load_job(work.then(j * JU), w_mlp_up, c * D + i * (2 * P) + j * P)
                with sp.Fori(0, DT // 2) as i:
                    work = Work(MLP.unit + DT * JU, MLP.job + DT, c * DT + i, 2 * JU, 2)
                    for j in range(2):
                        for half in range(2):
                            src = w_mlp_down[0, bass.ds(c * D + half * 2 * KU * P, 2 * KU * P),
                                             bass.ds(i * (2 * P) + j * P, P)]
                            load_half(work.then(j * JU), half, src.rearrange("(k p) c -> p k c", p=P))

        @block.gpsimd
        def _(pool):
            pool.memset(param_rows, 0.0).then_inc(rows_cleared, 1)
            pool.memset(ident[:, :], 0.0).then_inc(consts_ready, 1)
            pool.memset(ones[:, :], 1.0).then_inc(consts_ready, 1)
            pool.memset(causal[:, :], 0.0).then_inc(consts_ready, 1)
            pool.memset(mean2[:, 0:2], 1.0 / 64).then_inc(consts_ready, 1)
            pool.memset(mean2[:, 2:4], 1.0 / 128).then_inc(consts_ready, 1)
            pool.memset(tri, 1.0).then_inc(consts_ready, 1)
            pool.memset(one_half[:, :], 0.5).then_inc(consts_ready, 1)
            pool.wait_ge(consts_ready, 7)
            pool.affine_select(out=ident[:, :], in_=ident[:, :], compare_op=ALU.not_equal, fill=1.0,
                               base=0, pattern=[[-1, P]], channel_multiplier=1).then_inc(ident_ready, 1)
            pool.affine_select(out=mean2[:, 0:1], in_=mean2[:, 0:1], compare_op=ALU.is_ge, fill=0.0,
                               base=63, pattern=[[0, 1]], channel_multiplier=-1).then_inc(consts_ready, 1)
            pool.affine_select(out=mean2[:, 1:2], in_=mean2[:, 1:2], compare_op=ALU.is_ge, fill=0.0,
                               base=-64, pattern=[[0, 1]], channel_multiplier=1).then_inc(consts_ready, 1)
            pool.affine_select(out=causal[:, :], in_=causal[:, :], compare_op=ALU.is_ge, fill=MASKED,
                               base=0, pattern=[[-1, P]], channel_multiplier=1).then_inc(consts_ready, 1)
            pool.affine_select(out=tri, in_=tri, compare_op=ALU.is_ge, fill=0.0,
                               base=0, pattern=[[1, S]], channel_multiplier=-1).then_inc(tri_ready, 1)
            pool.iota(spare[:, :], [[-1, S]], base=S - P, channel_multiplier=1,
                      allow_small_or_imprecise_dtypes=True).then_inc(dist_ready, 1)
            pool.wait_ge(dist_ready, 1)
            pool.tensor_scalar(side[:, 3], spare[:, :], 0.0, 1.0, ALU.max, ALU.mult).then_inc(dist_ready, 1)
            pool.tensor_scalar(spare[:, :], spare[:, :], -0.5, 0.0, ALU.mult, ALU.add).then_inc(dist_ready, 1)
            pool.wait_ge(dist_ready, 3)
            pool.tensor_tensor(spare[:, :], spare[:, :], side[:, 3], ALU.add).then_inc(dist_ready, 1)
            pool.wait_ge(dist_ready, 4)
            pool.memset(spare[0:64, S - 64:S], MASKED * 2 ** H).then_inc(dist_ready, 1)
            with pool.Fori(0, H) as i:
                pool.wait_ge(logits_ready, i * (2 * TB) + TB)
                pool.wait_ge(dist_ready, i + 5)
                pool.wait_ge(consts_ready, 10)
                pool.tensor_tensor(spare[:, :], spare[:, :], one_half[:, :].broadcast_to([P, S]),
                                   ALU.mult).then_inc(dist_ready, 1)
                pool.wait_ge(bias_open, i * TB + TB)
                for b in range(TB):
                    diagonal = bias_fox[:, bias_at[b + 1] - P:bias_at[b + 1]]
                    pool.tensor_tensor(diagonal, diagonal, causal[:, :], ALU.add).then_inc(bias_ready, 1)
            pool.wait_ge(gate_scaled, 2 * DT)
            pool.memset(spare[:, :], 0.0).then_inc(sum_cleared, 1)
            for k in range(KU - 1, DT, KU):
                pool.wait_ge(m_hi, k + 1)
                pool.tensor_tensor(a_lo[:, k], main[:, k], a_hi[:, k].bitcast(F32),
                                   ALU.subtract).then_inc(m_ready_too, 1)

        @block.scalar
        def _(act):
            def round_unit(work, n):
                u = work.unit + n
                if not work.upt and u >= ALL_UNITS:
                    return
                slot, part = u // 2 % RAWS, KU * (u % 2)
                act.wait_ge(raw_loaded[slot], work.loads(n))
                at_least(act, unit_used, work.units_done(n + 1) - SPLITS)
                nc.scalar.activation(w_hi[:, u % SPLITS], raw[:, slot, part:part + KU],
                                     ACT.Copy).then_inc(hi_ready, 1)

            def take_for_norm(n, source, gain):
                at_least(act, norm_ready, n)
                nc.scalar.activation(squares, source[:, :], ACT.Square).then_inc(sq_ready, 1)
                nc.scalar.activation(scaled, source[:, :], ACT.Copy, scale=gain).then_inc(taken, 1)

            def head_step(kind, i, t, work):
                if t == 3 * JU:
                    values = work.then(2 * JU, 2)
                    act.wait_ge(unit_used, values.units_done(JU))
                    at_least(act, v_turned, i * 2 + kind)
                    if kind == 0:
                        at_least(act, o_ready, i * 2 - 1)
                    nc.scalar.activation(v_feat, jobs[values.bank()][:, :], ACT.Copy).then_inc(v_copied, 1)
                if t == 11 and kind == 1:
                    act.wait_ge(f_wide, i + 1)
                    for b in range(TB):
                        nc.scalar.activation(bias_fox[:, bias_at[b]:bias_at[b + 1]], scores[1][:, 0:P * (b + 1)],
                                             ACT.Identity, bias=neg_f[:, b, bass.ds(i, 1)]).then_inc(bias_open, 1)
                for b, when in enumerate(SOFTMAX_STEPS):
                    if t == when:
                        block_no = i * (2 * TB) + TB * kind + b
                        act.wait_ge(logits_ready, block_no + 1)
                        for m in range(2 - kind):
                            e = nc.scalar.activation(logits[m][:, 0:P * (b + 1)], logits[m][:, 0:P * (b + 1)],
                                                     ACT.Exp, scale=-1.0, bias=row_min[:, m:m + 1],
                                                     accum_out=row_sum[:, m:m + 1])
                        e.then_inc(exp_ready, 1)
                if kind == 1 and t == 22:
                    act.wait_ge(pv_ready, i * 2 + 2)
                    nc.scalar.activation(logits[0], heads_out[:, :], ACT.Copy).then_inc(o_copied, 1)
                    act.wait_ge(o_copied, i + 1)
                    nc.scalar.activation(tile(b_hi, i + H), logits[0], ACT.Copy).then_inc(o_hi, 1)

            def norm_step(kind, i, t, work):
                n = i * 5 + 2 * kind
                for which, gain in enumerate((q_gain[kind], k_gain[kind])):
                    if t == NORM_STEPS[which]:
                        act.wait_ge(unit_used, work.units_done((which + 1) * JU))
                        take_for_norm(n + which, jobs[work.then(0, which).bank()], gain)
                if kind == 0 and t == NORM_STEPS[2]:
                    act.wait_ge(pv_ready, i * 2 + 1)
                    take_for_norm(n + 4, heads_out, o_gain)
                if kind == 0 and t == NORM_STEPS[2] + NORM_LENGTH:
                    act.wait_ge(norm_ready, n + 5)
                    nc.scalar.activation(tile(b_hi, i), v_feat, ACT.Copy).then_inc(o_hi, 1)

            act.wait_ge(rows_cleared, 1)
            for r, (vector, n) in enumerate(((norm_mix, DT), (norm_mlp, DT), (b_gate, 2 * DT))):
                r = (0, DT, 2 * DT)[r]
                act.dma_start(side[r:r + n, 0, 0:P], vector.rearrange("a (r p) -> (a r) p", p=P)
                              ).then_inc(params_loaded, 16)

            def sum_x(b, e):
                act.wait_ge(x_loaded[2 * e], 16 * TB)
                act.wait_ge(x_loaded[2 * e + 1], 16 * TB)
                nc.scalar.activation(b_hi[:, 4 * b + 2 * e:4 * b + 2 * e + 2].rearrange("p a s -> p (a s)"),
                                     x_tok[:, b, D // 2 * e:D // 2 * (e + 1)], ACT.Square,
                                     accum_out=x_sums[:, 2 * b + e:2 * b + e + 1]).then_inc(x_summed, 1)

            def round_h(tiles):
                for k in tiles:
                    act.wait_ge(x_turned, k + 1)
                    nc.scalar.activation(a_hi[:, k], turn_banks[k % TURNS][:, :], ACT.Copy,
                                         scale=cols[:, k:k + 1]).then_inc(h_hi, 1)

            act.wait_ge(consts_ready, 2)
            nc.scalar.activation(x_sums[:, 0:1], ones[:, 0:1], ACT.Square).then_inc(table_loaded, 1)
            act.wait_ge(table_loaded, 1)
            act.wait_ge(cols_ready, 1)
            round_h(range(0, KU))
            round_unit(FORGET, 0)
            round_unit(FORGET, 1)
            sum_x(0, 0)
            round_h(range(KU, 2 * KU))
            sum_x(1, 0)
            round_h(range(2 * KU, 3 * KU))
            round_unit(FORGET, 2)
            round_unit(FORGET, 3)
            sum_x(2, 0)
            round_h(range(3 * KU, DT))
            for n in range(JU, JU + LEAD):
                round_unit(FORGET, n)
            sum_x(3, 0)
            for b in range(TB):
                sum_x(b, 1)
            act.wait_ge(unit_used, FORGET.units_done(JU))
            nc.scalar.activation(f_feat, jobs[FORGET.bank()][:, :], ACT.Copy).then_inc(f_copied, 1)

            def heads_turn(i, work):
                for u in range(HU):
                    round_unit(work, u + LEAD)
                    if isinstance(i, int) and i == 0 and u == 1:
                        act.wait_ge(lam_sums, 1)
                        nc.scalar.activation(lam[:, 2:4], stats[:, 0:2], ACT.Exp, scale=64.0).then_inc(lam_exps, 1)
                        act.wait_ge(f_neg, 1)
                        nc.scalar.activation(lf_t[:, 2], lf_t[:, 1], ACT.Exp).then_inc(f_exp, 1)
                        act.wait_ge(f_one, 1)
                        nc.scalar.activation(lf_t[:, 1], lf_t[:, 2], ACT.Ln).then_inc(f_ln, 1)
                    head_hooks(norm_step, u, i, work)
                    head_hooks(head_step, u, i, work)

            heads_turn(0, HEADS)
            with act.Fori(1, H) as i:
                heads_turn(i, Work(HEADS.unit, HEADS.job, i, HU, HJ))

            def merge(m, work, last=False):
                for u in range(MU):
                    round_unit(work, u + LEAD)
                    if isinstance(m, int) and m == 0:
                        head_hooks(norm_step, u, H, work)
                        head_hooks(head_step, u, H, work)
                    if isinstance(m, int) and m == 0 and u == 3:
                        act.wait_ge(r_row_wide, 1)
                        act.wait_ge(dist_ready, 5 + H)
                        nc.scalar.activation(spare[:, :], heads_out[:, :], ACT.Copy).then_inc(r_row_ready, 1)
                    for g, gate in enumerate((gate_d, gate_f)):
                        if u == (g + 1) * JU:
                            act.wait_ge(gate_scaled, m * 2 + g + 1)
                            nc.scalar.activation(gate, gate, ACT.Exp, scale=-1.0,
                                                 bias=neg_bgate[:, bass.ds(m + g * DT, 1)]).then_inc(gate_exp, 1)
                    if last and u >= 2 * JU:
                        for k in range((u - 2 * JU) * 3, (u - 2 * JU) * 3 + 3):
                            round_merged(k)

            def round_merged(k):
                act.wait_ge(unit_used, MERGE.unit + (DT - 1) * MU + 2 * JU)
                act.wait_ge(merged_ready, k + 1)
                nc.scalar.activation(a_hi[:, k], main[:, k], ACT.Copy).then_inc(m_hi, 1)

            merge(0, MERGE)
            with act.Fori(0, DT // 2 - 1) as i:
                work = Work(MERGE.unit + MU, MERGE.job + MJ, i, 2 * MU, 2 * MJ)
                merge(i * 2 + 1, work)
                merge(i * 2 + 2, work.then(MU, MJ))
            merge(DT - 1, MERGE.then((DT - 1) * MU, (DT - 1) * MJ), last=True)
            for k in range(2 * BU * 3, DT):
                round_merged(k)

            def projected(m, work):
                for u in range(JU):
                    round_unit(work, u + LEAD)
                    if u == 2:
                        act.wait_ge(xr_turned, m + 1)
                        at_least(act, sum_ready, m)
                        nc.scalar.activation(x_feat, turned[:, :], ACT.Copy).then_inc(xr_ready, 1)
                act.wait_ge(x2_ready, m + 1)
                at_least(act, sum_ready, m)
                nc.scalar.activation(x_sq, tile(main, m), ACT.Square).then_inc(x2_sq, 1)
                nc.scalar.activation(tile(b_hi, m), tile(main, m), ACT.Copy,
                                     scale=cols[:, bass.ds(m + DT, 1)]).then_inc(x2_hi, 1)

            for j in range(2):
                projected(j, PROJ.then(j * JU, j))
            with act.Fori(1, DT // 2) as i:
                work = Work(PROJ.unit, PROJ.job, i, 2 * JU, 2)
                for j in range(2):
                    projected(i * 2 + j, work.then(j * JU, j))

            def up(m, c, work, first=False):
                for u in range(JU):
                    round_unit(work, u + LEAD)
                if first:
                    act.wait_ge(wide_ready, 5 * H + 1)
                    nc.scalar.activation(spare[:, :], wide[:, :], ACT.Copy).then_inc(rms_ready, 1)
                act.wait_ge(up_squared, c * DT + m + 1)
                nc.scalar.activation(tile(a_hi, m), relu_sq, ACT.Copy).then_inc(up_hi, 1)

            def ups(c, first_turn):
                with act.Fori(first_turn, DT // 2) as i:
                    work = Work(MLP.unit, MLP.job, c * DT + i, 2 * JU, 2)
                    for j in range(2):
                        up(i * 2 + j, c, work.then(j * JU, j))

            def down_rounds(c):
                with act.Fori(0, DT // 2) as i:
                    work = Work(MLP.unit + DT * JU, MLP.job + DT, c * DT + i, 2 * JU, 2)
                    for u in range(2 * JU):
                        round_unit(work, u + LEAD)

            for j in range(2):
                up(j, 0, MLP.then(j * JU, j), first=j == 0)
            ups(0, 1)
            down_rounds(0)
            with act.Fori(1, CH - 1) as c:
                ups(c, 0)
                down_rounds(c)
            ups(CH - 1, 0)

            def store(j, m):
                act.wait_ge(fin_turned, m + 1)
                if j == 0:
                    at_least(act, out_stored[0], m * 8)
                else:
                    at_least(act, out_stored[1], m * 8 - 8)
                nc.scalar.activation(stage[j], (turned, wide)[j][:, :], ACT.Copy).then_inc(stage_ready, 1)
                act.wait_ge(stage_ready, m + 1)
                act.dma_start(outt[:, :, bass.ds(m * P, P)], stage[j].rearrange("p (b f) -> p b f", b=TB)
                              ).then_inc(out_stored[j], 16)

            LAST = MLP.then((CH - 1) * CU + DT * JU, (CH - 1) * CJ + DT)

            def last_down(m, work, j):
                for u in range(JU):
                    round_unit(work, u + LEAD)
                    if u == 2 and not (isinstance(m, int) and m == 0):
                        store(1 - j, m - 1)

            last_down(0, LAST, 0)
            for m in (1, 2):
                last_down(m, LAST.then(m * JU, m), m % 2)
            with act.Fori(1, DT // 2 - 1) as i:
                work = Work(LAST.unit + JU, LAST.job + 1, i, 2 * JU, 2)
                last_down(i * 2 + 1, work, 1)
                last_down(i * 2 + 2, work.then(JU), 0)
            last_down(DT - 1, LAST.then((DT - 1) * JU, DT - 1), 1)
            store(1, DT - 1)
            for j in range(2):
                act.wait_ge(out_stored[j], 16 * (DT // 2))

        @block.vector
        def _(dve):
            def split_unit(work, n):
                u = work.unit + n
                if not work.upt and u >= ALL_UNITS:
                    return
                slot, part = u // 2 % RAWS, KU * (u % 2)
                dve.wait_ge(hi_ready, work.units_done(n + 1))
                nc.vector.tensor_tensor(w_lo[:, u % SPLITS], raw[:, slot, part:part + KU],
                                        w_hi[:, u % SPLITS].bitcast(F32), ALU.subtract).then_inc(split_ready, 1)

            def rsqrt(v, ready, count, factor=None):
                bits = v[:, 5].bitcast(I32)
                steps = 0

                def step(instruction):
                    nonlocal steps
                    steps += 1
                    instruction.then_inc(ready, 1)
                    dve.wait_ge(ready, count + steps)

                step(nc.vector.tensor_scalar(v[:, 1], v[:, 0], -0.5, None, ALU.mult))
                step(nc.vector.tensor_scalar(bits, v[:, 0].bitcast(I32), 1, None, ALU.logical_shift_right))
                step(nc.vector.tensor_scalar(bits, bits, -1, RSQRT_MAGIC, ALU.mult, ALU.add))
                for last in (False, False, True):
                    step(nc.vector.tensor_tensor(v[:, 2], v[:, 5], v[:, 5], ALU.mult))
                    step(nc.vector.tensor_tensor(v[:, 3], v[:, 2], v[:, 1], ALU.mult))
                    if last and factor is not None:
                        step(nc.vector.scalar_tensor_tensor(v[:, 4], v[:, 3], 1.5, factor, ALU.add, ALU.mult))
                    elif last:
                        step(nc.vector.tensor_scalar(v[:, 4], v[:, 3], 1.5, None, ALU.add))
                    else:
                        step(nc.vector.scalar_tensor_tensor(v[:, 5], v[:, 3], 1.5, v[:, 5], ALU.add, ALU.mult))
                assert steps == RSQRT_STEPS

            def invert_rms(n, into, share=1.0, times_x_r=None):
                dve.wait_ge(stat_ready, n + 1)
                if times_x_r is not None:
                    nc.vector.tensor_tensor(stat[:, 1], stats[:, 0:8], x_r2[:, :], ALU.mult).then_inc(with_r, 1)
                    dve.wait_ge(with_r, times_x_r + 1)
                    nc.vector.tensor_scalar(stat[:, 0], stat[:, 1], EPS, None, ALU.add).then_inc(eps_ready, 1)
                else:
                    nc.vector.tensor_scalar(stat[:, 0], stats[:, 0:8], share, EPS, ALU.mult,
                                            ALU.add).then_inc(eps_ready, 1)
                dve.wait_ge(eps_ready, n + 1)
                rsqrt(stat, newton, n * RSQRT_STEPS, None if times_x_r is None else x_r[:, :])
                nc.vector.tensor_tensor(into.rearrange("p (a c) -> p a c", c=64),
                                        stat[:, 5].unsqueeze(2).broadcast_to([P, 8, 64]),
                                        stat[:, 4].unsqueeze(2).broadcast_to([P, 8, 64]),
                                        ALU.mult).then_inc(r_ready, 1)

            def scale_by_rms(n, result):
                dve.wait_ge(wide_ready, n + 1)
                dve.wait_ge(taken, n + 1)
                nc.vector.tensor_tensor(result, scaled, wide[:, :], ALU.mult).then_inc(norm_ready, 1)

            def take_logits(kind, i, b):
                block_no = i * (2 * TB) + TB * kind + b
                n = P * (b + 1)
                if kind == 0:
                    dve.wait_ge(dist_ready, i + 5)
                else:
                    dve.wait_ge(bias_ready, i * TB + b + 1)
                at_least(dve, probs_ready, block_no)
                dve.wait_ge(scores_ready, block_no + 1)
                nc.vector.memset(pause[:, :], 0.0)
                for m in range(2 - kind):
                    bias = spare[:, S - n:S] if kind == 0 else bias_fox[:, bias_at[b]:bias_at[b + 1]]
                    r = nc.vector.tensor_tensor_reduce(out=logits[m][:, 0:n], in0=scores[m][:, 0:n], in1=bias,
                                                       scale=1.0, scalar=3e38, op0=ALU.add, op1=ALU.min,
                                                       accum_out=row_min[:, m:m + 1])
                r.then_inc(logits_ready, 1)

            def take_probs(kind, i, b):
                block_no = i * (2 * TB) + TB * kind + b
                n = P * (b + 1)
                dve.wait_ge(exp_ready, block_no + 1)
                at_least(dve, probs_turned, block_no - 1)
                maps = 2 - kind
                nc.vector.reciprocal(row_inv[:, 0:maps], row_sum[:, 0:maps]).then_inc(inv_ready, 1)
                dve.wait_ge(inv_ready, block_no + 1)
                if kind == 0:
                    nc.vector.tensor_scalar(logits[1][:, 0:n], logits[1][:, 0:n], row_inv[:, 1:2], lam_col,
                                            ALU.mult, ALU.mult).then_inc(second_scaled, 1)
                    dve.wait_ge(second_scaled, i * TB + b + 1)
                    nc.vector.scalar_tensor_tensor(probs[b % 2][:, 0:n], logits[0][:, 0:n], row_inv[:, 0:1],
                                                   logits[1][:, 0:n], ALU.mult, ALU.subtract).then_inc(probs_ready, 1)
                else:
                    nc.vector.tensor_scalar(probs[b % 2][:, 0:n], logits[0][:, 0:n], row_inv[:, 0:1], None,
                                            ALU.mult).then_inc(probs_ready, 1)

            def keep_turned(kind, i, b):
                block_no = i * (2 * TB) + TB * kind + b
                dve.wait_ge(probs_turned, block_no + 1)
                at_least(dve, pv_ready, i * 2 + kind)
                nc.vector.tensor_copy(p_keys[:, 0:b + 1, P * b:P * (b + 1)],
                                      turned[:, 0:P * (b + 1)].rearrange("p (j q) -> p j q", q=P)
                                      ).then_inc(p_keys_ready, 1)

            def head_step(kind, i, t, work):
                if kind == 1 and t == 10:
                    at_least(dve, f_row_ready, 1)
                    nc.vector.tensor_scalar(f_pick, f_row[:, :], ident[0:H, bass.ds(i, 1)], None,
                                            ALU.mult).then_inc(f_picked, 1)
                for b, when in enumerate(SOFTMAX_STEPS):
                    if t == when + 1:
                        take_probs(kind, i, b)
                for b, when in enumerate(SOFTMAX_STEPS):
                    if t == when:
                        take_logits(kind, i, b)
                    if t == TURN_STEPS[kind][b]:
                        keep_turned(kind, i, b)
                if t == 14:
                    dve.wait_ge(v_turned, i * 2 + kind + 1)
                    nc.vector.tensor_tensor(v_tok[kind].rearrange("p (b d) -> p b d", b=TB),
                                            turned[:, :].rearrange("p (b d) -> p b d", b=TB),
                                            x_r1.broadcast_to([P, TB, P]), ALU.mult).then_inc(v_ready, 1)
                if kind == 1 and t == 23:
                    dve.wait_ge(o_hi, i * 2 + 2)
                    nc.vector.tensor_tensor(tile(b_lo, i + H), logits[0], tile(b_hi, i + H).bitcast(F32),
                                            ALU.subtract).then_inc(o_ready, 1)
                if kind == 0 and t == NORM_STEPS[2] + NORM_LENGTH + 1:
                    dve.wait_ge(o_hi, i * 2 + 1)
                    nc.vector.tensor_tensor(tile(b_lo, i), v_feat, tile(b_hi, i).bitcast(F32),
                                            ALU.subtract).then_inc(o_ready, 1)

            def scale_step(kind, i, t, work):
                n = i * 5 + 2 * kind
                for which, result in enumerate((qn[kind], kn[kind])):
                    if t == NORM_STEPS[which] + NORM_LENGTH:
                        scale_by_rms(n + which, result)
                if kind == 0 and t == NORM_STEPS[2] + NORM_LENGTH:
                    scale_by_rms(n + 4, v_feat)

            def norm_step(kind, i, t, work):
                n = i * 5 + 2 * kind
                for which in range(2):
                    if t == NORM_STEPS[which] + 1:
                        invert_rms(n + which, r_wide, times_x_r=i * 4 + (2 * kind + which))
                if kind == 0 and t == NORM_STEPS[2] + 1:
                    invert_rms(n + 4, r_wide)

            dve.wait_ge(cols_turned, 1)
            nc.vector.tensor_copy(cols[:, 0:64], stats[:, 0:64]).then_inc(cols_ready, 1)
            dve.wait_ge(cols_ready, 1)

            def split_h(tiles):
                for k in tiles:
                    dve.wait_ge(h_hi, k + 1)
                    nc.vector.scalar_tensor_tensor(a_lo[:, k], turn_banks[k % TURNS][:, :], cols[:, k:k + 1],
                                                   a_hi[:, k].bitcast(F32), ALU.mult,
                                                   ALU.subtract).then_inc(h_ready, 1)

            split_h(range(0, KU))
            split_unit(FORGET, 0)
            split_unit(FORGET, 1)
            split_h(range(KU, 3 * KU))
            split_unit(FORGET, 2)
            split_unit(FORGET, 3)
            split_h(range(3 * KU, DT))
            for n in range(JU, JU + LEAD):
                split_unit(FORGET, n)
            dve.wait_ge(small_turned, 1)
            nc.vector.tensor_copy(cols[:, 64:P], stats[:, 64:P]).then_inc(small_ready, 1)
            dve.wait_ge(small_ready, 1)
            nc.vector.tensor_scalar(neg_bgate[:, :], cols[:, 32:64], -1.0, None, ALU.mult)
            nc.vector.tensor_scalar(gains[:, 0:1], cols[:, 67:68], -(HD // 2) ** -0.5, None, ALU.mult)
            nc.vector.tensor_scalar(gains[:, 1:2], cols[:, 65:66], -HD ** -0.5, None, ALU.mult)
            nc.vector.tensor_scalar(gains[:, 2:3], cols[:, 64:65], 1.0 - LAMBDA_INIT, None,
                                    ALU.mult).then_inc(gains_ready, 1)
            nc.vector.tensor_tensor(lam[:, 5:6], cols[:, 69:70], cols[:, 70:71], ALU.mult).then_inc(lam_step, 1)
            dve.wait_ge(lam_step, 1)
            dve.wait_ge(consts_ready, 9)
            nc.vector.tensor_scalar(lam[:, 0:2], mean2[:, 0:2], lam[:, 5:6], None, ALU.mult).then_inc(lam_product, 1)

            dve.wait_ge(x_summed, 2 * TB)
            pairs = x_sums[:, :].rearrange("p (b e) -> p b e", e=2)
            nc.vector.tensor_tensor(x_stat[:, 1], pairs[:, :, 0], pairs[:, :, 1], ALU.add).then_inc(x_eps, 1)
            dve.wait_ge(x_eps, 1)
            nc.vector.tensor_scalar(x_stat[:, 0], x_stat[:, 1], 1.0 / D, EPS, ALU.mult, ALU.add).then_inc(x_eps, 1)
            dve.wait_ge(x_eps, 2)
            rsqrt(x_stat, x_newton, 0)
            nc.vector.tensor_tensor(x_r[:, :].rearrange("p (b e) -> p b e", e=2),
                                    x_stat[:, 5].unsqueeze(2).broadcast_to([P, TB, 2]),
                                    x_stat[:, 4].unsqueeze(2).broadcast_to([P, TB, 2]), ALU.mult).then_inc(x_r_ready, 1)
            dve.wait_ge(x_r_ready, 1)
            nc.vector.tensor_tensor(x_r2[:, :], x_r[:, :], x_r[:, :], ALU.mult).then_inc(x_r_ready, 1)
            dve.wait_ge(x_r_ready, 2)

            def forget_logits():
                dve.wait_ge(f_turned, 1)
                dve.wait_ge(bforget_loaded, 16)
                z = heads_out[:, :].rearrange("p (b c) -> p b c", b=TB)[:, :, P - NF:P]
                nc.vector.tensor_tensor(lf_t[:, 1], z, x_r1.broadcast_to([P, TB, NF]), ALU.mult).then_inc(f_logit, 1)
                dve.wait_ge(f_logit, 1)
                nc.vector.tensor_tensor(lf_t[:, 0], lf_t[:, 1], bforget[:, :].unsqueeze(1).broadcast_to([P, TB, NF]),
                                        ALU.add).then_inc(f_logit, 1)
                dve.wait_ge(f_logit, 2)
                nc.vector.scalar_tensor_tensor(lf_t[:, 1], lf_t[:, 0], -1.0, lf_t[:, 0], ALU.mult,
                                               ALU.min).then_inc(f_neg, 1)
                dve.wait_ge(f_exp, 1)
                nc.vector.tensor_scalar(lf_t[:, 2], lf_t[:, 2], 1.0, None, ALU.add).then_inc(f_one, 1)
                dve.wait_ge(f_ln, 1)
                nc.vector.scalar_tensor_tensor(lf[:, :, :], lf_t[:, 0], 0.0, lf_t[:, 1], ALU.min,
                                               ALU.subtract).then_inc(f_ready, 1)

            def heads_turn(i, work):
                first = isinstance(i, int) and i == 0
                for u in range(HU):
                    split_unit(work, u + LEAD)
                    if first and u == 1:
                        dve.wait_ge(lam_exps, 1)
                        nc.vector.scalar_tensor_tensor(lam_col, lam[:, 2:3], LAMBDA_INIT, lam[:, 3:4], ALU.add,
                                                       ALU.subtract).then_inc(lam_step, 1)
                        forget_logits()
                    if first and u == 3:
                        dve.wait_ge(f_summed, 1)
                        nc.vector.tensor_copy(f_row[:, :], heads_out[0:H, :]).then_inc(f_row_ready, 1)
                    if first and u == 4:
                        dve.wait_ge(f_back, 1)
                        nc.vector.tensor_scalar(neg_f[:, :, :], heads_out[:, 0:TB * H].rearrange("p (b h) -> p b h", b=TB),
                                                -1.0, None, ALU.mult).then_inc(neg_f_ready, 1)
                    head_hooks(scale_step, u, i, work)
                    head_hooks(head_step, u, i, work)
                    head_hooks(norm_step, u, i, work)

            heads_turn(0, HEADS)
            with dve.Fori(1, H) as i:
                heads_turn(i, Work(HEADS.unit, HEADS.job, i, HU, HJ))

            def merge(m, work, last=False):
                inverted, used = (MU - 2, MU - 1), (MU - 2, MU - 1)
                if not (isinstance(m, int) and m == 0):
                    inverted, used = (JU + 1, 2 * JU), (2 * JU + BU - 1, 2 * JU + 2 * BU - 1)
                for u in range(MU):
                    split_unit(work, u + LEAD)
                    if isinstance(m, int) and m == 0:
                        if u == NORM_STEPS[2] + NORM_LENGTH - HU:
                            dve.wait_ge(r_row_wide, 1)
                        head_hooks(scale_step, u, H, work)
                        head_hooks(head_step, u, H, work)
                        head_hooks(norm_step, u, H, work)
                    if isinstance(m, int) and m == 0 and u == 2:
                        dve.wait_ge(v_turned, 2 * H)
                        nc.vector.tensor_copy(v_feat.rearrange("p (a c) -> p a c", c=64),
                                              x_r[:, :].unsqueeze(2).broadcast_to([P, 2 * TB, 64])).then_inc(r_repeated, 1)
                    for g, gate in enumerate((gate_d, gate_f)):
                        if u == (g + 1) * JU:
                            dve.wait_ge(unit_used, work.units_done((g + 1) * JU))
                            dve.wait_ge(r_row_ready, 1)
                            if isinstance(m, int) and m == 0:
                                dve.wait_ge(probs_turned, 2 * TB * H - (0 if g else TB))
                            nc.vector.tensor_tensor(gate, jobs[work.then(0, g).bank()][:, :], spare[:, :],
                                                    ALU.mult).then_inc(gate_scaled, 1)
                        if u == inverted[g]:
                            dve.wait_ge(gate_exp, m * 2 + g + 1)
                            nc.vector.tensor_scalar(gate, gate, 1.0, None, ALU.add).then_inc(gate_one, 1)
                            dve.wait_ge(gate_one, m * 2 + g + 1)
                            nc.vector.reciprocal(gate, gate).then_inc(gate_ready, 1)
                    if last and u >= 2 * JU:
                        for k in range((u - 2 * JU) * 3, (u - 2 * JU) * 3 + 3):
                            split_merged(k)
                    for g, gate, part in ((0, gate_d, part_d), (1, gate_f, part_f)):
                        if u == used[g]:
                            dve.wait_ge(gate_ready, m * 2 + g + 1)
                            dve.wait_ge(unit_used, work.units_done(2 * JU + (g + 1) * BU))
                            nc.vector.tensor_tensor(part, jobs[work.then(0, g).bank()][:, :], gate,
                                                    ALU.mult).then_inc(parts_ready, 1)
                dve.wait_ge(parts_ready, m * 2 + 2)
                nc.vector.tensor_tensor(tile(main, m), part_d, part_f, ALU.add).then_inc(merged_ready, 1)

            def split_merged(k):
                if k % KU == KU - 1:
                    return
                dve.wait_ge(m_hi, k + 1)
                nc.vector.tensor_tensor(a_lo[:, k], main[:, k], a_hi[:, k].bitcast(F32),
                                        ALU.subtract).then_inc(m_ready, 1)

            merge(0, MERGE)
            with dve.Fori(0, DT // 2 - 1) as i:
                work = Work(MERGE.unit + MU, MERGE.job + MJ, i, 2 * MU, 2 * MJ)
                merge(i * 2 + 1, work)
                merge(i * 2 + 2, work.then(MU, MJ))
            merge(DT - 1, MERGE.then((DT - 1) * MU, (DT - 1) * MJ), last=True)
            for k in range(2 * BU * 3, DT):
                split_merged(k)

            def projected(m, work):
                for u in range(JU):
                    split_unit(work, u + LEAD)
                dve.wait_ge(unit_used, work.units_done(JU))
                dve.wait_ge(xr_ready, m + 1)
                nc.vector.tensor_tensor(tile(main, m), jobs[work.bank()][:, :], x_feat, ALU.add).then_inc(x2_ready, 1)
                dve.wait_ge(x2_sq, m + 1)
                dve.wait_ge(sum_cleared, 1)
                at_least(dve, sum_ready, m)
                nc.vector.tensor_tensor(spare[:, :], spare[:, :], x_sq, ALU.add).then_inc(sum_ready, 1)
                dve.wait_ge(x2_hi, m + 1)
                nc.vector.scalar_tensor_tensor(tile(b_lo, m), tile(main, m), cols[:, bass.ds(m + DT, 1)],
                                               tile(b_hi, m).bitcast(F32), ALU.mult, ALU.subtract).then_inc(x2_lo, 1)

            for j in range(2):
                projected(j, PROJ.then(j * JU, j))
            with dve.Fori(1, DT // 2) as i:
                work = Work(PROJ.unit, PROJ.job, i, 2 * JU, 2)
                for j in range(2):
                    projected(i * 2 + j, work.then(j * JU, j))

            def up(m, c, work, first=False):
                for u in range(JU):
                    split_unit(work, u + LEAD)
                    if first and u == 2:
                        invert_rms(5 * H, x_sq, share=P / D)
                n = c * DT + m + 1
                dve.wait_ge(unit_used, work.units_done(JU))
                dve.wait_ge(rms_ready, 1)
                nc.vector.tensor_tensor(relu_in, jobs[work.bank()][:, :], spare[:, :], ALU.mult).then_inc(up_scaled, 1)
                dve.wait_ge(up_scaled, n)
                nc.vector.scalar_tensor_tensor(relu_sq, relu_in, 0.0, relu_in, ALU.max, ALU.mult).then_inc(up_squared, 1)
                dve.wait_ge(up_hi, n)
                nc.vector.tensor_tensor(tile(a_lo, m), relu_sq, tile(a_hi, m).bitcast(F32),
                                        ALU.subtract).then_inc(up_ready, 1)

            def ups(c, first_turn):
                with dve.Fori(first_turn, DT // 2) as i:
                    work = Work(MLP.unit, MLP.job, c * DT + i, 2 * JU, 2)
                    for j in range(2):
                        up(i * 2 + j, c, work.then(j * JU, j))

            def downs(c):
                with dve.Fori(0, DT // 2) as i:
                    work = Work(MLP.unit + DT * JU, MLP.job + DT, c * DT + i, 2 * JU, 2)
                    for j in range(2):
                        for u in range(JU):
                            split_unit(work.then(j * JU), u + LEAD)
                        dve.wait_ge(unit_used, work.then(j * JU).units_done(JU))
                        at_least(dve, down_added, c * DT)
                        m = i * 2 + j
                        nc.vector.tensor_tensor(tile(main, m), jobs[work.then(0, j).bank()][:, :], tile(main, m),
                                                ALU.add).then_inc(down_added, 1)

            dve.wait_ge(x2_ready, DT)
            for j in range(2):
                up(j, 0, MLP.then(j * JU, j), first=j == 0)
            ups(0, 1)
            downs(0)
            with dve.Fori(1, CH - 1) as c:
                ups(c, 0)
                downs(c)
            ups(CH - 1, 0)
            dve.wait_ge(down_added, (CH - 1) * DT)

            LAST = MLP.then((CH - 1) * CU + DT * JU, (CH - 1) * CJ + DT)

            def last_down(m, work, j):
                for u in range(JU):
                    split_unit(work, u + LEAD)
                dve.wait_ge(unit_used, work.units_done(JU))
                at_least(dve, fin_turned, m - 1)
                nc.vector.tensor_tensor(fin[j], jobs[work.bank()][:, :], tile(main, m), ALU.add).then_inc(down_added, 1)

            last_down(0, LAST, 0)
            for m in (1, 2):
                last_down(m, LAST.then(m * JU, m), m % 2)
            with dve.Fori(1, DT // 2 - 1) as i:
                work = Work(LAST.unit + JU, LAST.job + 1, i, 2 * JU, 2)
                last_down(i * 2 + 1, work, 1)
                last_down(i * 2 + 2, work.then(JU), 0)
            last_down(DT - 1, LAST.then((DT - 1) * JU, DT - 1), 1)

        @block.tensor
        def _(pe):
            def job(work, act_hi, act_lo, first_tile=0, units=JU, before_unit=None):
                result = jobs[work.bank()]
                for n in range(units):
                    if before_unit is not None:
                        before_unit(n)
                    pe.wait_ge(split_ready, work.units_done(n + 1))
                    slot = (work.unit + n) % SPLITS
                    for k in range(KU):
                        f = first_tile + n * KU + k
                        nc.tensor.matmul(result[:, :], w_hi[:, slot, k], act_hi[:, f], start=(n == 0 and k == 0),
                                         stop=False)
                        nc.tensor.matmul(result[:, :], w_hi[:, slot, k], act_lo[:, f], start=False, stop=False)
                        done = nc.tensor.matmul(result[:, :], w_lo[:, slot, k], act_hi[:, f], start=False,
                                                stop=(n == units - 1 and k == KU - 1))
                    done.then_inc(unit_used, 1)

            def mean_squares(n, squared, averages):
                at_least(pe, eps_ready, n)
                for b in range(TB):
                    last = nc.tensor.matmul(stats[:, 2 * b:2 * b + 2], squared[:, P * b:P * (b + 1)], averages,
                                            start=True, stop=True)
                last.then_inc(stat_ready, 1)

            def widen(n, repeated):
                pe.wait_ge(r_ready, n + 1)
                at_least(pe, norm_ready, n)
                for b in range(TB):
                    last = nc.tensor.transpose(wide[:, P * b:P * (b + 1)], repeated[:, P * b:P * (b + 1)],
                                               ident[:, :])
                last.then_inc(wide_ready, 1)

            def norm_steps(n, kind, t, first):
                if t == first + 1:
                    pe.wait_ge(sq_ready, n + 1)
                    mean_squares(n, squares, mean2[:, 2 * kind:2 * kind + 2])
                if t == first + NORM_LENGTH:
                    widen(n, r_wide)

            def take_scores(kind, i, b):
                block_no = i * (2 * TB) + TB * kind + b
                at_least(pe, logits_ready, block_no)
                n = P * (b + 1)
                for m in range(2 - kind):
                    part = slice(64 * m, 64 * m + 64) if kind == 0 else slice(0, P)
                    last = nc.tensor.matmul(scores[m][:, 0:n], qn[kind][part, P * b:P * (b + 1)],
                                            kn[kind][part, 0:n], start=True, stop=True)
                last.then_inc(scores_ready, 1)

            def turn_probs(kind, i, b):
                block_no = i * (2 * TB) + TB * kind + b
                pe.wait_ge(probs_ready, block_no + 1)
                at_least(pe, p_keys_ready, block_no)
                pe.wait_ge(v_ready, i * 2 + kind + 1)
                for j in range(b + 1):
                    last = nc.tensor.transpose(turned[:, P * j:P * (j + 1)], probs[b % 2][:, P * j:P * (j + 1)],
                                               ident[:, :])
                last.then_inc(probs_turned, 1)

            def head_step(kind, i, t, work):
                n = i * 5 + 2 * kind
                for which in range(2):
                    norm_steps(n + which, kind, t, NORM_STEPS[which])
                if kind == 1 and t == 11:
                    pe.wait_ge(f_picked, i + 1)
                    pe.wait_ge(logits_ready, i * (2 * TB) + TB)
                    nc.tensor.matmul(scores[1][:, :], ones[0:H, :], f_pick, start=True, stop=True
                                     ).then_inc(f_wide, 1)
                if t == 13:
                    pe.wait_ge(v_copied, i * 2 + kind + 1)
                    at_least(pe, p_keys_ready, i * (2 * TB) + TB * kind)
                    for b in range(TB):
                        last = nc.tensor.transpose(turned[:, P * b:P * (b + 1)], v_feat[:, P * b:P * (b + 1)],
                                                   ident[:, :])
                    last.then_inc(v_turned, 1)
                if t == SOFTMAX_STEPS[0]:
                    pe.wait_ge(norm_ready, n + 2)
                for b, when in enumerate(SOFTMAX_STEPS):
                    if t == when:
                        take_scores(kind, i, b)
                for b, when in enumerate(TURN_STEPS[kind]):
                    if t == when:
                        turn_probs(kind, i, b)
                if t == PV_STEPS[kind]:
                    pe.wait_ge(p_keys_ready, i * (2 * TB) + TB * kind + TB)
                    if kind == 0:
                        at_least(pe, o_copied, i)
                    else:
                        pe.wait_ge(taken, i * 5 + 5)
                        if isinstance(i, int) and i == H - 1:
                            pe.wait_ge(r_row_ready, 1)
                    for j in range(TB):
                        last = nc.tensor.matmul(heads_out[:, P * j:S], v_tok[kind][:, P * j:P * (j + 1)],
                                                p_keys[:, j, P * j:S], start=(j == 0), stop=(j == TB - 1))
                    last.then_inc(pv_ready, 1)
                if kind == 0:
                    norm_steps(n + 4, 1, t, NORM_STEPS[2])

            pe.wait_ge(params_loaded, 16 * 3)
            pe.wait_ge(ident_ready, 1)
            nc.tensor.transpose(stats[:, 0:64], param_rows[0:64], ident[0:64, 0:64]).then_inc(cols_turned, 1)

            def turn_x(tiles):
                for k in tiles:
                    at_least(pe, h_ready, k - TURNS + 1)
                    pe.wait_ge(x_loaded[k // KU], 16 * TB)
                    for b in range(TB):
                        last = nc.tensor.transpose(turn_banks[k % TURNS][:, P * b:P * (b + 1)],
                                                   x_tok[:, b, P * k:P * (k + 1)], ident[:, :])
                    last.then_inc(x_turned, 1)

            turn_x(range(KU))

            def forget_unit(n):
                turn_x(range(KU * (n + 1), min(DT, KU * (n + 2))))
                pe.wait_ge(h_ready, KU * (n + 1))

            job(FORGET, a_hi, a_lo, before_unit=forget_unit)

            def forget_step(u):
                if u == 0:
                    pe.wait_ge(small_loaded, 16 * 11)
                    nc.tensor.transpose(stats[:, 64:P], param_rows[64:P], ident[64:P, 64:P]).then_inc(small_turned, 1)
                if u == 1:
                    pe.wait_ge(lam_product, 1)
                    nc.tensor.matmul(stats[:, 0:2], ones[:, :], lam[:, 0:2], start=True, stop=True).then_inc(lam_sums, 1)
                    pe.wait_ge(f_copied, 1)
                    for b in range(TB):
                        last = nc.tensor.transpose(heads_out[:, P * b:P * (b + 1)], f_feat[:, P * b:P * (b + 1)],
                                                   ident[:, :])
                    last.then_inc(f_turned, 1)
                if u == 3:
                    pe.wait_ge(f_ready, 1)
                    pe.wait_ge(tri_ready, 1)
                    for b in range(TB):
                        last = nc.tensor.matmul(heads_out[0:H, P * b:S], lf[:, b], tri[:, 0:S - P * b],
                                                start=(b == 0), stop=(b == TB - 1))
                    last.then_inc(f_summed, 1)
                if u == 4:
                    pe.wait_ge(f_row_ready, 1)
                    for b in range(TB):
                        last = nc.tensor.transpose(heads_out[:, H * b:H * (b + 1)], f_row[:, P * b:P * (b + 1)],
                                                   ident[0:H, 0:H])
                    last.then_inc(f_back, 1)
                if u == 5:
                    pe.wait_ge(neg_f_ready, 1)
                    pe.wait_ge(gains_ready, 1)
                    pe.wait_ge(lam_step, 2)

            def heads_turn(i, work):
                first = isinstance(i, int) and i == 0
                for j in range(HJ):
                    if j == 0:
                        at_least(pe, taken, i * 5 - 1)
                    elif j == 1:
                        pe.wait_ge(f_copied, 1) if first else pe.wait_ge(v_copied, i * 2)
                    elif j == 4:
                        pe.wait_ge(v_copied, i * 2 + 1)
                    else:
                        pe.wait_ge(taken, i * 5 + {2: 1, 3: 2, 5: 3}[j])

                    def before_unit(n):
                        if first:
                            forget_step(j * JU + n)
                        head_hooks(head_step, j * JU + n, i, work)

                    job(work.then(j * JU, j), a_hi, a_lo, before_unit=before_unit)

            heads_turn(0, HEADS)
            with pe.Fori(1, H) as i:
                heads_turn(i, Work(HEADS.unit, HEADS.job, i, HU, HJ))

            def merge(m, work):
                first = isinstance(m, int) and m == 0

                def hooks(at):
                    def before_unit(n):
                        head_hooks(head_step, at + n, H, work)
                        if at + n == 3:
                            pe.wait_ge(r_repeated, 1)
                            pe.wait_ge(taken, 5 * H)
                            for b in range(TB):
                                last = nc.tensor.transpose(heads_out[:, P * b:P * (b + 1)],
                                                           v_feat[:, P * b:P * (b + 1)], ident[:, :])
                            last.then_inc(r_row_wide, 1)
                    return before_unit if first else None

                if first:
                    pe.wait_ge(taken, 5 * H - 1)
                else:
                    pe.wait_ge(parts_ready, m * 2 - 1)
                job(work, a_hi, a_lo, before_unit=hooks(0))
                if first:
                    pe.wait_ge(v_copied, 2 * H)
                else:
                    pe.wait_ge(parts_ready, m * 2)
                job(work.then(JU), a_hi, a_lo, before_unit=hooks(JU))
                pe.wait_ge(gate_scaled, m * 2 + 1)
                if first:
                    pe.wait_ge(o_ready, 2 * H - 1)
                job(work.then(2 * JU, 2), b_hi, b_lo, 0, BU, before_unit=hooks(2 * JU))

                def last_hooks(n):
                    head_hooks(head_step, 2 * JU + BU + n, H, work)
                    if n == BU - 1:
                        pe.wait_ge(o_ready, 2 * H)

                pe.wait_ge(gate_scaled, m * 2 + 2)
                job(work.then(2 * JU + BU, 3), b_hi, b_lo, H, BU, before_unit=last_hooks if first else None)

            merge(0, MERGE)
            with pe.Fori(0, DT // 2 - 1) as i:
                work = Work(MERGE.unit + MU, MERGE.job + MJ, i, 2 * MU, 2 * MJ)
                merge(i * 2 + 1, work)
                merge(i * 2 + 2, work.then(MU, MJ))
            merge(DT - 1, MERGE.then((DT - 1) * MU, (DT - 1) * MJ))

            def projected(m, j, work):
                first = isinstance(m, int) and m == 0

                def before_unit(n):
                    if first:
                        pe.wait_ge(m_ready, (KU - 1) * (n + 1))
                        pe.wait_ge(m_ready_too, n + 1)
                    if n == 2:
                        if isinstance(m, int):
                            pe.wait_ge(xr_loaded[j], 16)
                        else:
                            pe.wait_ge(xr_loaded[j], m * 8 + (16 - 8 * j))
                        at_least(pe, xr_ready, m)
                        for b in range(TB):
                            last = nc.tensor.transpose(turned[:, P * b:P * (b + 1)],
                                                       x_slot[j][:, P * b:P * (b + 1)], ident[:, :])
                        last.then_inc(xr_turned, 1)

                if isinstance(m, int):
                    pe.wait_ge(parts_ready, 2 * DT - 1 + m)
                else:
                    pe.wait_ge(x2_ready, m - 1)
                job(work, a_hi, a_lo, before_unit=before_unit)

            for j in range(2):
                projected(j, j, PROJ.then(j * JU, j))
            with pe.Fori(1, DT // 2) as i:
                work = Work(PROJ.unit, PROJ.job, i, 2 * JU, 2)
                for j in range(2):
                    projected(i * 2 + j, j, work.then(j * JU, j))

            def ups(c, bank_taken):
                def turn(i, work):
                    for j in range(2):
                        m = i * 2 + j
                        at_start = isinstance(c, int) and isinstance(i, int) and c == 0
                        if isinstance(i, int):
                            pe.wait_ge(bank_taken, c * DT + (j - 1) if bank_taken is down_added else DT - 1 + j)
                        else:
                            pe.wait_ge(up_scaled, c * DT + m - 1)

                        def before_unit(n):
                            if at_start:
                                pe.wait_ge(x2_lo, min(DT, KU * (n + 1)))
                            if at_start and j == 0 and n == 2:
                                pe.wait_ge(sum_ready, DT)
                                mean_squares(5 * H, spare, mean2[:, 2:4])
                            if at_start and j == 1 and n == 0:
                                widen(5 * H, x_sq)

                        job(work.then(j * JU, j), b_hi, b_lo, before_unit=before_unit)

                turn(0, Work(MLP.unit, MLP.job, c * DT, 2 * JU, 2))
                with pe.Fori(1, DT // 2) as i:
                    turn(i, Work(MLP.unit, MLP.job, c * DT + i, 2 * JU, 2))

            def downs(c):
                def turn(i, work):
                    for j in range(2):
                        m = i * 2 + j
                        if isinstance(i, int):
                            pe.wait_ge(up_scaled, c * DT + DT - 1 + j)
                        else:
                            pe.wait_ge(down_added, c * DT + m - 1)

                        def before_unit(n):
                            if isinstance(i, int) and j == 0:
                                pe.wait_ge(up_ready, c * DT + KU * (n + 1))

                        job(work.then(j * JU, j), a_hi, a_lo, before_unit=before_unit)

                turn(0, Work(MLP.unit + DT * JU, MLP.job + DT, c * DT, 2 * JU, 2))
                with pe.Fori(1, DT // 2) as i:
                    turn(i, Work(MLP.unit + DT * JU, MLP.job + DT, c * DT + i, 2 * JU, 2))

            ups(0, x2_ready)
            downs(0)
            with pe.Fori(1, CH - 1) as c:
                ups(c, down_added)
                downs(c)
            ups(CH - 1, down_added)

            LAST = MLP.then((CH - 1) * CU + DT * JU, (CH - 1) * CJ + DT)
            done_before = (CH - 1) * DT

            def turn_output(m, j):
                pe.wait_ge(down_added, m + (done_before + 1))
                at_least(pe, stage_ready, m - 1)
                for b in range(TB):
                    last = nc.tensor.transpose((turned, wide)[j][:, P * b:P * (b + 1)], fin[j][:, P * b:P * (b + 1)],
                                               ident[:, :])
                last.then_inc(fin_turned, 1)

            def last_down(m, work, j):
                static = isinstance(m, int)
                if static and m <= 1:
                    pe.wait_ge(up_scaled, CH * DT - 1 + m)
                else:
                    pe.wait_ge(down_added, m + (done_before - 1))

                def before_unit(n):
                    if static and m == 0:
                        pe.wait_ge(up_ready, done_before + KU * (n + 1))
                    if n == 1 and not (static and m == 0):
                        turn_output(m - 1, 1 - j)

                job(work, a_hi, a_lo, before_unit=before_unit)

            last_down(0, LAST, 0)
            for m in (1, 2):
                last_down(m, LAST.then(m * JU, m), m % 2)
            with pe.Fori(1, DT // 2 - 1) as i:
                work = Work(LAST.unit + JU, LAST.job + 1, i, 2 * JU, 2)
                last_down(i * 2 + 1, work, 1)
                last_down(i * 2 + 2, work.then(JU), 0)
            last_down(DT - 1, LAST.then((DT - 1) * JU, DT - 1), 1)
            turn_output(DT - 1, 1)


INPUTS = ["x", "norm_mix", "w_in", "b_forget", "qnorm_diff", "knorm_diff", "lambda_q1", "lambda_k1", "lambda_q2",
          "lambda_k2", "subln_diff", "qnorm_fox", "knorm_fox", "w_branch_diff", "w_branch_fox", "w_gate", "b_gate",
          "w_out", "norm_mlp", "w_mlp_up", "w_mlp_down"]


def kernel(**inputs):
    import numpy as np
    import concourse.bacc as bacc
    from concourse.bass_utils import run_bass_kernel_spmd

    nc = bacc.Bacc("TRN2", target_bir_lowering=False, num_devices=1)
    arrays, args = {}, []
    for name in INPUTS:
        a = np.ascontiguousarray(inputs[name])
        arrays[f"in_{name}"] = a
        args.append(nc.dram_tensor(f"in_{name}", a.shape, mybir.dt.from_np(a.dtype), kind="ExternalInput").ap())
    shape = arrays["in_x"].shape
    args.append(nc.dram_tensor("out", shape, F32, kind="ExternalOutput").ap())
    build(nc, *args)
    result = run_bass_kernel_spmd(nc, [arrays], core_ids=[0])
    return result.results[0]["out"]
```

```python
import math
from contextlib import ExitStack

import concourse.bass as bass
from concourse import mybir

F32 = mybir.dt.float32
F32R = mybir.dt.float32r
I32 = mybir.dt.int32
ACT = mybir.ActivationFunctionType
ALU = mybir.AluOpType

P = 128
KU = 4
SPLITS = 4
RAWS = 4
LEAD = 3
EPS = 1e-6
RSQRT_MAGIC = 0x5F3759DF
RSQRT_STEPS = 12
SOFTMAX_STEPS = (14, 15, 17, 19)
TURN_STEPS = ((16, 17, 20, 22), (16, 17, 19, 21))
PV_STEPS = (23, 22)
NORM_STEPS = (4, 8, 24)
NORM_LENGTH = 4
MASKED = 1e30
LAMBDA_INIT = 0.8 - 0.6 * math.exp(-0.3 * 0)


def at_least(eng, sem, value):
    if not (isinstance(value, int) and value <= 0):
        eng.wait_ge(sem, value)


class Work:

    def __init__(self, unit, job, loop=0, units_per_turn=0, jobs_per_turn=0):
        assert units_per_turn % (2 * RAWS) == 0 and jobs_per_turn % 2 == 0
        self.unit, self.job = unit, job
        self.loop, self.upt, self.jpt = loop, units_per_turn, jobs_per_turn

    def then(self, units, jobs=1):
        return Work(self.unit + units, self.job + jobs, self.loop, self.upt, self.jpt)

    def units_done(self, n):
        return self.unit + n + self.loop * self.upt if self.upt else self.unit + n

    def loads(self, n):
        half = (self.unit + n) // 2
        v = 16 * (half // RAWS + 1)
        return v + self.loop * (16 * self.upt // 2 // RAWS) if self.upt else v

    def bank(self):
        return self.job % 2


def tile(tensor, m):
    return tensor[:, m] if isinstance(m, int) else tensor[:, bass.ds(m, 1)].rearrange("p a s -> p (a s)")


def build(nc, x, norm_mix, w_in, b_forget, qnorm_diff, knorm_diff, lambda_q1, lambda_k1, lambda_q2,
          lambda_k2, subln_diff, qnorm_fox, knorm_fox, w_branch_diff, w_branch_fox, w_gate, b_gate,
          w_out, norm_mlp, w_mlp_up, w_mlp_down, out):
    _, S, D = x.shape
    assert x.shape[0] == 1 and w_in.shape[0] == 1 and S == 512
    DT = D // P
    TB = S // P
    HD = qnorm_fox.shape[1]
    WD, WF = w_branch_diff.shape[1], w_branch_fox.shape[1]
    H = WD // P
    NF = b_forget.shape[1]
    FF = w_mlp_up.shape[2]
    CH = FF // D
    JU = DT // KU
    BU = H // KU
    assert HD == P and WF == WD and NF == H == 8 and DT == 16 and CH * D == FF

    FORGET = Work(0, 0)
    HEADS = FORGET.then(JU)
    HU, HJ = 6 * JU, 6
    MERGE = HEADS.then(H * HU, H * HJ)
    MU, MJ = 2 * JU + 2 * BU, 4
    PROJ = MERGE.then(DT * MU, DT * MJ)
    MLP = PROJ.then(DT * JU, DT)
    CU, CJ = 2 * DT * JU, 2 * DT
    ALL_UNITS = MLP.unit + CH * CU

    xt = x[0].rearrange("(b p) d -> p b d", p=P)
    outt = out[0].rearrange("(b p) d -> p b d", p=P)

    with ExitStack() as ctx:
        def sb(name, shape, dt=F32):
            return ctx.enter_context(nc.sbuf_tensor(name, shape, dt))

        def sem(name):
            return ctx.enter_context(nc.semaphore(name))

        a_hi, a_lo = sb("a_hi", [P, DT, S], F32R), sb("a_lo", [P, DT, S], F32R)
        b_hi, b_lo = sb("b_hi", [P, DT, S], F32R), sb("b_lo", [P, DT, S], F32R)
        main = sb("main", [P, DT, S])
        side = sb("side", [P, 4, S])
        raw = sb("raw", [P, RAWS, 2 * KU, P])
        w_hi, w_lo = sb("w_hi", [P, SPLITS, KU, P], F32R), sb("w_lo", [P, SPLITS, KU, P], F32R)
        spare = sb("spare", [P, S])
        k_lo = sb("k_lo", [P, S], F32R)
        ident = sb("ident", [P, P])
        ones = sb("ones", [P, P])
        causal = sb("causal", [P, P])
        cols = sb("cols", [P, P])
        neg_bgate = sb("neg_bgate", [P, 2 * DT])
        gains = sb("gains", [P, 8])
        halves = sb("halves", [P, 2])
        stat, x_stat = sb("stat", [P, 7, 8]), sb("x_stat", [P, 6, TB])
        x_sums, x_r = sb("x_sums", [P, 2 * TB]), sb("x_r", [P, 2 * TB])
        x_eps = sb("x_eps", [P, 2 * TB])
        x_r1 = x_r[:, :].rearrange("p (b e) -> p b e", e=2)[:, :, 0:1]
        bforget = sb("bforget", [P, NF])
        lf = sb("lf", [P, TB, NF])
        lf_t = sb("lf_t", [P, 3, TB, NF])
        neg_f = sb("neg_f", [P, TB, H])
        lam = sb("lam", [P, 6])
        pause = sb("pause", [P, 1])
        one_half = sb("one_half", [P, 1])
        row_min, row_sum, row_inv = sb("row_min", [P, 2]), sb("row_sum", [P, 2]), sb("row_inv", [P, 2])

        x_tok = main[:, :, :].rearrange("p (b f) s -> p b (f s)", b=TB)
        qn_fox, kn_fox = main[:, 2], main[:, 3]
        q_pair, k_pair = [b_hi[:, H - 1], b_hi[:, 2 * H - 1]], [b_lo[:, H - 1], b_lo[:, 2 * H - 1]]
        qk_normed = main[:, 1]
        maps = [slice(0, HD // 2), slice(HD // 2, HD)]
        v_tok = [main[:, 4], main[:, 5]]
        v_feat, squares, scaled = main[:, 6], main[:, 7], main[:, 8]
        r_repeated = main[:, 0]
        r_wide = squares
        p_keys = main[:, 9:13]
        bias_fox = main[:, 13:16].rearrange("p a s -> p (a s)")
        f_repeated, f_row = bias_fox[:, 0:S], bias_fox[0:H, 0:S]
        bias_at = [P * b * (b + 1) // 2 for b in range(TB + 1)]
        logits = [side[:, 0], side[:, 1]]
        probs = [side[:, 2], side[:, 3]]
        x_slot, x_feat, x_sq = [side[:, 1], side[:, 0]], side[:, 2], side[:, 3]
        fin, stage = [side[:, 0], side[:, 1]], [side[:, 2], side[:, 3]]
        gate_d, gate_f, part_d, part_f = (side[:, j] for j in (1, 2, 3, 0))
        relu_in, relu_sq = side[:, 0], side[:, 1]
        param_rows, f_feat, tri = side[:, 0, 0:P], side[:, 1], side[:, 2]
        q_gain = [gains[:, 0:1], gains[:, 1:2]]
        k_gain = [cols[:, 68:69], cols[:, 66:67]]
        o_gain = gains[:, 2:3]
        lam_col = lam[:, 4:5]

        jobs = [ctx.enter_context(nc.psum_tensor(f"job{i}", [P, S], F32)) for i in range(2)]
        scores = [ctx.enter_context(nc.psum_tensor(f"scores{i}", [P, S], F32)) for i in range(2)]
        turned = ctx.enter_context(nc.psum_tensor("turned", [P, S], F32))
        wide = ctx.enter_context(nc.psum_tensor("wide", [P, S], F32))
        stats = ctx.enter_context(nc.psum_tensor("stats", [P, S], F32))
        heads_out = ctx.enter_context(nc.psum_tensor("heads_out", [P, S], F32))
        turn_banks = [scores[0], scores[1], turned, wide, heads_out, jobs[1]]
        TURNS = len(turn_banks)

        raw_loaded = [sem(f"raw_loaded{i}") for i in range(RAWS)]
        x_loaded = [sem(f"x_loaded{i}") for i in range(JU)]
        xr_loaded = [sem(f"xr_loaded{i}") for i in range(2)]
        out_stored = [sem(f"out_stored{i}") for i in range(2)]
        (hi_ready, split_ready, unit_used) = map(
            sem, ("hi_ready split_ready unit_used").split())
        (rows_cleared, params_loaded, small_loaded, bforget_loaded, ident_ready, consts_ready,
         tri_ready, dist_ready, table_loaded, cols_turned, cols_ready, small_turned, small_ready,
         gains_ready, lam_product, lam_sums, lam_exps, lam_step) = map(
            sem, ("rows_cleared params_loaded small_loaded bforget_loaded ident_ready consts_ready tri_ready "
                  "dist_ready table_loaded cols_turned cols_ready small_turned small_ready gains_ready "
                  "lam_product lam_sums lam_exps lam_step").split())
        (x_summed, x_stepped, x_newton, x_r_ready, x_turned, h_hi, h_ready) = map(
            sem, ("x_summed x_stepped x_newton x_r_ready x_turned h_hi h_ready").split())
        (f_copied, f_turned, f_logit, f_neg, f_exp, f_one, f_ln, f_ready, f_summed, f_row_ready, f_back,
         neg_f_ready) = map(
            sem, ("f_copied f_turned f_logit f_neg f_exp f_one f_ln f_ready f_summed f_row_ready f_back "
                  "neg_f_ready").split())
        (sq_ready, taken, stat_ready, squares_summed, eps_ready, newton, r_ready, wide_ready, norm_ready) = map(
            sem, ("sq_ready taken stat_ready squares_summed eps_ready newton r_ready wide_ready norm_ready").split())
        (qk_hi, qk_split, scores_ready, logits_ready, exp_ready, inv_ready, second_scaled, probs_ready, probs_turned,
         p_keys_ready, v_copied, v_turned, v_ready, pv_ready, o_copied, o_hi, o_ready, f_by_tokens,
         f_wide, bias_open, bias_ready) = map(
            sem, ("qk_hi qk_split scores_ready logits_ready exp_ready inv_ready second_scaled probs_ready probs_turned "
                  "p_keys_ready v_copied v_turned v_ready pv_ready o_copied o_hi o_ready f_by_tokens f_wide "
                  "bias_open bias_ready").split())
        (r_copied, r_row_wide, r_row_ready, gate_scaled, gate_exp, gate_one, gate_ready, parts_ready,
         merged_ready, m_hi, m_ready, m_ready_too, sum_cleared) = map(
            sem, ("r_copied r_row_wide r_row_ready gate_scaled gate_exp gate_one gate_ready parts_ready "
                  "merged_ready m_hi m_ready m_ready_too sum_cleared").split())
        (xr_turned, xr_ready, x2_ready, x2_sq, x2_hi, x2_lo, sum_ready, rms_ready) = map(
            sem, ("xr_turned xr_ready x2_ready x2_sq x2_hi x2_lo sum_ready rms_ready").split())
        (up_scaled, up_squared, up_hi, up_ready, down_added, fin_turned, stage_ready) = map(
            sem, ("up_scaled up_squared up_hi up_ready down_added fin_turned stage_ready").split())

        def head_hooks(step, u, i, work):
            half = HU // 2
            if not (isinstance(i, int) and i == 0):
                before = work.then(-HU, -HJ)
                step(0, i - 1, u + HU, before)
                step(1, i - 1, u + half, before.then(half, HJ // 2))
            if not (isinstance(i, int) and i == H):
                step(0, i, u, work)
                step(1, i, u - half, work.then(half, HJ // 2))

        block = ctx.enter_context(nc.Block())

        @block.sync
        def _(sp):
            def load_half(work, half, source):
                slot = (work.unit // 2 + half) % RAWS
                at_least(sp, split_ready, work.units_done(2 * half) - 2 * RAWS + 2)
                sp.dma_start(raw[:, slot], source).then_inc(raw_loaded[slot], 16)

            def load_job(work, weights, col, halves=2):
                w = weights[0].rearrange("(k p) c -> p k c", p=P)
                for half in range(halves):
                    k = 2 * KU * half
                    load_half(work, half, w[:, k:k + 2 * KU, bass.ds(col, P)])

            w = w_in[0].rearrange("(k p) c -> p k c", p=P)
            for quarter in range(JU):
                features = slice(KU * P * quarter, KU * P * (quarter + 1))
                for b in range(TB):
                    sp.dma_start(x_tok[:, b, features], xt[:, b, features]).then_inc(x_loaded[quarter], 16)
                if quarter % 2 == 1:
                    k = KU * (quarter - 1)
                    load_half(FORGET, quarter // 2, w[:, k:k + 2 * KU, w_in.shape[2] - P:])

            def head_loads(work, i, first_job=0):
                for j in range(first_job, HJ):
                    load_job(work.then(j * JU, j), w_in, i * P + j * WD)

            load_job(HEADS, w_in, 0)
            sp.wait_ge(rows_cleared, 1)
            for r, c, vector in ((64, 0, subln_diff), (65, 0, qnorm_fox), (66, 0, knorm_fox),
                                 (67, 0, qnorm_diff), (67, 64, qnorm_diff), (68, 0, knorm_diff),
                                 (68, 64, knorm_diff), (69, 0, lambda_q1), (69, 64, lambda_q2),
                                 (70, 0, lambda_k1), (70, 64, lambda_k2)):
                sp.dma_start(side[r:r + 1, 0, c:c + vector.shape[1]], vector).then_inc(small_loaded, 16)
            sp.dma_start(bforget[:, :], b_forget[0:1, :].broadcast_to([P, NF])).then_inc(bforget_loaded, 16)
            head_loads(HEADS, 0, first_job=1)
            with sp.Fori(1, H) as i:
                head_loads(Work(HEADS.unit, HEADS.job, i, HU, HJ), i)

            def merge_loads(work, m):
                load_job(work, w_gate, m * P)
                load_job(work.then(JU), w_gate, m * P + D)
                load_job(work.then(2 * JU, 2), w_branch_diff, m * P, halves=1)
                load_job(work.then(2 * JU + BU, 3), w_branch_fox, m * P, halves=1)

            with sp.Fori(0, DT // 2) as i:
                work = Work(MERGE.unit, MERGE.job, i, 2 * MU, 2 * MJ)
                for j in range(2):
                    merge_loads(work.then(j * MU, j * MJ), i * 2 + j)

            def load_residual(j, m):
                at_least(sp, xr_turned, m - 1)
                sp.dma_start(x_slot[j].rearrange("p (b f) -> p b f", b=TB),
                             xt[:, :, bass.ds(m * P, P)]).then_inc(xr_loaded[j], 16)

            load_job(PROJ, w_out, 0)
            load_job(PROJ.then(JU), w_out, P)
            sp.wait_ge(parts_ready, 2 * DT - 1)
            load_residual(0, 0)
            sp.wait_ge(merged_ready, DT)
            load_residual(1, 1)
            with sp.Fori(1, DT // 2) as i:
                work = Work(PROJ.unit, PROJ.job, i, 2 * JU, 2)
                for j in range(2):
                    load_job(work.then(j * JU), w_out, i * (2 * P) + j * P)
                    load_residual(j, i * 2 + j)

            with sp.Fori(0, CH) as c:
                with sp.Fori(0, DT // 2) as i:
                    work = Work(MLP.unit, MLP.job, c * DT + i, 2 * JU, 2)
                    for j in range(2):
                        load_job(work.then(j * JU), w_mlp_up, c * D + i * (2 * P) + j * P)
                with sp.Fori(0, DT // 2) as i:
                    work = Work(MLP.unit + DT * JU, MLP.job + DT, c * DT + i, 2 * JU, 2)
                    for j in range(2):
                        for half in range(2):
                            src = w_mlp_down[0, bass.ds(c * D + half * 2 * KU * P, 2 * KU * P),
                                             bass.ds(i * (2 * P) + j * P, P)]
                            load_half(work.then(j * JU), half, src.rearrange("(k p) c -> p k c", p=P))

        @block.gpsimd
        def _(pool):
            pool.memset(param_rows, 0.0).then_inc(rows_cleared, 1)
            pool.memset(ident[:, :], 0.0).then_inc(consts_ready, 1)
            pool.memset(ones[:, :], 1.0).then_inc(consts_ready, 1)
            pool.memset(causal[:, :], 0.0).then_inc(consts_ready, 1)
            pool.memset(halves[:, :], 1.0).then_inc(consts_ready, 1)
            pool.memset(tri, 1.0).then_inc(consts_ready, 1)
            pool.memset(one_half[:, :], 0.5).then_inc(consts_ready, 1)
            pool.wait_ge(consts_ready, 6)
            pool.affine_select(out=ident[:, :], in_=ident[:, :], compare_op=ALU.not_equal, fill=1.0,
                               base=0, pattern=[[-1, P]], channel_multiplier=1).then_inc(ident_ready, 1)
            pool.affine_select(out=halves[:, 0:1], in_=halves[:, 0:1], compare_op=ALU.is_ge, fill=0.0,
                               base=63, pattern=[[0, 1]], channel_multiplier=-1).then_inc(consts_ready, 1)
            pool.affine_select(out=halves[:, 1:2], in_=halves[:, 1:2], compare_op=ALU.is_ge, fill=0.0,
                               base=-64, pattern=[[0, 1]], channel_multiplier=1).then_inc(consts_ready, 1)
            pool.affine_select(out=causal[:, :], in_=causal[:, :], compare_op=ALU.is_ge, fill=MASKED,
                               base=0, pattern=[[-1, P]], channel_multiplier=1).then_inc(consts_ready, 1)
            pool.affine_select(out=tri, in_=tri, compare_op=ALU.is_ge, fill=0.0,
                               base=0, pattern=[[1, S]], channel_multiplier=-1).then_inc(tri_ready, 1)
            pool.iota(spare[:, :], [[-1, S]], base=S - P, channel_multiplier=1,
                      allow_small_or_imprecise_dtypes=True).then_inc(dist_ready, 1)
            pool.wait_ge(dist_ready, 1)
            pool.tensor_scalar(side[:, 3], spare[:, :], 0.0, 1.0, ALU.max, ALU.mult).then_inc(dist_ready, 1)
            pool.tensor_scalar(spare[:, :], spare[:, :], -0.5, 0.0, ALU.mult, ALU.add).then_inc(dist_ready, 1)
            pool.wait_ge(dist_ready, 3)
            pool.tensor_tensor(spare[:, :], spare[:, :], side[:, 3], ALU.add).then_inc(dist_ready, 1)
            pool.wait_ge(dist_ready, 4)
            pool.memset(spare[0:64, S - 64:S], MASKED * 2 ** H).then_inc(dist_ready, 1)
            with pool.Fori(0, H) as i:
                pool.wait_ge(logits_ready, i * (2 * TB) + TB)
                pool.wait_ge(dist_ready, i + 5)
                pool.wait_ge(consts_ready, 9)
                pool.tensor_tensor(spare[:, :], spare[:, :], one_half[:, :].broadcast_to([P, S]),
                                   ALU.mult).then_inc(dist_ready, 1)
                pool.wait_ge(bias_open, i * TB + TB)
                for b in range(TB):
                    diagonal = bias_fox[:, bias_at[b + 1] - P:bias_at[b + 1]]
                    pool.tensor_tensor(diagonal, diagonal, causal[:, :], ALU.add).then_inc(bias_ready, 1)
            pool.wait_ge(gate_scaled, 2 * DT)
            pool.memset(spare[:, :], 0.0).then_inc(sum_cleared, 1)
            for k in range(KU - 1, DT, KU):
                pool.wait_ge(m_hi, k + 1)
                pool.tensor_tensor(a_lo[:, k], main[:, k], a_hi[:, k].bitcast(F32),
                                   ALU.subtract).then_inc(m_ready_too, 1)

        @block.scalar
        def _(act):
            def round_unit(work, n):
                u = work.unit + n
                if not work.upt and u >= ALL_UNITS:
                    return
                slot, part = u // 2 % RAWS, KU * (u % 2)
                act.wait_ge(raw_loaded[slot], work.loads(n))
                at_least(act, unit_used, work.units_done(n + 1) - SPLITS)
                nc.scalar.activation(w_hi[:, u % SPLITS], raw[:, slot, part:part + KU],
                                     ACT.Copy).then_inc(hi_ready, 1)

            def take_for_norm(n, source, gain):
                at_least(act, norm_ready, n)
                nc.scalar.activation(squares, source[:, :], ACT.Square).then_inc(sq_ready, 1)
                nc.scalar.activation(scaled, source[:, :], ACT.Copy, scale=gain).then_inc(taken, 1)

            def head_step(kind, i, t, work):
                if t == 3 * JU:
                    values = work.then(2 * JU, 2)
                    act.wait_ge(unit_used, values.units_done(JU))
                    at_least(act, v_turned, i * 2 + kind)
                    if kind == 0:
                        at_least(act, o_ready, i * 2 - 1)
                    nc.scalar.activation(v_feat, jobs[values.bank()][:, :], ACT.Copy).then_inc(v_copied, 1)
                if t == 11 and kind == 1:
                    act.wait_ge(f_wide, i + 1)
                    for b in range(TB):
                        nc.scalar.activation(bias_fox[:, bias_at[b]:bias_at[b + 1]], scores[1][:, 0:P * (b + 1)],
                                             ACT.Identity, scale=-1.0,
                                             bias=neg_f[:, b, bass.ds(i, 1)]).then_inc(bias_open, 1)
                for b, when in enumerate(SOFTMAX_STEPS):
                    if t == when:
                        block_no = i * (2 * TB) + TB * kind + b
                        act.wait_ge(logits_ready, block_no + 1)
                        for m in range(2 - kind):
                            e = nc.scalar.activation(logits[m][:, 0:P * (b + 1)], logits[m][:, 0:P * (b + 1)],
                                                     ACT.Exp, scale=-1.0, bias=row_min[:, m:m + 1],
                                                     accum_out=row_sum[:, m:m + 1])
                        e.then_inc(exp_ready, 1)
                if kind == 1 and t == 22:
                    act.wait_ge(pv_ready, i * 2 + 2)
                    nc.scalar.activation(logits[0], heads_out[:, :], ACT.Copy).then_inc(o_copied, 1)
                    act.wait_ge(o_copied, i + 1)
                    nc.scalar.activation(tile(b_hi, i + H), logits[0], ACT.Copy).then_inc(o_hi, 1)

            def norm_step(kind, i, t, work):
                n = i * 5 + 2 * kind
                for which, gain in enumerate((q_gain[kind], k_gain[kind])):
                    if t == NORM_STEPS[which]:
                        act.wait_ge(unit_used, work.units_done((which + 1) * JU))
                        take_for_norm(n + which, jobs[work.then(0, which).bank()], gain)
                for which in range(2 if kind == 0 else 0):
                    if t == NORM_STEPS[which] + NORM_LENGTH:
                        act.wait_ge(norm_ready, n + which + 1)
                        for m in range(2):
                            for half in (maps[m],) if which == 0 else maps:
                                last = nc.scalar.activation((q_pair, k_pair)[which][m][half], qk_normed[maps[m]],
                                                            ACT.Copy)
                        last.then_inc(qk_hi, 1)
                if kind == 0 and t == NORM_STEPS[2]:
                    act.wait_ge(pv_ready, i * 2 + 1)
                    take_for_norm(n + 4, heads_out, o_gain)
                if kind == 0 and t == NORM_STEPS[2] + NORM_LENGTH:
                    act.wait_ge(norm_ready, n + 5)
                    nc.scalar.activation(tile(b_hi, i), v_feat, ACT.Copy).then_inc(o_hi, 1)

            act.wait_ge(rows_cleared, 1)
            for r, (vector, n) in enumerate(((norm_mix, DT), (norm_mlp, DT), (b_gate, 2 * DT))):
                r = (0, DT, 2 * DT)[r]
                act.dma_start(side[r:r + n, 0, 0:P], vector.rearrange("a (r p) -> (a r) p", p=P)
                              ).then_inc(params_loaded, 16)

            def sum_x(b, e):
                act.wait_ge(x_loaded[2 * e], 16 * TB)
                act.wait_ge(x_loaded[2 * e + 1], 16 * TB)
                nc.scalar.activation(b_hi[:, 4 * b + 2 * e:4 * b + 2 * e + 2].rearrange("p a s -> p (a s)"),
                                     x_tok[:, b, D // 2 * e:D // 2 * (e + 1)], ACT.Square,
                                     accum_out=x_sums[:, 2 * b + e:2 * b + e + 1]).then_inc(x_summed, 1)

            def round_h(tiles):
                for k in tiles:
                    act.wait_ge(x_turned, k + 1)
                    nc.scalar.activation(a_hi[:, k], turn_banks[k % TURNS][:, :], ACT.Copy,
                                         scale=cols[:, k:k + 1]).then_inc(h_hi, 1)

            act.wait_ge(consts_ready, 2)
            nc.scalar.activation(x_sums[:, 0:1], ones[:, 0:1], ACT.Square).then_inc(table_loaded, 1)
            act.wait_ge(table_loaded, 1)
            act.wait_ge(cols_ready, 1)
            round_h(range(0, KU))
            round_unit(FORGET, 0)
            round_unit(FORGET, 1)
            sum_x(0, 0)
            round_h(range(KU, 2 * KU))
            sum_x(1, 0)
            round_h(range(2 * KU, 3 * KU))
            round_unit(FORGET, 2)
            round_unit(FORGET, 3)
            sum_x(2, 0)
            round_h(range(3 * KU, DT))
            for n in range(JU, JU + LEAD):
                round_unit(FORGET, n)
            sum_x(3, 0)
            for b in range(TB):
                sum_x(b, 1)
            act.wait_ge(unit_used, FORGET.units_done(JU))
            nc.scalar.activation(f_feat, jobs[FORGET.bank()][:, :], ACT.Copy).then_inc(f_copied, 1)

            def heads_turn(i, work):
                for u in range(HU):
                    round_unit(work, u + LEAD)
                    if isinstance(i, int) and i == 0 and u == 2:
                        act.wait_ge(lam_sums, 1)
                        nc.scalar.activation(lam[:, 2:4], stats[:, 0:2], ACT.Exp).then_inc(lam_exps, 1)
                        act.wait_ge(f_neg, 1)
                        nc.scalar.activation(lf_t[:, 2], lf_t[:, 1], ACT.Exp).then_inc(f_exp, 1)
                        act.wait_ge(f_one, 1)
                        nc.scalar.activation(lf_t[:, 1], lf_t[:, 2], ACT.Ln).then_inc(f_ln, 1)
                    head_hooks(norm_step, u, i, work)
                    head_hooks(head_step, u, i, work)

            heads_turn(0, HEADS)
            with act.Fori(1, H) as i:
                heads_turn(i, Work(HEADS.unit, HEADS.job, i, HU, HJ))

            def merge(m, work, last=False):
                for u in range(MU):
                    round_unit(work, u + LEAD)
                    if isinstance(m, int) and m == 0:
                        head_hooks(norm_step, u, H, work)
                        head_hooks(head_step, u, H, work)
                    if isinstance(m, int) and m == 0 and u == 3:
                        act.wait_ge(r_row_wide, 1)
                        act.wait_ge(dist_ready, 5 + H)
                        nc.scalar.activation(spare[:, :], heads_out[:, :], ACT.Copy).then_inc(r_row_ready, 1)
                    for g, gate in enumerate((gate_d, gate_f)):
                        if u == (g + 1) * JU:
                            act.wait_ge(gate_scaled, m * 2 + g + 1)
                            nc.scalar.activation(gate, gate, ACT.Exp, scale=-1.0,
                                                 bias=neg_bgate[:, bass.ds(m + g * DT, 1)]).then_inc(gate_exp, 1)
                    if last and u >= 2 * JU:
                        for k in range((u - 2 * JU) * 3, (u - 2 * JU) * 3 + 3):
                            round_merged(k)

            def round_merged(k):
                act.wait_ge(unit_used, MERGE.unit + (DT - 1) * MU + 2 * JU)
                act.wait_ge(merged_ready, k + 1)
                nc.scalar.activation(a_hi[:, k], main[:, k], ACT.Copy).then_inc(m_hi, 1)

            merge(0, MERGE)
            with act.Fori(0, DT // 2 - 1) as i:
                work = Work(MERGE.unit + MU, MERGE.job + MJ, i, 2 * MU, 2 * MJ)
                merge(i * 2 + 1, work)
                merge(i * 2 + 2, work.then(MU, MJ))
            merge(DT - 1, MERGE.then((DT - 1) * MU, (DT - 1) * MJ), last=True)
            for k in range(2 * BU * 3, DT):
                round_merged(k)

            def projected(m, work):
                for u in range(JU):
                    round_unit(work, u + LEAD)
                    if u == 2:
                        act.wait_ge(xr_turned, m + 1)
                        at_least(act, sum_ready, m)
                        nc.scalar.activation(x_feat, turned[:, :], ACT.Copy).then_inc(xr_ready, 1)
                act.wait_ge(x2_ready, m + 1)
                at_least(act, sum_ready, m)
                nc.scalar.activation(x_sq, tile(main, m), ACT.Square).then_inc(x2_sq, 1)
                nc.scalar.activation(tile(b_hi, m), tile(main, m), ACT.Copy,
                                     scale=cols[:, bass.ds(m + DT, 1)]).then_inc(x2_hi, 1)

            for j in range(2):
                projected(j, PROJ.then(j * JU, j))
            with act.Fori(1, DT // 2) as i:
                work = Work(PROJ.unit, PROJ.job, i, 2 * JU, 2)
                for j in range(2):
                    projected(i * 2 + j, work.then(j * JU, j))

            def up(m, c, work, first=False):
                for u in range(JU):
                    round_unit(work, u + LEAD)
                if first:
                    act.wait_ge(wide_ready, 5 * H + 1)
                    nc.scalar.activation(spare[:, :], wide[:, :], ACT.Copy).then_inc(rms_ready, 1)
                act.wait_ge(up_squared, c * DT + m + 1)
                nc.scalar.activation(tile(a_hi, m), relu_sq, ACT.Copy).then_inc(up_hi, 1)

            def ups(c, first_turn):
                with act.Fori(first_turn, DT // 2) as i:
                    work = Work(MLP.unit, MLP.job, c * DT + i, 2 * JU, 2)
                    for j in range(2):
                        up(i * 2 + j, c, work.then(j * JU, j))

            def down_rounds(c):
                with act.Fori(0, DT // 2) as i:
                    work = Work(MLP.unit + DT * JU, MLP.job + DT, c * DT + i, 2 * JU, 2)
                    for u in range(2 * JU):
                        round_unit(work, u + LEAD)

            for j in range(2):
                up(j, 0, MLP.then(j * JU, j), first=j == 0)
            ups(0, 1)
            down_rounds(0)
            with act.Fori(1, CH - 1) as c:
                ups(c, 0)
                down_rounds(c)
            ups(CH - 1, 0)

            def store(j, m):
                act.wait_ge(fin_turned, m + 1)
                if j == 0:
                    at_least(act, out_stored[0], m * 8)
                else:
                    at_least(act, out_stored[1], m * 8 - 8)
                nc.scalar.activation(stage[j], (turned, wide)[j][:, :], ACT.Copy).then_inc(stage_ready, 1)
                act.wait_ge(stage_ready, m + 1)
                act.dma_start(outt[:, :, bass.ds(m * P, P)], stage[j].rearrange("p (b f) -> p b f", b=TB)
                              ).then_inc(out_stored[j], 16)

            LAST = MLP.then((CH - 1) * CU + DT * JU, (CH - 1) * CJ + DT)

            def last_down(m, work, j):
                for u in range(JU):
                    round_unit(work, u + LEAD)
                    if u == 2 and not (isinstance(m, int) and m == 0):
                        store(1 - j, m - 1)

            last_down(0, LAST, 0)
            for m in (1, 2):
                last_down(m, LAST.then(m * JU, m), m % 2)
            with act.Fori(1, DT // 2 - 1) as i:
                work = Work(LAST.unit + JU, LAST.job + 1, i, 2 * JU, 2)
                last_down(i * 2 + 1, work, 1)
                last_down(i * 2 + 2, work.then(JU), 0)
            last_down(DT - 1, LAST.then((DT - 1) * JU, DT - 1), 1)
            store(1, DT - 1)
            for j in range(2):
                act.wait_ge(out_stored[j], 16 * (DT // 2))

        @block.vector
        def _(dve):
            def split_unit(work, n):
                u = work.unit + n
                if not work.upt and u >= ALL_UNITS:
                    return
                slot, part = u // 2 % RAWS, KU * (u % 2)
                dve.wait_ge(hi_ready, work.units_done(n + 1))
                nc.vector.tensor_tensor(w_lo[:, u % SPLITS], raw[:, slot, part:part + KU],
                                        w_hi[:, u % SPLITS].bitcast(F32), ALU.subtract).then_inc(split_ready, 1)

            def rsqrt(v, ready, count):
                bits = v[:, 5].bitcast(I32)
                steps = 0

                def step(instruction, wait=True):
                    nonlocal steps
                    steps += 1
                    instruction.then_inc(ready, 1)
                    if wait:
                        dve.wait_ge(ready, count + steps)

                step(nc.vector.tensor_scalar(v[:, 1], v[:, 0], -0.5, None, ALU.mult), wait=False)
                step(nc.vector.tensor_scalar(bits, v[:, 0].bitcast(I32), 1, None, ALU.logical_shift_right))
                step(nc.vector.tensor_scalar(bits, bits, -1, RSQRT_MAGIC, ALU.mult, ALU.add))
                for last in (False, False, True):
                    step(nc.vector.tensor_tensor(v[:, 2], v[:, 5], v[:, 5], ALU.mult))
                    step(nc.vector.tensor_tensor(v[:, 3], v[:, 2], v[:, 1], ALU.mult))
                    if last:
                        step(nc.vector.tensor_scalar(v[:, 4], v[:, 3], 1.5, None, ALU.add))
                    else:
                        step(nc.vector.scalar_tensor_tensor(v[:, 5], v[:, 3], 1.5, v[:, 5], ALU.add, ALU.mult))
                assert steps == RSQRT_STEPS

            def invert_rms(n, into, width, count=None, scaled_x=False):
                dve.wait_ge(stat_ready, n + 1)
                groups = S // width
                nc.vector.tensor_reduce(stat[:, 6, 0:groups], stats[:, :].rearrange("p (a c) -> p a c", c=width),
                                        mybir.AxisListType.X, ALU.add).then_inc(squares_summed, 1)
                dve.wait_ge(squares_summed, n + 1)
                a, sums, eps = stat[:, 0], stat[:, 6, 0:groups], x_eps[:, :]
                if groups == TB:
                    sums = sums.unsqueeze(2).broadcast_to([P, TB, 2])
                    a, eps = (v.rearrange("p (b e) -> p b e", e=2) for v in (a, eps))
                if scaled_x:
                    nc.vector.scalar_tensor_tensor(a, sums, 1.0 / width, eps, ALU.mult, ALU.add).then_inc(eps_ready, 1)
                else:
                    nc.vector.tensor_scalar(a, sums, 1.0 / (count or width), EPS, ALU.mult,
                                            ALU.add).then_inc(eps_ready, 1)
                dve.wait_ge(eps_ready, n + 1)
                rsqrt(stat, newton, n * RSQRT_STEPS)
                nc.vector.tensor_tensor(into.rearrange("p (a c) -> p a c", c=64),
                                        stat[:, 5].unsqueeze(2).broadcast_to([P, 8, 64]),
                                        stat[:, 4].unsqueeze(2).broadcast_to([P, 8, 64]),
                                        ALU.mult).then_inc(r_ready, 1)

            def scale_by_rms(n, result):
                dve.wait_ge(wide_ready, n + 1)
                dve.wait_ge(taken, n + 1)
                nc.vector.tensor_tensor(result, scaled, wide[:, :], ALU.mult).then_inc(norm_ready, 1)

            def take_logits(kind, i, b):
                block_no = i * (2 * TB) + TB * kind + b
                n = P * (b + 1)
                if kind == 0:
                    dve.wait_ge(dist_ready, i + 5)
                else:
                    dve.wait_ge(bias_ready, i * TB + b + 1)
                at_least(dve, probs_ready, block_no)
                dve.wait_ge(scores_ready, block_no + 1)
                nc.vector.memset(pause[:, :], 0.0)
                for m in range(2 - kind):
                    bias = spare[:, S - n:S] if kind == 0 else bias_fox[:, bias_at[b]:bias_at[b + 1]]
                    r = nc.vector.tensor_tensor_reduce(out=logits[m][:, 0:n], in0=scores[m][:, 0:n], in1=bias,
                                                       scale=1.0, scalar=3e38, op0=ALU.add, op1=ALU.min,
                                                       accum_out=row_min[:, m:m + 1])
                r.then_inc(logits_ready, 1)

            def take_probs(kind, i, b):
                block_no = i * (2 * TB) + TB * kind + b
                n = P * (b + 1)
                dve.wait_ge(exp_ready, block_no + 1)
                at_least(dve, probs_turned, block_no - 1)
                count = 2 - kind
                nc.vector.reciprocal(row_inv[:, 0:count], row_sum[:, 0:count]).then_inc(inv_ready, 1)
                dve.wait_ge(inv_ready, block_no + 1)
                if kind == 0:
                    nc.vector.tensor_scalar(logits[1][:, 0:n], logits[1][:, 0:n], row_inv[:, 1:2], lam_col,
                                            ALU.mult, ALU.mult).then_inc(second_scaled, 1)
                    dve.wait_ge(second_scaled, i * TB + b + 1)
                    nc.vector.scalar_tensor_tensor(probs[b % 2][:, 0:n], logits[0][:, 0:n], row_inv[:, 0:1],
                                                   logits[1][:, 0:n], ALU.mult, ALU.subtract).then_inc(probs_ready, 1)
                else:
                    nc.vector.tensor_scalar(probs[b % 2][:, 0:n], logits[0][:, 0:n], row_inv[:, 0:1], None,
                                            ALU.mult).then_inc(probs_ready, 1)

            def keep_turned(kind, i, b):
                block_no = i * (2 * TB) + TB * kind + b
                dve.wait_ge(probs_turned, block_no + 1)
                at_least(dve, pv_ready, i * 2 + kind)
                nc.vector.tensor_copy(p_keys[:, 0:b + 1, P * b:P * (b + 1)],
                                      turned[:, 0:P * (b + 1)].rearrange("p (j q) -> p j q", q=P)
                                      ).then_inc(p_keys_ready, 1)

            def head_step(kind, i, t, work):
                if kind == 1 and t == 8:
                    dve.wait_ge(neg_f_ready, 1)
                    nc.vector.tensor_copy(f_repeated.rearrange("p (b c) -> p b c", b=TB),
                                          neg_f[:, :, bass.ds(i, 1)].broadcast_to([P, TB, P])
                                          ).then_inc(f_by_tokens, 1)
                for b, when in enumerate(SOFTMAX_STEPS):
                    if t == when + 1:
                        take_probs(kind, i, b)
                for b, when in enumerate(SOFTMAX_STEPS):
                    if t == when:
                        take_logits(kind, i, b)
                    if t == TURN_STEPS[kind][b]:
                        keep_turned(kind, i, b)
                if t == 14:
                    dve.wait_ge(v_turned, i * 2 + kind + 1)
                    nc.vector.tensor_tensor(v_tok[kind].rearrange("p (b d) -> p b d", b=TB),
                                            turned[:, :].rearrange("p (b d) -> p b d", b=TB),
                                            x_r1.broadcast_to([P, TB, P]), ALU.mult).then_inc(v_ready, 1)
                if kind == 1 and t == 23:
                    dve.wait_ge(o_hi, i * 2 + 2)
                    nc.vector.tensor_tensor(tile(b_lo, i + H), logits[0], tile(b_hi, i + H).bitcast(F32),
                                            ALU.subtract).then_inc(o_ready, 1)
                if kind == 0 and t == NORM_STEPS[2] + NORM_LENGTH + 1:
                    dve.wait_ge(o_hi, i * 2 + 1)
                    nc.vector.tensor_tensor(tile(b_lo, i), v_feat, tile(b_hi, i).bitcast(F32),
                                            ALU.subtract).then_inc(o_ready, 1)

            def scale_step(kind, i, t, work):
                n = i * 5 + 2 * kind
                for which, result in enumerate((qk_normed, qk_normed) if kind == 0 else (qn_fox, kn_fox)):
                    if t == NORM_STEPS[which] + NORM_LENGTH:
                        scale_by_rms(n + which, result)
                if kind == 0 and t == NORM_STEPS[2] + NORM_LENGTH:
                    scale_by_rms(n + 4, v_feat)

            def split_step(kind, i, t, work):
                for which in range(2 if kind == 0 else 0):
                    if t == NORM_STEPS[which] + NORM_LENGTH + 1:
                        dve.wait_ge(qk_hi, i * 2 + which + 1)
                        for m in range(2):
                            hi = (q_pair, k_pair)[which][m][maps[m]].bitcast(F32)
                            lo = q_pair[m][maps[1 - m]] if which == 0 else k_lo[maps[m]]
                            last = nc.vector.tensor_tensor(lo, qk_normed[maps[m]], hi, ALU.subtract)
                        last.then_inc(qk_split, 1)

            def norm_step(kind, i, t, work):
                n = i * 5 + 2 * kind
                for which in range(2):
                    if t == NORM_STEPS[which] + 1 + kind * which:
                        invert_rms(n + which, r_wide, HD // (2 - kind), scaled_x=True)
                if kind == 0 and t == NORM_STEPS[2] + 1:
                    invert_rms(n + 4, r_wide, HD)

            dve.wait_ge(cols_turned, 1)
            nc.vector.tensor_copy(cols[:, 0:64], stats[:, 0:64]).then_inc(cols_ready, 1)
            dve.wait_ge(cols_ready, 1)

            def split_h(tiles):
                for k in tiles:
                    dve.wait_ge(h_hi, k + 1)
                    nc.vector.scalar_tensor_tensor(a_lo[:, k], turn_banks[k % TURNS][:, :], cols[:, k:k + 1],
                                                   a_hi[:, k].bitcast(F32), ALU.mult,
                                                   ALU.subtract).then_inc(h_ready, 1)

            split_h(range(0, KU))
            split_unit(FORGET, 0)
            split_unit(FORGET, 1)
            split_h(range(KU, 3 * KU))
            split_unit(FORGET, 2)
            split_unit(FORGET, 3)
            split_h(range(3 * KU, DT))
            for n in range(JU, JU + LEAD):
                split_unit(FORGET, n)
            dve.wait_ge(small_turned, 1)
            nc.vector.tensor_copy(cols[:, 64:P], stats[:, 64:P]).then_inc(small_ready, 1)
            dve.wait_ge(small_ready, 1)
            nc.vector.tensor_scalar(neg_bgate[:, :], cols[:, 32:64], -1.0, None, ALU.mult)
            nc.vector.tensor_scalar(gains[:, 0:1], cols[:, 67:68], -(HD // 2) ** -0.5, None, ALU.mult)
            nc.vector.tensor_scalar(gains[:, 1:2], cols[:, 65:66], -HD ** -0.5, None, ALU.mult)
            nc.vector.tensor_scalar(gains[:, 2:3], cols[:, 64:65], 1.0 - LAMBDA_INIT, None,
                                    ALU.mult).then_inc(gains_ready, 1)
            nc.vector.tensor_tensor(lam[:, 5:6], cols[:, 69:70], cols[:, 70:71], ALU.mult).then_inc(lam_step, 1)
            dve.wait_ge(lam_step, 1)
            dve.wait_ge(consts_ready, 8)
            nc.vector.tensor_scalar(lam[:, 0:2], halves[:, :], lam[:, 5:6], None, ALU.mult).then_inc(lam_product, 1)

            dve.wait_ge(x_summed, 2 * TB)
            pairs = x_sums[:, :].rearrange("p (b e) -> p b e", e=2)
            nc.vector.tensor_tensor(x_stat[:, 1], pairs[:, :, 0], pairs[:, :, 1], ALU.add).then_inc(x_stepped, 1)
            dve.wait_ge(x_stepped, 1)
            nc.vector.tensor_scalar(x_stat[:, 0], x_stat[:, 1], 1.0 / D, EPS, ALU.mult, ALU.add).then_inc(x_stepped, 1)
            dve.wait_ge(x_stepped, 2)
            rsqrt(x_stat, x_newton, 0)
            nc.vector.tensor_tensor(x_r[:, :].rearrange("p (b e) -> p b e", e=2),
                                    x_stat[:, 5].unsqueeze(2).broadcast_to([P, TB, 2]),
                                    x_stat[:, 4].unsqueeze(2).broadcast_to([P, TB, 2]), ALU.mult).then_inc(x_r_ready, 1)
            nc.vector.tensor_scalar(x_eps[:, :].rearrange("p (b e) -> p b e", e=2),
                                    x_stat[:, 0].unsqueeze(2).broadcast_to([P, TB, 2]), EPS, None,
                                    ALU.mult).then_inc(x_r_ready, 1)
            dve.wait_ge(x_r_ready, 2)

            def forget_logits():
                dve.wait_ge(f_turned, 1)
                dve.wait_ge(bforget_loaded, 16)
                z = heads_out[:, :].rearrange("p (b c) -> p b c", b=TB)[:, :, P - NF:P]
                nc.vector.tensor_tensor(lf_t[:, 1], z, x_r1.broadcast_to([P, TB, NF]), ALU.mult).then_inc(f_logit, 1)
                dve.wait_ge(f_logit, 1)
                nc.vector.tensor_tensor(lf_t[:, 0], lf_t[:, 1], bforget[:, :].unsqueeze(1).broadcast_to([P, TB, NF]),
                                        ALU.add).then_inc(f_logit, 1)
                dve.wait_ge(f_logit, 2)
                nc.vector.scalar_tensor_tensor(lf_t[:, 1], lf_t[:, 0], -1.0, lf_t[:, 0], ALU.mult,
                                               ALU.min).then_inc(f_neg, 1)
                dve.wait_ge(f_exp, 1)
                nc.vector.tensor_scalar(lf_t[:, 2], lf_t[:, 2], 1.0, None, ALU.add).then_inc(f_one, 1)
                dve.wait_ge(f_ln, 1)
                nc.vector.scalar_tensor_tensor(lf[:, :, :], lf_t[:, 0], 0.0, lf_t[:, 1], ALU.min,
                                               ALU.subtract).then_inc(f_ready, 1)

            def heads_turn(i, work):
                first = isinstance(i, int) and i == 0
                for u in range(HU):
                    head_hooks(scale_step, u, i, work)
                    head_hooks(head_step, u, i, work)
                    head_hooks(split_step, u, i, work)
                    split_unit(work, u + LEAD)
                    if first and u == 2:
                        dve.wait_ge(lam_exps, 1)
                        nc.vector.scalar_tensor_tensor(lam_col, lam[:, 2:3], LAMBDA_INIT, lam[:, 3:4], ALU.add,
                                                       ALU.subtract).then_inc(lam_step, 1)
                        forget_logits()
                    if first and u == 4:
                        dve.wait_ge(f_summed, 1)
                        nc.vector.tensor_copy(f_row, heads_out[0:H, :]).then_inc(f_row_ready, 1)
                    if first and u == 5:
                        dve.wait_ge(f_back, 1)
                        nc.vector.tensor_scalar(neg_f[:, :, :],
                                                heads_out[:, 0:TB * H].rearrange("p (b h) -> p b h", b=TB), -1.0, None,
                                                ALU.mult).then_inc(neg_f_ready, 1)
                    head_hooks(norm_step, u, i, work)

            heads_turn(0, HEADS)
            with dve.Fori(1, H) as i:
                heads_turn(i, Work(HEADS.unit, HEADS.job, i, HU, HJ))

            def merge(m, work, last=False):
                inverted, used = (JU + 1, MU - 1), (MU - 2, MU - 1)
                if not (isinstance(m, int) and m == 0):
                    inverted, used = (JU + 1, 2 * JU), (2 * JU + BU - 1, 2 * JU + 2 * BU - 1)
                for u in range(MU):
                    if isinstance(m, int) and m == 0:
                        head_hooks(scale_step, u, H, work)
                        head_hooks(head_step, u, H, work)
                    split_unit(work, u + LEAD)
                    if isinstance(m, int) and m == 0:
                        head_hooks(norm_step, u, H, work)
                    if isinstance(m, int) and m == 0 and u == 0:
                        nc.vector.tensor_copy(r_repeated.rearrange("p (a c) -> p a c", c=64),
                                              x_r[:, :].unsqueeze(2).broadcast_to([P, 2 * TB, 64])
                                              ).then_inc(r_copied, 1)
                    for g, gate in enumerate((gate_d, gate_f)):
                        if u == (g + 1) * JU:
                            dve.wait_ge(unit_used, work.units_done((g + 1) * JU))
                            dve.wait_ge(r_row_ready, 1)
                            if isinstance(m, int) and m == 0:
                                dve.wait_ge(probs_turned, 2 * TB * H - (0 if g else TB))
                            nc.vector.tensor_tensor(gate, jobs[work.then(0, g).bank()][:, :], spare[:, :],
                                                    ALU.mult).then_inc(gate_scaled, 1)
                        if u == inverted[g]:
                            dve.wait_ge(gate_exp, m * 2 + g + 1)
                            nc.vector.tensor_scalar(gate, gate, 1.0, None, ALU.add).then_inc(gate_one, 1)
                            dve.wait_ge(gate_one, m * 2 + g + 1)
                            nc.vector.reciprocal(gate, gate).then_inc(gate_ready, 1)
                    for g, gate, part in ((0, gate_d, part_d), (1, gate_f, part_f)):
                        if u == used[g]:
                            dve.wait_ge(gate_ready, m * 2 + g + 1)
                            dve.wait_ge(unit_used, work.units_done(2 * JU + (g + 1) * BU))
                            nc.vector.tensor_tensor(part, jobs[work.then(0, g).bank()][:, :], gate,
                                                    ALU.mult).then_inc(parts_ready, 1)
                    if last and u >= 2 * JU:
                        for k in range((u - 2 * JU) * 3, (u - 2 * JU) * 3 + 3):
                            split_merged(k)
                dve.wait_ge(parts_ready, m * 2 + 2)
                nc.vector.tensor_tensor(tile(main, m), part_d, part_f, ALU.add).then_inc(merged_ready, 1)

            def split_merged(k):
                if k % KU == KU - 1:
                    return
                dve.wait_ge(m_hi, k + 1)
                nc.vector.tensor_tensor(a_lo[:, k], main[:, k], a_hi[:, k].bitcast(F32),
                                        ALU.subtract).then_inc(m_ready, 1)

            merge(0, MERGE)
            with dve.Fori(0, DT // 2 - 1) as i:
                work = Work(MERGE.unit + MU, MERGE.job + MJ, i, 2 * MU, 2 * MJ)
                merge(i * 2 + 1, work)
                merge(i * 2 + 2, work.then(MU, MJ))
            merge(DT - 1, MERGE.then((DT - 1) * MU, (DT - 1) * MJ), last=True)
            for k in range(2 * BU * 3, DT):
                split_merged(k)

            def projected(m, work):
                for u in range(JU):
                    split_unit(work, u + LEAD)
                dve.wait_ge(unit_used, work.units_done(JU))
                dve.wait_ge(xr_ready, m + 1)
                nc.vector.tensor_tensor(tile(main, m), jobs[work.bank()][:, :], x_feat, ALU.add).then_inc(x2_ready, 1)
                dve.wait_ge(x2_sq, m + 1)
                dve.wait_ge(sum_cleared, 1)
                at_least(dve, sum_ready, m)
                nc.vector.tensor_tensor(spare[:, :], spare[:, :], x_sq, ALU.add).then_inc(sum_ready, 1)
                dve.wait_ge(x2_hi, m + 1)
                nc.vector.scalar_tensor_tensor(tile(b_lo, m), tile(main, m), cols[:, bass.ds(m + DT, 1)],
                                               tile(b_hi, m).bitcast(F32), ALU.mult, ALU.subtract).then_inc(x2_lo, 1)

            for j in range(2):
                projected(j, PROJ.then(j * JU, j))
            with dve.Fori(1, DT // 2) as i:
                work = Work(PROJ.unit, PROJ.job, i, 2 * JU, 2)
                for j in range(2):
                    projected(i * 2 + j, work.then(j * JU, j))

            def up(m, c, work, first=False):
                for u in range(JU):
                    split_unit(work, u + LEAD)
                    if first and u == 2:
                        invert_rms(5 * H, x_sq, P, count=D)
                n = c * DT + m + 1
                dve.wait_ge(unit_used, work.units_done(JU))
                dve.wait_ge(rms_ready, 1)
                nc.vector.tensor_tensor(relu_in, jobs[work.bank()][:, :], spare[:, :], ALU.mult).then_inc(up_scaled, 1)
                dve.wait_ge(up_scaled, n)
                nc.vector.scalar_tensor_tensor(relu_sq, relu_in, 0.0, relu_in, ALU.max,
                                               ALU.mult).then_inc(up_squared, 1)
                dve.wait_ge(up_hi, n)
                nc.vector.tensor_tensor(tile(a_lo, m), relu_sq, tile(a_hi, m).bitcast(F32),
                                        ALU.subtract).then_inc(up_ready, 1)

            def ups(c, first_turn):
                with dve.Fori(first_turn, DT // 2) as i:
                    work = Work(MLP.unit, MLP.job, c * DT + i, 2 * JU, 2)
                    for j in range(2):
                        up(i * 2 + j, c, work.then(j * JU, j))

            def downs(c):
                with dve.Fori(0, DT // 2) as i:
                    work = Work(MLP.unit + DT * JU, MLP.job + DT, c * DT + i, 2 * JU, 2)
                    for j in range(2):
                        for u in range(JU):
                            split_unit(work.then(j * JU), u + LEAD)
                        dve.wait_ge(unit_used, work.then(j * JU).units_done(JU))
                        at_least(dve, down_added, c * DT)
                        m = i * 2 + j
                        nc.vector.tensor_tensor(tile(main, m), jobs[work.then(0, j).bank()][:, :], tile(main, m),
                                                ALU.add).then_inc(down_added, 1)

            dve.wait_ge(x2_ready, DT)
            for j in range(2):
                up(j, 0, MLP.then(j * JU, j), first=j == 0)
            ups(0, 1)
            downs(0)
            with dve.Fori(1, CH - 1) as c:
                ups(c, 0)
                downs(c)
            ups(CH - 1, 0)
            dve.wait_ge(down_added, (CH - 1) * DT)

            LAST = MLP.then((CH - 1) * CU + DT * JU, (CH - 1) * CJ + DT)

            def last_down(m, work, j):
                for u in range(JU):
                    split_unit(work, u + LEAD)
                dve.wait_ge(unit_used, work.units_done(JU))
                at_least(dve, fin_turned, m - 1)
                nc.vector.tensor_tensor(fin[j], jobs[work.bank()][:, :], tile(main, m), ALU.add).then_inc(down_added, 1)

            last_down(0, LAST, 0)
            for m in (1, 2):
                last_down(m, LAST.then(m * JU, m), m % 2)
            with dve.Fori(1, DT // 2 - 1) as i:
                work = Work(LAST.unit + JU, LAST.job + 1, i, 2 * JU, 2)
                last_down(i * 2 + 1, work, 1)
                last_down(i * 2 + 2, work.then(JU), 0)
            last_down(DT - 1, LAST.then((DT - 1) * JU, DT - 1), 1)

        @block.tensor
        def _(pe):
            def job(work, act_hi, act_lo, first_tile=0, units=JU, before_unit=None):
                result = jobs[work.bank()]
                for n in range(units):
                    if before_unit is not None:
                        before_unit(n)
                    pe.wait_ge(split_ready, work.units_done(n + 1))
                    slot = (work.unit + n) % SPLITS
                    for k in range(KU):
                        f = first_tile + n * KU + k
                        nc.tensor.matmul(result[:, :], w_hi[:, slot, k], act_hi[:, f], start=(n == 0 and k == 0),
                                         stop=False)
                        nc.tensor.matmul(result[:, :], w_hi[:, slot, k], act_lo[:, f], start=False, stop=False)
                        done = nc.tensor.matmul(result[:, :], w_lo[:, slot, k], act_hi[:, f], start=False,
                                                stop=(n == units - 1 and k == KU - 1))
                    done.then_inc(unit_used, 1)

            def turn_squares(n, squared):
                at_least(pe, eps_ready, n)
                for b in range(TB):
                    last = nc.tensor.transpose(stats[:, P * b:P * (b + 1)], squared[:, P * b:P * (b + 1)],
                                               ident[:, :])
                last.then_inc(stat_ready, 1)

            def widen(n, repeated):
                pe.wait_ge(r_ready, n + 1)
                at_least(pe, norm_ready, n)
                for b in range(TB):
                    last = nc.tensor.transpose(wide[:, P * b:P * (b + 1)], repeated[:, P * b:P * (b + 1)],
                                               ident[:, :])
                last.then_inc(wide_ready, 1)

            def norm_steps(n, kind, t, first):
                if t == first + 1:
                    pe.wait_ge(sq_ready, n + 1)
                    turn_squares(n, squares)
                if t == first + NORM_LENGTH:
                    widen(n, r_wide)

            def take_scores(kind, i, b):
                block_no = i * (2 * TB) + TB * kind + b
                at_least(pe, logits_ready, block_no)
                n = P * (b + 1)
                queries = slice(P * b, n)
                if kind == 1:
                    last = nc.tensor.matmul(scores[0][:, 0:n], qn_fox[:, queries], kn_fox[:, 0:n], start=True,
                                            stop=True)
                wide_n = max(n, 2 * P)
                for m in range(2 - 2 * kind):
                    nc.tensor.matmul(scores[m][:, 0:wide_n], q_pair[m][:, queries], k_pair[m][:, 0:wide_n],
                                     start=True, stop=False)
                    last = nc.tensor.matmul(scores[m][:, 0:wide_n], q_pair[m][maps[m], queries],
                                            k_lo[maps[m], 0:wide_n], start=False, stop=True)
                last.then_inc(scores_ready, 1)

            def turn_probs(kind, i, b):
                block_no = i * (2 * TB) + TB * kind + b
                pe.wait_ge(probs_ready, block_no + 1)
                at_least(pe, p_keys_ready, block_no)
                pe.wait_ge(v_ready, i * 2 + kind + 1)
                for j in range(b + 1):
                    last = nc.tensor.transpose(turned[:, P * j:P * (j + 1)], probs[b % 2][:, P * j:P * (j + 1)],
                                               ident[:, :])
                last.then_inc(probs_turned, 1)

            def head_step(kind, i, t, work):
                n = i * 5 + 2 * kind
                for which in range(2):
                    norm_steps(n + which, kind, t, NORM_STEPS[which])
                if kind == 1 and t == 11:
                    pe.wait_ge(f_by_tokens, i + 1)
                    pe.wait_ge(logits_ready, i * (2 * TB) + TB)
                    for b in range(TB):
                        last = nc.tensor.transpose(scores[1][:, P * b:P * (b + 1)],
                                                   f_repeated[:, P * b:P * (b + 1)], ident[:, :])
                    last.then_inc(f_wide, 1)
                if t == 14:
                    pe.wait_ge(v_copied, i * 2 + kind + 1)
                    at_least(pe, p_keys_ready, i * (2 * TB) + TB * kind)
                    for b in range(TB):
                        last = nc.tensor.transpose(turned[:, P * b:P * (b + 1)], v_feat[:, P * b:P * (b + 1)],
                                                   ident[:, :])
                    last.then_inc(v_turned, 1)
                if t == SOFTMAX_STEPS[0]:
                    if kind == 0:
                        pe.wait_ge(qk_split, i * 2 + 2)
                    else:
                        pe.wait_ge(norm_ready, n + 2)
                for b, when in enumerate(SOFTMAX_STEPS):
                    if t == when:
                        take_scores(kind, i, b)
                for b, when in enumerate(TURN_STEPS[kind]):
                    if t == when:
                        turn_probs(kind, i, b)
                if t == PV_STEPS[kind]:
                    pe.wait_ge(p_keys_ready, i * (2 * TB) + TB * kind + TB)
                    if kind == 0:
                        at_least(pe, o_copied, i)
                    else:
                        pe.wait_ge(taken, i * 5 + 5)
                        if isinstance(i, int) and i == H - 1:
                            pe.wait_ge(r_row_ready, 1)
                    for j in range(TB):
                        last = nc.tensor.matmul(heads_out[:, P * j:S], v_tok[kind][:, P * j:P * (j + 1)],
                                                p_keys[:, j, P * j:S], start=(j == 0), stop=(j == TB - 1))
                    last.then_inc(pv_ready, 1)
                if kind == 0:
                    norm_steps(n + 4, 1, t, NORM_STEPS[2])

            pe.wait_ge(params_loaded, 16 * 3)
            pe.wait_ge(ident_ready, 1)
            nc.tensor.transpose(stats[:, 0:64], param_rows[0:64], ident[0:64, 0:64]).then_inc(cols_turned, 1)

            def turn_x(tiles):
                for k in tiles:
                    at_least(pe, h_ready, k - TURNS + 1)
                    pe.wait_ge(x_loaded[k // KU], 16 * TB)
                    for b in range(TB):
                        last = nc.tensor.transpose(turn_banks[k % TURNS][:, P * b:P * (b + 1)],
                                                   x_tok[:, b, P * k:P * (k + 1)], ident[:, :])
                    last.then_inc(x_turned, 1)

            turn_x(range(KU))

            def forget_unit(n):
                turn_x(range(KU * (n + 1), min(DT, KU * (n + 2))))
                pe.wait_ge(h_ready, KU * (n + 1))

            job(FORGET, a_hi, a_lo, before_unit=forget_unit)

            def forget_step(u):
                if u == 0:
                    pe.wait_ge(small_loaded, 16 * 11)
                    nc.tensor.transpose(stats[:, 64:P], param_rows[64:P], ident[64:P, 64:P]).then_inc(small_turned, 1)
                if u == 1:
                    pe.wait_ge(lam_product, 1)
                    nc.tensor.matmul(stats[:, 0:2], ones[:, :], lam[:, 0:2], start=True,
                                     stop=True).then_inc(lam_sums, 1)
                if u == 2:
                    pe.wait_ge(f_copied, 1)
                    for b in range(TB):
                        last = nc.tensor.transpose(heads_out[:, P * b:P * (b + 1)], f_feat[:, P * b:P * (b + 1)],
                                                   ident[:, :])
                    last.then_inc(f_turned, 1)
                if u == 4:
                    pe.wait_ge(f_ready, 1)
                    pe.wait_ge(tri_ready, 1)
                    for b in range(TB):
                        last = nc.tensor.matmul(heads_out[0:H, P * b:S], lf[:, b], tri[:, 0:S - P * b],
                                                start=(b == 0), stop=(b == TB - 1))
                    last.then_inc(f_summed, 1)
                if u == 5:
                    pe.wait_ge(f_row_ready, 1)
                    for b in range(TB):
                        last = nc.tensor.transpose(heads_out[:, H * b:H * (b + 1)], f_row[:, P * b:P * (b + 1)],
                                                   ident[0:H, 0:H])
                    last.then_inc(f_back, 1)
                    pe.wait_ge(gains_ready, 1)
                    pe.wait_ge(lam_step, 2)
                if u == 6:
                    pe.wait_ge(neg_f_ready, 1)

            def heads_turn(i, work):
                first = isinstance(i, int) and i == 0
                for j in range(HJ):
                    if j == 0:
                        at_least(pe, taken, i * 5 - 1)
                    elif j == 1:
                        pe.wait_ge(f_copied, 1) if first else pe.wait_ge(v_copied, i * 2)
                    elif j == 4:
                        pe.wait_ge(v_copied, i * 2 + 1)
                    else:
                        pe.wait_ge(taken, i * 5 + {2: 1, 3: 2, 5: 3}[j])

                    def before_unit(n):
                        if first:
                            forget_step(j * JU + n)
                        head_hooks(head_step, j * JU + n, i, work)

                    job(work.then(j * JU, j), a_hi, a_lo, before_unit=before_unit)

            heads_turn(0, HEADS)
            with pe.Fori(1, H) as i:
                heads_turn(i, Work(HEADS.unit, HEADS.job, i, HU, HJ))

            def merge(m, work):
                first = isinstance(m, int) and m == 0

                def hooks(at):
                    def before_unit(n):
                        head_hooks(head_step, at + n, H, work)
                        if at + n == 2:
                            pe.wait_ge(r_copied, 1)
                            pe.wait_ge(taken, 5 * H)
                            for b in range(TB):
                                last = nc.tensor.transpose(heads_out[:, P * b:P * (b + 1)],
                                                           r_repeated[:, P * b:P * (b + 1)], ident[:, :])
                            last.then_inc(r_row_wide, 1)
                    return before_unit if first else None

                if first:
                    pe.wait_ge(taken, 5 * H - 1)
                else:
                    pe.wait_ge(parts_ready, m * 2 - 1)
                job(work, a_hi, a_lo, before_unit=hooks(0))
                if first:
                    pe.wait_ge(v_copied, 2 * H)
                else:
                    pe.wait_ge(parts_ready, m * 2)
                job(work.then(JU), a_hi, a_lo, before_unit=hooks(JU))
                pe.wait_ge(gate_scaled, m * 2 + 1)
                if first:
                    pe.wait_ge(o_ready, 2 * H - 1)
                job(work.then(2 * JU, 2), b_hi, b_lo, 0, BU, before_unit=hooks(2 * JU))

                def last_hooks(n):
                    head_hooks(head_step, 2 * JU + BU + n, H, work)
                    if n == BU - 1:
                        pe.wait_ge(o_ready, 2 * H)

                pe.wait_ge(gate_scaled, m * 2 + 2)
                job(work.then(2 * JU + BU, 3), b_hi, b_lo, H, BU, before_unit=last_hooks if first else None)

            merge(0, MERGE)
            with pe.Fori(0, DT // 2 - 1) as i:
                work = Work(MERGE.unit + MU, MERGE.job + MJ, i, 2 * MU, 2 * MJ)
                merge(i * 2 + 1, work)
                merge(i * 2 + 2, work.then(MU, MJ))
            merge(DT - 1, MERGE.then((DT - 1) * MU, (DT - 1) * MJ))

            def projected(m, j, work):
                first = isinstance(m, int) and m == 0

                def before_unit(n):
                    if first:
                        pe.wait_ge(m_ready, (KU - 1) * (n + 1))
                        pe.wait_ge(m_ready_too, n + 1)
                    if n == 2:
                        if isinstance(m, int):
                            pe.wait_ge(xr_loaded[j], 16)
                        else:
                            pe.wait_ge(xr_loaded[j], m * 8 + (16 - 8 * j))
                        at_least(pe, xr_ready, m)
                        for b in range(TB):
                            last = nc.tensor.transpose(turned[:, P * b:P * (b + 1)],
                                                       x_slot[j][:, P * b:P * (b + 1)], ident[:, :])
                        last.then_inc(xr_turned, 1)

                if isinstance(m, int):
                    pe.wait_ge(parts_ready, 2 * DT - 1 + m)
                else:
                    pe.wait_ge(x2_ready, m - 1)
                job(work, a_hi, a_lo, before_unit=before_unit)

            for j in range(2):
                projected(j, j, PROJ.then(j * JU, j))
            with pe.Fori(1, DT // 2) as i:
                work = Work(PROJ.unit, PROJ.job, i, 2 * JU, 2)
                for j in range(2):
                    projected(i * 2 + j, j, work.then(j * JU, j))

            def ups(c, bank_taken):
                def turn(i, work):
                    for j in range(2):
                        m = i * 2 + j
                        at_start = isinstance(c, int) and isinstance(i, int) and c == 0
                        if isinstance(i, int):
                            pe.wait_ge(bank_taken, c * DT + (j - 1) if bank_taken is down_added else DT - 1 + j)
                        else:
                            pe.wait_ge(up_scaled, c * DT + m - 1)

                        def before_unit(n):
                            if at_start:
                                pe.wait_ge(x2_lo, min(DT, KU * (n + 1)))
                            if at_start and j == 0 and n == 2:
                                pe.wait_ge(sum_ready, DT)
                                turn_squares(5 * H, spare)
                            if at_start and j == 1 and n == 0:
                                widen(5 * H, x_sq)

                        job(work.then(j * JU, j), b_hi, b_lo, before_unit=before_unit)

                turn(0, Work(MLP.unit, MLP.job, c * DT, 2 * JU, 2))
                with pe.Fori(1, DT // 2) as i:
                    turn(i, Work(MLP.unit, MLP.job, c * DT + i, 2 * JU, 2))

            def downs(c):
                def turn(i, work):
                    for j in range(2):
                        m = i * 2 + j
                        if isinstance(i, int):
                            pe.wait_ge(up_scaled, c * DT + DT - 1 + j)
                        else:
                            pe.wait_ge(down_added, c * DT + m - 1)

                        def before_unit(n):
                            if isinstance(i, int) and j == 0:
                                pe.wait_ge(up_ready, c * DT + KU * (n + 1))

                        job(work.then(j * JU, j), a_hi, a_lo, before_unit=before_unit)

                turn(0, Work(MLP.unit + DT * JU, MLP.job + DT, c * DT, 2 * JU, 2))
                with pe.Fori(1, DT // 2) as i:
                    turn(i, Work(MLP.unit + DT * JU, MLP.job + DT, c * DT + i, 2 * JU, 2))

            ups(0, x2_ready)
            downs(0)
            with pe.Fori(1, CH - 1) as c:
                ups(c, down_added)
                downs(c)
            ups(CH - 1, down_added)

            LAST = MLP.then((CH - 1) * CU + DT * JU, (CH - 1) * CJ + DT)
            done_before = (CH - 1) * DT

            def turn_output(m, j):
                pe.wait_ge(down_added, m + (done_before + 1))
                at_least(pe, stage_ready, m - 1)
                for b in range(TB):
                    last = nc.tensor.transpose((turned, wide)[j][:, P * b:P * (b + 1)], fin[j][:, P * b:P * (b + 1)],
                                               ident[:, :])
                last.then_inc(fin_turned, 1)

            def last_down(m, work, j):
                static = isinstance(m, int)
                if static and m <= 1:
                    pe.wait_ge(up_scaled, CH * DT - 1 + m)
                else:
                    pe.wait_ge(down_added, m + (done_before - 1))

                def before_unit(n):
                    if static and m == 0:
                        pe.wait_ge(up_ready, done_before + KU * (n + 1))
                    if n == 1 and not (static and m == 0):
                        turn_output(m - 1, 1 - j)

                job(work, a_hi, a_lo, before_unit=before_unit)

            last_down(0, LAST, 0)
            for m in (1, 2):
                last_down(m, LAST.then(m * JU, m), m % 2)
            with pe.Fori(1, DT // 2 - 1) as i:
                work = Work(LAST.unit + JU, LAST.job + 1, i, 2 * JU, 2)
                last_down(i * 2 + 1, work, 1)
                last_down(i * 2 + 2, work.then(JU), 0)
            last_down(DT - 1, LAST.then((DT - 1) * JU, DT - 1), 1)
            turn_output(DT - 1, 1)


INPUTS = ["x", "norm_mix", "w_in", "b_forget", "qnorm_diff", "knorm_diff", "lambda_q1", "lambda_k1", "lambda_q2",
          "lambda_k2", "subln_diff", "qnorm_fox", "knorm_fox", "w_branch_diff", "w_branch_fox", "w_gate", "b_gate",
          "w_out", "norm_mlp", "w_mlp_up", "w_mlp_down"]


def kernel(**inputs):
    import numpy as np
    import concourse.bacc as bacc
    from concourse.bass_utils import run_bass_kernel_spmd

    nc = bacc.Bacc("TRN2", target_bir_lowering=False, num_devices=1)
    arrays, args = {}, []
    for name in INPUTS:
        a = np.ascontiguousarray(inputs[name])
        arrays[f"in_{name}"] = a
        args.append(nc.dram_tensor(f"in_{name}", a.shape, mybir.dt.from_np(a.dtype), kind="ExternalInput").ap())
    shape = arrays["in_x"].shape
    args.append(nc.dram_tensor("out", shape, F32, kind="ExternalOutput").ap())
    build(nc, *args)
    result = run_bass_kernel_spmd(nc, [arrays], core_ids=[0])
    return result.results[0]["out"]
```
